# Optimizing a Trainium2 kernel written in Bass

```python
import math
import jax, jax.numpy as jnp
from jax import lax
import numpy as np

D_MODEL = 1024
BATCH = 1
SEQ = 512
DEPTH = 2

N_MIXERS = 2
EPS = 1e-6
NEG_INF = -1e30
FORCE_SCORE = 1e9

N_HEADS = 16
HEAD_DIM = 64
N_KV_GROUPS = 4
HEADS_PER_GROUP = N_HEADS // N_KV_GROUPS
ATTN_WIDTH = N_HEADS * HEAD_DIM
KV_WIDTH = N_KV_GROUPS * HEAD_DIM
CMP_BLOCK = 32
CMP_STRIDE = 16
CMP_HIDDEN = 256
SEL_BLOCK = 64
SEL_TOPK = 16
WINDOW = 512
Q_BLOCK = 64
NSA_IN = ATTN_WIDTH + 6 * KV_WIDTH + 3 * N_HEADS + ATTN_WIDTH

SSM_WIDTH = D_MODEL
SSM_GROUP = 16
SSM_GROUPS = SSM_WIDTH // SSM_GROUP
SSM_STATE = 64
SCAN_CHUNK = 128
DT_MIN = 1e-3
DT_MAX = 1e-1


def _rmsnorm(x, g):
    xf = x.astype(jnp.float32)
    y = xf * lax.rsqrt(jnp.mean(xf * xf, axis=-1, keepdims=True) + EPS) * g.astype(jnp.float32)
    return y.astype(x.dtype)

def _masked_softmax(s, mask):
    s = jnp.where(mask, s, NEG_INF)
    m = jnp.max(s, axis=-1, keepdims=True)
    p = jnp.where(mask, jnp.exp(s - m), 0.0)
    return p / jnp.maximum(jnp.sum(p, axis=-1, keepdims=True), 1e-30)

def _alibi_slopes():
    h = jnp.arange(1, N_HEADS + 1, dtype=jnp.float32)
    return jnp.exp2(-8.0 * h / N_HEADS).reshape(N_KV_GROUPS, HEADS_PER_GROUP)

def _compress(k, cmp_idx, pe, w1, w2):
    bsz = k.shape[0]
    n_cmp = cmp_idx.shape[0]
    blk = k[:, cmp_idx] + pe[:, None, :]
    blk = jnp.transpose(blk, (0, 1, 3, 2, 4)).reshape(bsz, n_cmp, N_KV_GROUPS, CMP_BLOCK * HEAD_DIM)
    return jax.nn.silu(blk @ w1) @ w2

def _nsa_mixer(h, w_in, cmp_k_pe, cmp_k_w1, cmp_k_w2, cmp_v_pe, cmp_v_w1, cmp_v_w2, w_out):
    f32 = jnp.float32
    bsz, seq, _ = h.shape
    G, R = N_KV_GROUPS, HEADS_PER_GROUP
    n_cmp = (seq - CMP_BLOCK) // CMP_STRIDE + 1
    n_blocks = seq // SEL_BLOCK
    n_sel = min(SEL_TOPK, n_blocks)

    splits = [ATTN_WIDTH + i * KV_WIDTH for i in range(7)] + [ATTN_WIDTH + 6 * KV_WIDTH + 3 * N_HEADS]
    q, kc, vc, ks, vs, kw, vw, gates, z = jnp.split(h @ w_in, splits, axis=-1)
    q = q.reshape(bsz, seq, G, R, HEAD_DIM) * (HEAD_DIM ** -0.5)
    kc, vc, ks, vs, kw, vw = [a.reshape(bsz, seq, G, HEAD_DIM) for a in (kc, vc, ks, vs, kw, vw)]
    gates = jax.nn.sigmoid(gates.astype(f32)).reshape(bsz, seq, 3, G, R)
    slopes = _alibi_slopes()

    cmp_start = jnp.arange(n_cmp) * CMP_STRIDE
    cmp_idx = cmp_start[:, None] + jnp.arange(CMP_BLOCK)[None, :]
    k_cmp = _compress(kc, cmp_idx, cmp_k_pe, cmp_k_w1, cmp_k_w2)
    v_cmp = _compress(vc, cmp_idx, cmp_v_pe, cmp_v_w1, cmp_v_w2)
    cmp_end = cmp_start + CMP_BLOCK - 1
    cmp_center = cmp_start.astype(f32) + 0.5 * (CMP_BLOCK - 1)

    sel_start = jnp.arange(n_blocks) * SEL_BLOCK
    overlap = ((cmp_start[:, None] <= sel_start[None, :] + SEL_BLOCK - 1)
               & (cmp_end[:, None] >= sel_start[None, :])).astype(f32)

    ks_blk = jnp.transpose(ks.reshape(bsz, n_blocks, SEL_BLOCK, G, HEAD_DIM), (0, 3, 1, 2, 4))
    vs_blk = jnp.transpose(vs.reshape(bsz, n_blocks, SEL_BLOCK, G, HEAD_DIM), (0, 3, 1, 2, 4))
    gather = jax.vmap(jax.vmap(lambda kb, ix: kb[ix]))

    kw_pad = jnp.pad(kw, ((0, 0), (WINDOW, 0), (0, 0), (0, 0)))
    vw_pad = jnp.pad(vw, ((0, 0), (WINDOW, 0), (0, 0), (0, 0)))

    def block(qi):
        q0 = qi * Q_BLOCK
        t = q0 + jnp.arange(Q_BLOCK, dtype=jnp.int32)
        tf = t.astype(f32)
        qb = lax.dynamic_slice_in_dim(q, q0, Q_BLOCK, axis=1)
        gb = lax.dynamic_slice_in_dim(gates, q0, Q_BLOCK, axis=1)

        s_c = jnp.einsum('bqgrd,bngd->bgrqn', qb, k_cmp, preferred_element_type=f32)
        s_c = s_c - slopes[None, :, :, None, None] * (tf[:, None] - cmp_center[None, :])
        p_c = _masked_softmax(s_c, (cmp_end[None, :] <= t[:, None]))
        o_c = jnp.einsum('bgrqn,bngd->bqgrd', p_c, v_cmp)

        imp = jnp.einsum('bgrqn,nj->bgqj', p_c, overlap)
        j = jnp.arange(n_blocks)[None, :]
        jt = (t // SEL_BLOCK)[:, None]
        forced = (j == 0) | (j == jt) | (j == jt - 1)
        imp = jnp.where(forced, FORCE_SCORE, jnp.where(j > jt, -FORCE_SCORE, imp))
        _, sel_idx = lax.top_k(imp, n_sel)

        k_sel = gather(ks_blk, sel_idx)
        v_sel = gather(vs_blk, sel_idx).reshape(bsz, G, Q_BLOCK, n_sel * SEL_BLOCK, HEAD_DIM)
        pos_s = sel_idx[..., None] * SEL_BLOCK + jnp.arange(SEL_BLOCK)
        d_s = t[None, None, :, None, None] - pos_s
        s_s = jnp.einsum('bqgrd,bgqnkd->bgrqnk', qb, k_sel, preferred_element_type=f32)
        s_s = s_s - slopes[None, :, :, None, None, None] * d_s[:, :, None].astype(f32)
        s_s = s_s.reshape(bsz, G, R, Q_BLOCK, n_sel * SEL_BLOCK)
        m_s = (d_s >= 0)[:, :, None].reshape(bsz, G, 1, Q_BLOCK, n_sel * SEL_BLOCK)
        p_s = _masked_softmax(s_s, m_s)
        o_s = jnp.einsum('bgrqm,bgqmd->bqgrd', p_s, v_sel)

        kwb = lax.dynamic_slice_in_dim(kw_pad, q0, Q_BLOCK + WINDOW, axis=1)
        vwb = lax.dynamic_slice_in_dim(vw_pad, q0, Q_BLOCK + WINDOW, axis=1)
        pos_w = q0 - WINDOW + jnp.arange(Q_BLOCK + WINDOW, dtype=jnp.int32)
        d_w = t[:, None] - pos_w[None, :]
        m_w = (pos_w[None, :] >= 0) & (d_w >= 0) & (d_w < WINDOW)
        s_w = jnp.einsum('bqgrd,bkgd->bgrqk', qb, kwb, preferred_element_type=f32)
        s_w = s_w - slopes[None, :, :, None, None] * d_w.astype(f32)
        p_w = _masked_softmax(s_w, m_w)
        o_w = jnp.einsum('bgrqk,bkgd->bqgrd', p_w, vwb)

        return (gb[:, :, 0, :, :, None] * o_c + gb[:, :, 1, :, :, None] * o_s
                + gb[:, :, 2, :, :, None] * o_w)

    o = lax.map(block, jnp.arange(seq // Q_BLOCK, dtype=jnp.int32))
    o = jnp.moveaxis(o, 0, 1).reshape(bsz, seq, ATTN_WIDTH)
    o = (o * jax.nn.silu(z.astype(f32))).astype(h.dtype)
    return o @ w_out

def _complex_affine_combine(left, right):
    ar_i, ai_i, br_i, bi_i = left
    ar_j, ai_j, br_j, bi_j = right
    ar = ar_j * ar_i - ai_j * ai_i
    ai = ar_j * ai_i + ai_j * ar_i
    br = ar_j * br_i - ai_j * bi_i + br_j
    bi = ar_j * bi_i + ai_j * br_i + bi_j
    return ar, ai, br, bi

def _s5_mixer(h, w_in, log_dt, lambda_re, lambda_im, b_re, b_im, c_re, c_im, d_skip, w_glu, w_out):
    f32 = jnp.float32
    bsz, seq, _ = h.shape
    G, C, P = SSM_GROUPS, SSM_GROUP, SSM_STATE
    u, z = jnp.split(h @ w_in, 2, axis=-1)
    u = u.astype(f32).reshape(bsz, seq, G, C)

    dt = jnp.exp(log_dt.astype(f32))[:, None]
    lre = jnp.minimum(lambda_re.astype(f32), -1e-4)
    lim = lambda_im.astype(f32)
    mag = jnp.exp(lre * dt)
    ab_re = mag * jnp.cos(lim * dt)
    ab_im = mag * jnp.sin(lim * dt)
    den = lre * lre + lim * lim
    nr = ab_re - 1.0
    coef_re = (nr * lre + ab_im * lim) / den
    coef_im = (ab_im * lre - nr * lim) / den
    br32, bi32 = b_re.astype(f32), b_im.astype(f32)
    bb_re = coef_re[..., None] * br32 - coef_im[..., None] * bi32
    bb_im = coef_re[..., None] * bi32 + coef_im[..., None] * br32
    cr32, ci32 = c_re.astype(f32), c_im.astype(f32)

    n_chunks = seq // SCAN_CHUNK
    u_chunks = jnp.moveaxis(u.reshape(bsz, n_chunks, SCAN_CHUNK, G, C), 1, 0)
    a_re = jnp.broadcast_to(ab_re, (bsz, SCAN_CHUNK, G, P))
    a_im = jnp.broadcast_to(ab_im, (bsz, SCAN_CHUNK, G, P))

    def chunk_step(carry, u_c):
        x_re, x_im = carry
        bu_re = jnp.einsum('gpc,bkgc->bkgp', bb_re, u_c)
        bu_im = jnp.einsum('gpc,bkgc->bkgp', bb_im, u_c)
        ar, ai, sr, si = lax.associative_scan(_complex_affine_combine, (a_re, a_im, bu_re, bu_im), axis=1)
        xr = sr + ar * x_re[:, None] - ai * x_im[:, None]
        xi = si + ar * x_im[:, None] + ai * x_re[:, None]
        y = jnp.einsum('gcp,bkgp->bkgc', cr32, xr) - jnp.einsum('gcp,bkgp->bkgc', ci32, xi)
        return (xr[:, -1], xi[:, -1]), y

    x0 = jnp.zeros((bsz, G, P), f32)
    _, y = lax.scan(chunk_step, (x0, x0), u_chunks)
    y = jnp.moveaxis(y, 0, 1).reshape(bsz, seq, G, C) + d_skip.astype(f32) * u
    y = jax.nn.gelu(y.reshape(bsz, seq, SSM_WIDTH)).astype(h.dtype)
    ga, gb = jnp.split(y @ w_glu, 2, axis=-1)
    y = ga * jax.nn.sigmoid(gb)
    y = y * jax.nn.silu(z)
    return y @ w_out

def _normal(key, shape, scale):
    return jax.random.normal(key, shape, jnp.float32) * scale

def _nsa_params(key, p):
    ks = jax.random.split(key, 9)
    return {
        p + 'norm': 1.0 + _normal(ks[0], (D_MODEL,), 0.02),
        p + 'w_in': _normal(ks[1], (D_MODEL, NSA_IN), D_MODEL ** -0.5),
        p + 'cmp_k_pe': _normal(ks[2], (CMP_BLOCK, HEAD_DIM), 0.02),
        p + 'cmp_k_w1': _normal(ks[3], (CMP_BLOCK * HEAD_DIM, CMP_HIDDEN), (CMP_BLOCK * HEAD_DIM) ** -0.5),
        p + 'cmp_k_w2': _normal(ks[4], (CMP_HIDDEN, HEAD_DIM), CMP_HIDDEN ** -0.5),
        p + 'cmp_v_pe': _normal(ks[5], (CMP_BLOCK, HEAD_DIM), 0.02),
        p + 'cmp_v_w1': _normal(ks[6], (CMP_BLOCK * HEAD_DIM, CMP_HIDDEN), (CMP_BLOCK * HEAD_DIM) ** -0.5),
        p + 'cmp_v_w2': _normal(ks[7], (CMP_HIDDEN, HEAD_DIM), CMP_HIDDEN ** -0.5),
        p + 'w_out': _normal(ks[8], (ATTN_WIDTH, D_MODEL), ATTN_WIDTH ** -0.5),
    }

def _s5_params(key, p):
    ks = jax.random.split(key, 12)
    n = jnp.arange(SSM_STATE, dtype=jnp.float32)[None, :]
    return {
        p + 'norm': 1.0 + _normal(ks[0], (D_MODEL,), 0.02),
        p + 'w_in': _normal(ks[1], (D_MODEL, 2 * SSM_WIDTH), D_MODEL ** -0.5),
        p + 'log_dt': jax.random.uniform(ks[2], (SSM_GROUPS,), jnp.float32, math.log(DT_MIN), math.log(DT_MAX)),
        p + 'lambda_re': -0.5 + _normal(ks[3], (SSM_GROUPS, SSM_STATE), 0.01),
        p + 'lambda_im': math.pi * n + _normal(ks[4], (SSM_GROUPS, SSM_STATE), 0.01),
        p + 'b_re': _normal(ks[5], (SSM_GROUPS, SSM_STATE, SSM_GROUP), (2 * SSM_GROUP) ** -0.5),
        p + 'b_im': _normal(ks[6], (SSM_GROUPS, SSM_STATE, SSM_GROUP), (2 * SSM_GROUP) ** -0.5),
        p + 'c_re': _normal(ks[7], (SSM_GROUPS, SSM_GROUP, SSM_STATE), SSM_STATE ** -0.5),
        p + 'c_im': _normal(ks[8], (SSM_GROUPS, SSM_GROUP, SSM_STATE), SSM_STATE ** -0.5),
        p + 'd': _normal(ks[9], (SSM_GROUPS, SSM_GROUP), 1.0),
        p + 'w_glu': _normal(ks[10], (SSM_WIDTH, 2 * SSM_WIDTH), SSM_WIDTH ** -0.5),
        p + 'w_out': _normal(ks[11], (SSM_WIDTH, D_MODEL), SSM_WIDTH ** -0.5),
    }

def first_inputs(seed: int = 0) -> dict:
    key = jax.random.key(seed)
    kx, k0, k1, k2, k3, kf = jax.random.split(key, 6)
    inputs = {'x': jax.random.normal(kx, (BATCH, SEQ, D_MODEL), jnp.float32)}
    inputs.update(_nsa_params(k0, 'l0_'))
    inputs.update(_s5_params(k1, 'l1_'))
    inputs.update(_nsa_params(k2, 'l2_'))
    inputs.update(_s5_params(k3, 'l3_'))
    inputs['final_norm'] = 1.0 + _normal(kf, (D_MODEL,), 0.02)
    return inputs

def first_block(x,
              l0_norm, l0_w_in, l0_cmp_k_pe, l0_cmp_k_w1, l0_cmp_k_w2, l0_cmp_v_pe, l0_cmp_v_w1, l0_cmp_v_w2, l0_w_out,
              l1_norm, l1_w_in, l1_log_dt, l1_lambda_re, l1_lambda_im, l1_b_re, l1_b_im, l1_c_re, l1_c_im, l1_d, l1_w_glu, l1_w_out,
              l2_norm, l2_w_in, l2_cmp_k_pe, l2_cmp_k_w1, l2_cmp_k_w2, l2_cmp_v_pe, l2_cmp_v_w1, l2_cmp_v_w2, l2_w_out,
              l3_norm, l3_w_in, l3_log_dt, l3_lambda_re, l3_lambda_im, l3_b_re, l3_b_im, l3_c_re, l3_c_im, l3_d, l3_w_glu, l3_w_out,
              final_norm):
    nsa_layers = [
        (l0_norm, l0_w_in, l0_cmp_k_pe, l0_cmp_k_w1, l0_cmp_k_w2, l0_cmp_v_pe, l0_cmp_v_w1, l0_cmp_v_w2, l0_w_out),
        (l2_norm, l2_w_in, l2_cmp_k_pe, l2_cmp_k_w1, l2_cmp_k_w2, l2_cmp_v_pe, l2_cmp_v_w1, l2_cmp_v_w2, l2_w_out),
    ]
    s5_layers = [
        (l1_norm, l1_w_in, l1_log_dt, l1_lambda_re, l1_lambda_im, l1_b_re, l1_b_im, l1_c_re, l1_c_im, l1_d, l1_w_glu, l1_w_out),
        (l3_norm, l3_w_in, l3_log_dt, l3_lambda_re, l3_lambda_im, l3_b_re, l3_b_im, l3_c_re, l3_c_im, l3_d, l3_w_glu, l3_w_out),
    ]
    h = x
    for i in range(DEPTH):
        if i % N_MIXERS == 0:
            params = nsa_layers[i // N_MIXERS]
            y = _nsa_mixer(_rmsnorm(h, params[0]), *params[1:])
        else:
            params = s5_layers[i // N_MIXERS]
            y = _s5_mixer(_rmsnorm(h, params[0]), *params[1:])
        h = h + y.astype(h.dtype)
    return _rmsnorm(h, final_norm)


DEPTH_2 = 1

RET_HEADS = 4
RET_DK = 128
RET_DV = 256
RET_CHUNK = 128
GLA_HEADS = 4
GLA_DK = 128
GLA_DV = 256
GLA_RANK = 16
GLA_TAU = 16.0
GLA_LOG_GATE_MIN = -1.0
GLA_CHUNK = 64
SWA_Q_HEADS = 16
SWA_KV_HEADS = 4
SWA_HEAD_DIM = 64
SWA_WINDOW = 128
N_BRANCH = 3
BRANCH_WIDTH = RET_HEADS * RET_DV
D_FF = -(-8 * D_MODEL // (3 * 256)) * 256
NORM_EPS = 1e-6
GN_EPS = 1e-5

IN_SPLITS = (
    RET_HEADS * RET_DK, RET_HEADS * RET_DK, RET_HEADS * RET_DV, RET_HEADS * RET_DV,
    GLA_HEADS * GLA_DK, GLA_HEADS * GLA_DK, GLA_HEADS * GLA_DV, GLA_HEADS * GLA_DV, GLA_RANK,
    SWA_Q_HEADS * SWA_HEAD_DIM, SWA_KV_HEADS * SWA_HEAD_DIM, SWA_KV_HEADS * SWA_HEAD_DIM,
    N_BRANCH * D_MODEL,
)
D_IN = sum(IN_SPLITS)


def _split_points():
    return [int(o) for o in np.cumsum(IN_SPLITS)[:-1]]

def rmsnorm(x, w):
    xf = x.astype(jnp.float32)
    y = xf * lax.rsqrt(jnp.mean(xf * xf, axis=-1, keepdims=True) + NORM_EPS)
    return (y * w.astype(jnp.float32)).astype(x.dtype)

def head_groupnorm(o, w, b):
    B, S, H, dv = o.shape
    of = o.astype(jnp.float32)
    mu = jnp.mean(of, axis=-1, keepdims=True)
    var = jnp.mean(jnp.square(of - mu), axis=-1, keepdims=True)
    y = ((of - mu) * lax.rsqrt(var + GN_EPS)).reshape(B, S, H * dv)
    return y * w.astype(jnp.float32) + b.astype(jnp.float32)

def head_rmsnorm(o, w):
    B, S, H, dv = o.shape
    of = o.astype(jnp.float32)
    y = of * lax.rsqrt(jnp.mean(of * of, axis=-1, keepdims=True) + NORM_EPS)
    return y.reshape(B, S, H * dv) * w.astype(jnp.float32)

def retention(q, k, v):
    B, S, H, dk = q.shape
    dv = v.shape[-1]
    C = RET_CHUNK
    N = S // C
    log_g = jnp.log1p(-jnp.exp2(-5.0 - jnp.arange(H, dtype=jnp.float32)))
    q = (q * dk ** -0.5).reshape(B, N, C, H, dk)
    k = k.reshape(B, N, C, H, dk)
    v = v.reshape(B, N, C, H, dv)
    pos = jnp.arange(C, dtype=jnp.float32)
    rel = pos[:, None] - pos[None, :]
    decay = jnp.exp(jnp.where((rel >= 0)[None], rel[None] * log_g[:, None, None], -jnp.inf))
    scores = jnp.einsum('bnihd,bnjhd->bnhij', q, k) * decay
    intra = jnp.einsum('bnhij,bnjhe->bnihe', scores, v)
    zeta = jnp.exp((C - 1 - pos)[None, :] * log_g[:, None])
    kv = jnp.einsum('bnjhd,bnjhe,hj->nbhde', k, v, zeta)
    gamma_c = jnp.exp(C * log_g)[None, :, None, None]

    def step(R, kv_n):
        return gamma_c * R + kv_n, R

    _, states = lax.scan(step, jnp.zeros(kv.shape[1:], kv.dtype), kv)
    xi = jnp.exp((pos + 1.0)[:, None] * log_g[None, :])
    inter = jnp.einsum('bnihd,nbhde->bnihe', q * xi[:, :, None], states)
    return (intra + inter).reshape(B, S, H, dv)

def gla(q, k, v, log_a):
    B, S, H, dk = q.shape
    dv = v.shape[-1]
    C = GLA_CHUNK
    N = S // C
    q = (q * dk ** -0.5).reshape(B, N, C, H, dk)
    k = k.reshape(B, N, C, H, dk)
    v = v.reshape(B, N, C, H, dv)
    b = jnp.cumsum(log_a.reshape(B, N, C, H, dk), axis=2)
    b_last = b[:, :, -1:]
    q_dec = q * jnp.exp(b)
    k_inv = k * jnp.exp(-b)
    causal = jnp.tril(jnp.ones((C, C), dtype=bool))
    A = jnp.where(causal, jnp.einsum('bnihd,bnjhd->bnhij', q_dec, k_inv), 0.0)
    intra = jnp.einsum('bnhij,bnjhe->bnihe', A, v)
    kv = jnp.einsum('bnjhd,bnjhe->nbhde', k * jnp.exp(b_last - b), v)
    chunk_decay = jnp.moveaxis(jnp.exp(b_last[:, :, 0]), 1, 0)

    def step(St, inp):
        kv_n, a_n = inp
        return a_n[..., None] * St + kv_n, St

    _, states = lax.scan(step, jnp.zeros(kv.shape[1:], kv.dtype), (kv, chunk_decay))
    inter = jnp.einsum('bnihd,nbhde->bnihe', q_dec, states)
    return (intra + inter).reshape(B, S, H, dv)

def swa_sinks(q, k, v, sinks):
    B, S, Hq, dh = q.shape
    Hkv = k.shape[2]
    G = Hq // Hkv
    W = SWA_WINDOW
    N = S // W
    slopes = jnp.exp2(-8.0 * jnp.arange(1, Hq + 1, dtype=jnp.float32) / Hq).reshape(Hkv, G)
    qb = q.reshape(B, N, W, Hkv, G, dh)
    kb = k.reshape(B, N, W, Hkv, dh)
    vb = v.reshape(B, N, W, Hkv, dh)

    def with_prev(t):
        prev = jnp.pad(t[:, :-1], ((0, 0), (1, 0), (0, 0), (0, 0), (0, 0)))
        return jnp.concatenate([prev, t], axis=2)

    kk, vv = with_prev(kb), with_prev(vb)
    scores = jnp.einsum('bnqhgd,bnkhd->bnhgqk', qb, kk).astype(jnp.float32) * dh ** -0.5
    qpos = W + jnp.arange(W)
    kpos = jnp.arange(2 * W)
    dist = qpos[:, None] - kpos[None, :]
    blk = jnp.arange(N)
    valid = ((dist >= 0) & (dist < W))[None] & ((blk[:, None, None] > 0) | (kpos[None, None, :] >= W))
    logits = scores - slopes[:, :, None, None] * dist.astype(jnp.float32)
    logits = jnp.where(valid[None, :, None, None], logits, -jnp.inf)
    sink = sinks.astype(jnp.float32).reshape(Hkv, G)[:, :, None, None]
    m = jnp.maximum(jnp.max(logits, axis=-1, keepdims=True), sink)
    p = jnp.exp(logits - m)
    probs = p / (jnp.sum(p, axis=-1, keepdims=True) + jnp.exp(sink - m))
    out = jnp.einsum('bnhgqk,bnkhd->bnqhgd', probs.astype(v.dtype), vv)
    return out.reshape(B, S, Hq * dh)

def second_inputs(seed: int = 0) -> dict:
    key = jax.random.key(seed)
    ks = jax.random.split(key, 17)
    f32 = jnp.float32

    def nrm(k, shape, scale):
        return jax.random.normal(k, shape, f32) * scale

    def gain(k, n):
        return 1.0 + nrm(k, (DEPTH_2, n), 0.05)

    return {
        'x': nrm(ks[0], (BATCH, SEQ, D_MODEL), 1.0),
        'norm_mix_pre': gain(ks[1], D_MODEL),
        'norm_mix_post': gain(ks[2], D_MODEL),
        'w_in': nrm(ks[3], (DEPTH_2, D_MODEL, D_IN), D_MODEL ** -0.5),
        'ret_norm_w': gain(ks[4], RET_HEADS * RET_DV),
        'ret_norm_b': nrm(ks[5], (DEPTH_2, RET_HEADS * RET_DV), 0.02),
        'gla_w_alpha2': nrm(ks[6], (DEPTH_2, GLA_RANK, GLA_HEADS * GLA_DK), GLA_RANK ** -0.5),
        'gla_b_alpha': nrm(ks[7], (DEPTH_2, GLA_HEADS * GLA_DK), 0.1),
        'gla_norm_w': gain(ks[8], GLA_HEADS * GLA_DV),
        'attn_sinks': nrm(ks[9], (DEPTH_2, SWA_Q_HEADS), 0.5),
        'w_branch': nrm(ks[10], (DEPTH_2, N_BRANCH, BRANCH_WIDTH, D_MODEL), BRANCH_WIDTH ** -0.5),
        'w_out': nrm(ks[11], (DEPTH_2, D_MODEL, D_MODEL), D_MODEL ** -0.5),
        'norm_ffn_pre': gain(ks[12], D_MODEL),
        'norm_ffn_post': gain(ks[13], D_MODEL),
        'ffn_w_gate': nrm(ks[14], (DEPTH_2, D_MODEL, D_FF), D_MODEL ** -0.5),
        'ffn_w_up': nrm(ks[15], (DEPTH_2, D_MODEL, D_FF), D_MODEL ** -0.5),
        'ffn_w_down': nrm(ks[16], (DEPTH_2, D_FF, D_MODEL), D_FF ** -0.5),
    }

def second_block(x, norm_mix_pre, norm_mix_post, w_in, ret_norm_w, ret_norm_b, gla_w_alpha2,
              gla_b_alpha, gla_norm_w, attn_sinks, w_branch, w_out, norm_ffn_pre, norm_ffn_post,
              ffn_w_gate, ffn_w_up, ffn_w_down):
    B, S, _ = x.shape
    split_points = _split_points()
    for l in range(DEPTH_2):
        h = rmsnorm(x, norm_mix_pre[l])
        proj = h @ w_in[l]
        (rq, rk, rv, rg, gq, gk, gv, gg, ga, sq, sk, sv, gate_logits) = jnp.split(proj, split_points, axis=-1)

        o_ret = retention(rq.reshape(B, S, RET_HEADS, RET_DK), rk.reshape(B, S, RET_HEADS, RET_DK),
                          rv.reshape(B, S, RET_HEADS, RET_DV))
        o_ret = (head_groupnorm(o_ret, ret_norm_w[l], ret_norm_b[l]) * jax.nn.silu(rg)).astype(x.dtype)

        z = (ga @ gla_w_alpha2[l] + gla_b_alpha[l]).astype(jnp.float32)
        log_a = jnp.maximum(jax.nn.log_sigmoid(z) / GLA_TAU, GLA_LOG_GATE_MIN)
        o_gla = gla(gq.reshape(B, S, GLA_HEADS, GLA_DK), gk.reshape(B, S, GLA_HEADS, GLA_DK),
                    gv.reshape(B, S, GLA_HEADS, GLA_DV), log_a.reshape(B, S, GLA_HEADS, GLA_DK))
        o_gla = (head_rmsnorm(o_gla, gla_norm_w[l]) * jax.nn.silu(gg)).astype(x.dtype)

        o_swa = swa_sinks(sq.reshape(B, S, SWA_Q_HEADS, SWA_HEAD_DIM),
                          sk.reshape(B, S, SWA_KV_HEADS, SWA_HEAD_DIM),
                          sv.reshape(B, S, SWA_KV_HEADS, SWA_HEAD_DIM), attn_sinks[l]).astype(x.dtype)

        branches = jnp.stack([o_ret, o_gla, o_swa], axis=2)
        projected = jnp.einsum('bsnc,ncd->bsnd', branches, w_branch[l])
        gates = jax.nn.sigmoid(gate_logits.reshape(B, S, N_BRANCH, D_MODEL))
        merged = jnp.sum(gates * projected, axis=2)
        x = x + rmsnorm(merged @ w_out[l], norm_mix_post[l])

        h = rmsnorm(x, norm_ffn_pre[l])
        f = (jax.nn.silu(h @ ffn_w_gate[l]) * (h @ ffn_w_up[l])) @ ffn_w_down[l]
        x = x + rmsnorm(f, norm_ffn_post[l])
    return x


def setup_inputs(seed=0):
    out = dict(first_inputs(seed))
    for name, value in second_inputs(seed + 1).items():
        if name != "x":
            out[name + "_2"] = value
    return out


def reference(
    x, l0_norm, l0_w_in, l0_cmp_k_pe, l0_cmp_k_w1, l0_cmp_k_w2, l0_cmp_v_pe, l0_cmp_v_w1,
    l0_cmp_v_w2, l0_w_out, l1_norm, l1_w_in, l1_log_dt, l1_lambda_re, l1_lambda_im, l1_b_re,
    l1_b_im, l1_c_re, l1_c_im, l1_d, l1_w_glu, l1_w_out, l2_norm, l2_w_in, l2_cmp_k_pe,
    l2_cmp_k_w1, l2_cmp_k_w2, l2_cmp_v_pe, l2_cmp_v_w1, l2_cmp_v_w2, l2_w_out, l3_norm, l3_w_in,
    l3_log_dt, l3_lambda_re, l3_lambda_im, l3_b_re, l3_b_im, l3_c_re, l3_c_im, l3_d, l3_w_glu,
    l3_w_out, final_norm, norm_mix_pre_2, norm_mix_post_2, w_in_2, ret_norm_w_2, ret_norm_b_2,
    gla_w_alpha2_2, gla_b_alpha_2, gla_norm_w_2, attn_sinks_2, w_branch_2, w_out_2,
    norm_ffn_pre_2, norm_ffn_post_2, ffn_w_gate_2, ffn_w_up_2, ffn_w_down_2,
):
    x = first_block(
        x, l0_norm, l0_w_in, l0_cmp_k_pe, l0_cmp_k_w1, l0_cmp_k_w2, l0_cmp_v_pe, l0_cmp_v_w1,
        l0_cmp_v_w2, l0_w_out, l1_norm, l1_w_in, l1_log_dt, l1_lambda_re, l1_lambda_im, l1_b_re,
        l1_b_im, l1_c_re, l1_c_im, l1_d, l1_w_glu, l1_w_out, l2_norm, l2_w_in, l2_cmp_k_pe,
        l2_cmp_k_w1, l2_cmp_k_w2, l2_cmp_v_pe, l2_cmp_v_w1, l2_cmp_v_w2, l2_w_out, l3_norm,
        l3_w_in, l3_log_dt, l3_lambda_re, l3_lambda_im, l3_b_re, l3_b_im, l3_c_re, l3_c_im,
        l3_d, l3_w_glu, l3_w_out, final_norm,
    )
    return second_block(
        x, norm_mix_pre_2, norm_mix_post_2, w_in_2, ret_norm_w_2, ret_norm_b_2, gla_w_alpha2_2,
        gla_b_alpha_2, gla_norm_w_2, attn_sinks_2, w_branch_2, w_out_2, norm_ffn_pre_2,
        norm_ffn_post_2, ffn_w_gate_2, ffn_w_up_2, ffn_w_down_2,
    )


_drawn_inputs = setup_inputs


def setup_inputs(seed=0):
    import zlib

    import numpy as np

    out = dict(_drawn_inputs(seed))
    spreads = {}
    factors = {'l0_norm': 4.169,
     'l0_cmp_k_pe': 8.0,
     'l0_cmp_v_pe': 8.0,
     'l1_norm': 5.293,
     'l1_lambda_re': 8.0,
     'l1_b_re': 2.787,
     'l1_b_im': 2.768,
     'l1_c_re': 2.811,
     'l1_c_im': 2.799,
     'ret_norm_b_2': 5.272,
     'attn_sinks_2': 5.125}
    for name, (base, spread) in spreads.items():
        noise = np.random.default_rng([zlib.crc32(name.encode()), seed]).standard_normal(out[name].shape)
        drawn = base * np.exp(spread * noise) if base else spread * noise
        out[name] = __import__('jax').numpy.asarray(drawn.astype(out[name].dtype))
    for name, factor in factors.items():
        out[name] = (out[name] * factor).astype(out[name].dtype)
    return out
```

```python
from contextlib import ExitStack

import numpy as np

import concourse.bass as bass
from concourse import mybir

F32 = mybir.dt.float32
F32R = mybir.dt.float32r
U32 = mybir.dt.uint32
ALU = mybir.AluOpType
ACT = mybir.ActivationFunctionType
AX = mybir.AxisListType.X

S = 512
D = 1024
KT = 8
NEG = -1.0e30
MASKED = 3.0e33
RR = 3
RH = 3
LOOK = 2


class Sem:

    def __init__(self, handle):
        self.handle = handle
        self.n = 0


class Queue:

    def __init__(self, sem):
        self.sem = Sem(sem)
        self.items = []
        self.seen = {}

    def wait(self, *toks):
        for t in toks:
            if t is None:
                continue
            if isinstance(t, list):
                self.wait(*t)
                continue
            s, n = t
            if self.seen.get(s, 0) < n:
                self.seen[s] = n
                self.items.append((0, s.handle, n))

    def do(self, fn, *toks):
        self.wait(*toks)
        self.sem.n += 1
        self.items.append((1, fn, self.sem.handle, 1))
        return (self.sem, self.sem.n)

    def quiet(self, fn, *toks):
        self.wait(*toks)
        self.items.append((2, fn))

    def dma(self, fn, sem, *toks):
        self.wait(*toks)
        sem.n += 16
        self.items.append((1, fn, sem.handle, 16))
        return (sem, sem.n)

    def now(self):
        return (self.sem, self.sem.n) if self.sem.n else None

    def play(self, eng):
        for it in self.items:
            if it[0] == 0:
                eng.wait_ge(it[1], it[2])
            elif it[0] == 1:
                it[1](eng).then_inc(it[2], it[3])
            else:
                it[1](eng)


class Slot:
    def __init__(self, ap):
        self.ap = ap
        self.free = None
        self.busy = False


class Pool:

    def __init__(self, aps):
        self.slots = [Slot(a) for a in aps]
        self.at = 0

    def take(self):
        for _ in self.slots:
            s = self.slots[self.at]
            self.at = (self.at + 1) % len(self.slots)
            if not s.busy:
                s.busy = True
                return s
        raise RuntimeError("no free buffer")

    @staticmethod
    def give(slot, *toks):
        slot.free = list(toks)
        slot.busy = False


class Weights:

    def __init__(self, ins, sp, act, dve, raw, hi, lo, sems, plan):
        self.ins = ins
        self.sp, self.act, self.dve = sp, act, dve
        self.raw, self.hi, self.lo = raw, hi, lo
        self.sems = sems
        self.plan = plan
        self.asked = []
        self.rawfree = [None] * RR
        self.rawuser = [-1] * RR
        self.ringfree = [None] * RH
        self.ringuser = [-1] * RH
        self.loaded = {}
        self.ready = {}
        self.done = set()
        self.nsplit = 0
        self.splits = 0

    def pump(self, upto):
        if self.plan is None:
            return
        while True:
            moved = False
            i = len(self.loaded)
            if i < len(self.plan) and i <= upto + RR:
                r = i % RR
                u = self.rawuser[r]
                if u < 0 or u in self.done:
                    _, (name, at, lo), n, _ = self.plan[i]
                    dst = self.raw[r][:, 0:n]
                    src = self.ins[name][at][:, lo:lo + n]
                    self.loaded[i] = self.sp.dma(
                        lambda e, dst=dst, src=src: e.dma_start(dst, src), self.sems[r], self.rawfree[r])
                    self.rawuser[r] = i
                    moved = True
            j = self.nsplit
            if j < len(self.plan) and j <= upto and j in self.loaded:
                _, _, n, split = self.plan[j]
                if not split:
                    self.ready[j] = (self.raw[j % RR], None, [self.loaded[j]], None)
                    self.nsplit += 1
                    moved = True
                else:
                    q = self.splits % RH
                    u = self.ringuser[q]
                    if u < 0 or u in self.done:
                        raw = self.raw[j % RR][:, 0:n]
                        hi = self.hi[q][:, 0:n]
                        lo = self.lo[q][:, 0:n]
                        a = self.act.do(lambda e, o=hi, i_=raw: e.activation(o, i_, ACT.Copy),
                                        self.loaded[j], self.ringfree[q])
                        v = self.dve.do(lambda e, o=lo, i_=raw, h=hi: e.tensor_tensor(
                            o, i_, h.bitcast(F32), ALU.subtract), a, self.ringfree[q])
                        self.rawfree[j % RR] = [a, v]
                        self.done.add(("raw", j))
                        self.rawuser[j % RR] = -1
                        self.ringuser[q] = j
                        self.ready[j] = (self.hi[q], self.lo[q], [a, v], q)
                        self.splits += 1
                        self.nsplit += 1
                        moved = True
            if not moved:
                return

    def get(self, key, src, n, split=True):
        i = len(self.asked)
        self.asked.append((key, src, n, split))
        if self.plan is None:
            return i, self.hi[0] if split else self.raw[0], self.lo[0], []
        assert self.plan[i][0] == key
        self.pump(i + LOOK)
        hi, lo, toks, _ = self.ready[i]
        return i, hi, lo, toks

    def release(self, i, tok):
        if self.plan is None:
            return
        if self.asked[i][3]:
            q = self.ready[i][3]
            self.ringfree[q] = tok
            self.ringuser[q] = -1
        else:
            self.rawfree[i % RR] = tok
            self.rawuser[i % RR] = -1


class Core:
    pass


def gemm(c, w, col, K, hi, lo, toks, M=128, N=512, bank=None, first=True, last=True):
    bank = bank or c.banks.take()
    k0 = 0
    while k0 < K:
        nk = min(8, K - k0)
        i, wh, wl, wt = c.w.get((w, col, k0), (w, (col,), k0 * M), nk * M)
        for k in range(k0, k0 + nk):
            for p, (a, b) in enumerate(((wh, hi), (wh, lo), (wl, hi))):
                st = first and k == 0 and p == 0
                sp = last and k == K - 1 and p == 2
                lhs = a[:, (k - k0) * M:(k - k0 + 1) * M]
                fn = lambda e, o=bank.ap[0:M, 0:N], l=lhs, r=b(k), st=st, sp=sp: e.matmul(o, l, r, start=st, stop=sp)
                if k == k0 + nk - 1 and p == 2:
                    tok = c.pe.do(fn, wt, toks[k], bank.free)
                else:
                    c.pe.quiet(fn, wt, toks[k], bank.free)
        c.w.release(i, tok)
        k0 += nk
    return bank, tok


def gemm_tok(c, w, m, n, kper, hi, lo, toks):
    banks = [c.banks.take() for _ in range(4)]
    for j in range(KT // kper):
        i, wh, wl, wt = c.w.get((w, m, j), (w, (m, j), 0), kper * n)
        for t in range(4):
            for kk in range(kper):
                k = j * kper + kk
                for p, (a, b) in enumerate(((hi, wh), (lo, wh), (hi, wl))):
                    st = k == 0 and p == 0
                    sp = k == KT - 1 and p == 2
                    fn = lambda e, o=banks[t].ap[:, 0:n], l=a(k)[:, t * 128:(t + 1) * 128], \
                        r=b[:, kk * n:(kk + 1) * n], st=st, sp=sp: e.matmul(o, l, r, start=st, stop=sp)
                    if kk == kper - 1 and p == 2:
                        tok = c.pe.do(fn, wt, toks[k], banks[t].free)
                    else:
                        c.pe.quiet(fn, wt, toks[k], banks[t].free)
            if j == KT // kper - 1:
                banks[t].tok = tok
        c.w.release(i, tok)
    return banks


def split(c, src, hi, lo, *toks):
    a = c.act.do(lambda e, hi=hi, src=src: e.activation(hi, src, ACT.Copy), *toks)
    v = c.dve.do(lambda e, lo=lo, src=src, hi=hi: e.tensor_tensor(lo, src, hi.bitcast(F32), ALU.subtract), a, *toks)
    return [a, v]


def inv_rms(c, tiles, toks, n, eps, scale):
    acc = c.nacc
    last = None
    for k, t in enumerate(tiles):
        if k == 0:
            last = c.act.do(lambda e, t=t, acc=acc: e.activation(acc[:, :], t, ACT.Square), toks[k], c.nfree)
        else:
            s = c.sq.take()
            a = c.act.do(lambda e, t=t, s=s: e.activation(s.ap, t, ACT.Square), toks[k], s.free)
            last = c.dve.do(lambda e, s=s, acc=acc: e.tensor_tensor(acc[:, :], acc[:, :], s.ap, ALU.add), a, last)
            c.sq.give(s, last)
    b = c.banks.take()
    p = c.pe.do(lambda e, b=b, acc=acc, c=c: e.matmul(b.ap, c.ones[:, :], acc[:, :], start=True, stop=True), last, b.free)
    a = c.act.do(lambda e, b=b, scale=scale, c=c, eps=eps: e.activation(c.rs[:, :], b.ap, ACT.Sqrt, bias=c.epst[:, eps:eps + 1], scale=scale), p, c.nfree)
    c.banks.give(b, a)
    r = c.dve.do(lambda e, c=c: e.reciprocal(c.rs[:, :], c.rs[:, :]), a)
    return r


def norm(c, X, xtoks, g, hi, lo, hfree, perm=False):
    r = inv_rms(c, [X[:, k, :] for k in range(KT)], xtoks, D, 0, 1.0 / D)
    out = []
    for k in range(KT):
        s = c.sq.take()
        x = X[:, k, :]
        rs = c.rs[:, :]
        o = s.ap
        if perm:
            x = x.rearrange("p (n s) -> p s n", s=8)
            rs = rs.rearrange("p (n s) -> p s n", s=8)
            o = o.rearrange("p (s n) -> p s n", s=8)
        v = c.dve.do(lambda e, x=x, o=o, k=k, rs=rs, g=g: e.scalar_tensor_tensor(
            o, x, g[:, k:k + 1], rs, ALU.mult, ALU.mult), r, s.free, c.gtok)
        a = c.act.do(lambda e, s=s, k=k, hi=hi: e.activation(hi(k), s.ap, ACT.Copy), v, hfree)
        v2 = c.dve.do(lambda e, s=s, k=k, lo=lo, hi=hi: e.tensor_tensor(lo(k), s.ap, hi(k).bitcast(F32), ALU.subtract), a, hfree)
        c.sq.give(s, v2)
        out.append([a, v2])
    c.nfree = v2
    return out


def barrier(c):
    toks = [q.now() for q in c.queues] + c.dma_toks
    for q in c.queues:
        q.wait(*toks)
    c.dma_toks = []


def load(c, dst, src, *toks):
    t = c.sp.dma(lambda e, dst=dst, src=src: e.dma_start(dst, src), c.dsem(), *toks)
    return t


def nsa(c, X, xtoks):
    pe, act, dve, gp, banks = c.pe, c.act, c.dve, c.gp, c.banks
    I = c.ins
    with ExitStack() as ctx:
        def sb(name, shape, dt=F32):
            return ctx.enter_context(c.nc.sbuf_tensor(name, shape, dt))

        qT = sb("qT", [128, 8, S])
        ksT = sb("ksT", [128, 2, S])
        kwT = sb("kwT", [128, 2, S])
        vsw = sb("vsw", [128, 4, 512])
        zs = sb("zs", [128, 8, S])
        gT = sb("gT", [48, S])
        gate = sb("gate", [128, 4, 48])
        kcT = sb("kcT", [128, 2, 32])
        vc = sb("vc", [128, 64])
        pcT = sb("pcT", [128, 4, S])
        dist = sb("dist", [128, S])
        st = sb("st", [128, 64])

        d_dist = load(c, dist[:, :], I["c_dist"])
        H = norm(c, X, xtoks, c.g_l0, c.hhi, c.hlo, None)
        proj = lambda w, col, **kw: gemm(c, w, col, KT, c.hhi, c.hlo, H, **kw)

        with ExitStack() as cx:
            def sc(name, shape, dt=F32):
                return cx.enter_context(c.nc.sbuf_tensor(name, shape, dt))
            blk = [sc(f"blk{i}", [128, 16, 128]) for i in range(2)]
            pe2 = sc("pe2", [128, 2, 32])
            w2 = sc("w2", [128, 2, 2, 64])
            hid = sc("hid", [128, 2, 2, 128])
            biasc = sc("biasc", [128, 4, 512])
            maskc = sc("maskc", [128, 4, 32])
            sC = sc("sC", [128, 512])
            cs = sc("cs", [128, 3, 16])
            d_pe = load(c, pe2[:, :, :], I["cmp_pe"])
            d_w2 = load(c, w2[:, :, :, :], I["cmp_w2"])
            d_bc = load(c, biasc[:, :, :], I["c_biasc"])
            d_mc = load(c, maskc[:, :, :], I["c_maskc"])
            zt = [gp.do(lambda e, i=i, blk=blk: e.memset(blk[i][:, :, :], 0.0)) for i in range(2)]
            btoks = []
            for i in range(2):
                bt = []
                for gpair in range(2):
                    b, tok = proj("w_kvc", 2 * i + gpair)
                    src = b.ap.rearrange("p (n q two) -> p two q n", q=8, two=2)
                    for a in range(2):
                        for par in range(2):
                            for hf in range(2):
                                o = blk[i][par * 64:par * 64 + 64, hf * 8:hf * 8 + 8, :].rearrange(
                                    "p q (g n) -> p q g n", g=4)[:, :, 2 * gpair + a, 0:31]
                                i0 = src[a * 64:a * 64 + 64, par, :, hf:hf + 31]
                                i1 = pe2[a * 64:a * 64 + 64, i, :].rearrange("p (q two) -> p two q", two=2)[
                                    :, par, hf * 8:hf * 8 + 8].unsqueeze(2).broadcast_to([64, 8, 31])
                                v = dve.do(lambda e, o=o, i0=i0, i1=i1: e.tensor_tensor(o, i0, i1, ALU.add),
                                           tok, d_pe, zt[i])
                    banks.give(b, v)
                    bt.append(v)
                btoks.append(bt)
            b, tok = proj("w_gate", 0, M=48)
            tg = act.do(lambda e, b=b, gT=gT: e.activation(gT[:, :], b.ap[0:48, :], ACT.Sigmoid), tok)
            banks.give(b, tg)
            b = banks.take()
            for t in range(4):
                tok = pe.do(lambda e, t=t, b=b, gT=gT, c=c: e.transpose(b.ap[:, t * 48:t * 48 + 48], gT[:, t * 128:t * 128 + 128],
                                                            c.ident[0:48, 0:48]), tg, b.free)
            tgate = dve.do(lambda e, b=b, gate=gate: e.tensor_copy(gate[:, :, :].rearrange("p a b -> p (a b)"), b.ap[:, 0:192]), tok)
            banks.give(b, tgate)
            for i in range(2):
                b = banks.take()
                for m in range(2):
                    for hf in range(2):
                        j, w1, _, wt = c.w.get(("cmp_w1", i, m, hf), ("cmp_w1", (i, m, hf), 0), 1024, split=False)
                        for q in range(8):
                            fn = lambda e, b=b, m=m, q=q, hf=hf, i=i, w1=w1, blk=blk: e.matmul(
                                b.ap[:, m * 128:m * 128 + 128], w1[:, q * 128:q * 128 + 128],
                                blk[i][:, hf * 8 + q, :], start=(hf == 0 and q == 0), stop=(hf == 1 and q == 7))
                            tok = pe.do(fn, wt, btoks[i], b.free)
                        c.w.release(j, tok)
                th = act.do(lambda e, b=b, i=i, hid=hid: e.activation(hid[:, i, :, :].rearrange("p a b -> p (a b)"),
                                                             b.ap[:, 0:256], ACT.Silu), tok)
                banks.give(b, th)
                b = banks.take()
                if i == 0:
                    for g in range(4):
                        for m in range(2):
                            fn = lambda e, g=g, m=m, b=b, w2=w2, hid=hid: e.matmul(
                                b.ap[(g % 2) * 64:(g % 2) * 64 + 64, (g // 2) * 32:(g // 2) * 32 + 32],
                                w2[:, 0, m, :], hid[:, 0, m, g * 32:g * 32 + 32], start=(m == 0), stop=(m == 1))
                            tok = pe.do(fn, th, d_w2, b.free)
                    tkc = act.do(lambda e, b=b, kcT=kcT: e.activation(kcT[:, :, :].rearrange("p a b -> p (a b)"),
                                                             b.ap[:, 0:64], ACT.Copy), tok)
                    banks.give(b, tkc)
                else:
                    for m in range(2):
                        fn = lambda e, m=m, b=b, hid=hid, w2=w2: e.matmul(b.ap[:, 0:64], hid[:, 1, m, :], w2[:, 1, m, :],
                                                          start=(m == 0), stop=(m == 1))
                        tok = pe.do(fn, th, d_w2, b.free)
                    tvc = act.do(lambda e, b=b, vc=vc: e.activation(vc[:, :], b.ap[:, 0:64], ACT.Copy), tok)
                    banks.give(b, tvc)
            tq = []
            for t in range(8):
                b, tok = proj("w_q", t)
                a = act.do(lambda e, b=b, t=t, qT=qT: e.activation(qT[:, t, :], b.ap, ACT.Copy, scale=0.125), tok)
                banks.give(b, a)
                tq.append(a)
            tk = []
            for i, dst in enumerate((ksT, kwT)):
                for g2 in range(2):
                    b, tok = proj("w_ksw", 2 * i + g2)
                    a = act.do(lambda e, b=b, dst=dst, g2=g2: e.activation(dst[:, g2, :], b.ap, ACT.Copy), tok)
                    banks.give(b, a)
                    tk.append(a)
            tv = []
            for t, b in enumerate(gemm_tok(c, "w_vsw", 0, 512, 2, c.hhi, c.hlo, H)):
                a = act.do(lambda e, b=b, t=t, vsw=vsw: e.activation(vsw[:, t, :], b.ap, ACT.Copy), b.tok)
                banks.give(b, a)
                tv.append(a)

            tpc = []
            prev = None
            for j in range(4):
                for a in range(2):
                    b = banks.take()
                    for t in range(8):
                        r, g2 = t % 4, t // 4
                        col = (r * 2 + g2) * 32
                        fn = lambda e, b=b, t=t, a=a, j=j, col=col, qT=qT, kcT=kcT: e.matmul(
                            b.ap[:, col:col + 32], qT[a * 64:a * 64 + 64, t, j * 128:j * 128 + 128],
                            kcT[a * 64:a * 64 + 64, t // 4, :], start=True, stop=True)
                        tok = pe.do(fn, tq, tkc, b.free)
                    view = lambda ap, a=a: ap.rearrange("p (h a n) -> p h a n", a=2, n=32)[:, :, a, :]
                    v = dve.do(lambda e, b=b, j=j, view=view, sC=sC, biasc=biasc: e.tensor_tensor(
                        view(sC[:, :]), b.ap[:, 0:256].rearrange("p (h n) -> p h n", n=32), view(biasc[:, j, :]),
                        ALU.add), tok, d_bc, prev)
                    banks.give(b, v)
                s3 = sC[:, :].rearrange("p (h n) -> p h n", n=32)
                bc = lambda ap: ap.unsqueeze(2).broadcast_to([128, 16, 32])
                v = dve.do(lambda e, s3=s3, cs=cs: e.tensor_reduce(cs[:, 0, :], s3, axis=AX, op=ALU.max), v)
                v = dve.do(lambda e, s3=s3, bc=bc, cs=cs: e.tensor_tensor(s3, s3, bc(cs[:, 0, :]), ALU.subtract), v)
                a = act.do(lambda e, sC=sC: e.activation(sC[:, :], sC[:, :], ACT.Exp), v)
                v = dve.do(lambda e, j=j, s3=s3, maskc=maskc: e.tensor_tensor(s3, s3, maskc[:, j, :].unsqueeze(1).broadcast_to(
                    [128, 16, 32]), ALU.mult), a, d_mc)
                v = dve.do(lambda e, s3=s3, cs=cs: e.tensor_reduce(cs[:, 1, :], s3, axis=AX, op=ALU.add), v)
                v = dve.do(lambda e, cs=cs: e.tensor_scalar(cs[:, 1, :], cs[:, 1, :], 1e-30, None, ALU.max), v)
                v = dve.do(lambda e, cs=cs: e.reciprocal(cs[:, 2, :], cs[:, 1, :]), v)
                v = dve.do(lambda e, j=j, cs=cs, gate=gate: e.tensor_tensor(
                    cs[:, 0, :].rearrange("p (r g) -> p r g", g=4), cs[:, 2, :].rearrange("p (r g) -> p r g", g=4),
                    gate[:, j, 0:16].rearrange("p (g r) -> p r g", g=4), ALU.mult), v, tgate)
                v = dve.do(lambda e, s3=s3, bc=bc, cs=cs: e.tensor_tensor(s3, s3, bc(cs[:, 0, :]), ALU.mult), v)
                b = banks.take()
                for r in range(4):
                    tok = pe.do(lambda e, b=b, r=r, sC=sC, c=c: e.transpose(b.ap[:, r * 128:r * 128 + 128],
                                                                sC[:, r * 128:r * 128 + 128], c.ident[:, :]), v, b.free)
                prev = tok
                a = act.do(lambda e, b=b, j=j, pcT=pcT: e.activation(pcT[:, :, j * 128:j * 128 + 128],
                                                            b.ap.rearrange("p (r q) -> p r q", r=4), ACT.Copy), tok)
                banks.give(b, a)
                tpc.append(a)
            tz = []
            for t in range(8):
                b, tok = proj("w_z0", t)
                a = act.do(lambda e, b=b, t=t, zs=zs: e.activation(zs[:, t, :], b.ap, ACT.Silu), tok)
                banks.give(b, a)
                tz.append(a)
            hdone = tok
            cmpdone = [pe.now(), act.now(), dve.now(), gp.now()]
        if c.tap == "proj":
            return dict(qT=qT, ksT=ksT, vsw=vsw, gate=gate, kcT=kcT, vc=vc, pcT=pcT, zs=zs)

        with ExitStack() as cx:
            def sc(name, shape, dt=F32):
                return cx.enter_context(c.nc.sbuf_tensor(name, shape, dt))
            for q in (pe, act, dve, gp):
                q.wait(cmpdone)
            Pb = Pool([sc(f"Pb{i}", [128, 2, 512])[:, :, :] for i in range(3)])
            pT = Pool([sc(f"pT{i}", [128, 4, 128])[:, :, :] for i in range(4)])
            bias = Pool([sc(f"bias{i}", [128, 512])[:, :] for i in range(2)])
            stp = Pool([sc(f"stp{i}", [128, 8])[:, :] for i in range(4)])
            units = [(t, a, j) for t in range(8) for a in range(2) for j in range(4)]
            live = {}
            ob = {}
            otok = []
            htoks = []

            def stage_a(u):
                t, a, j = units[u]
                g2, r = t // 4, t % 4
                h = (2 * g2 + a) * 4 + r
                W = 128 * (j + 1)
                if j == 0:
                    bs = bias.take()
                    slope = -float(np.exp2(np.float32(-8.0 * (h + 1) / 16)))
                    bt = gp.do(lambda e, slope=slope, bs=bs, dist=dist: e.tensor_scalar(bs.ap, dist[:, :], slope, 1.0, ALU.mult, ALU.mult),
                               d_dist, bs.free)
                    live["bias", t, a] = (bs, bt)
                bs, bt = live["bias", t, a]
                P = Pb.take()
                s = stp.take()
                vs_ = []
                for br, K in enumerate((ksT, kwT)):
                    b = banks.take()
                    tok = pe.do(lambda e, b=b, K=K, qT=qT, t=t, g2=g2, W=W, a=a, j=j: e.matmul(
                        b.ap[:, 0:W], qT[a * 64:a * 64 + 64, t, j * 128:j * 128 + 128],
                        K[a * 64:a * 64 + 64, g2, 0:W], start=True, stop=True), tq[t], tk[2 * br + g2], b.free)
                    v = dve.do(lambda e, b=b, br=br, P=P, bs=bs, s=s, W=W: e.tensor_tensor_reduce(
                        out=P.ap[:, br, 0:W], in0=b.ap[:, 0:W], in1=bs.ap[:, 512 - W:512], scale=1.0, scalar=-3.0e38,
                        op0=ALU.add, op1=ALU.max, accum_out=s.ap[:, br:br + 1]), tok, bt, P.free, s.free)
                    banks.give(b, v)
                if j == 3:
                    bias.give(bs, v)
                v = dve.do(lambda e, s=s: e.tensor_scalar(s.ap[:, 2:4], s.ap[:, 0:2], -1.0, None, ALU.mult), v)
                for br in range(2):
                    x = act.do(lambda e, br=br, P=P, W=W, s=s: e.activation(P.ap[:, br, 0:W], P.ap[:, br, 0:W], ACT.Exp,
                                                            bias=s.ap[:, 2 + br:3 + br],
                                                            accum_out=s.ap[:, 4 + br:5 + br]), v)
                live[u] = (P, s, x)

            def stage_b(u):
                t, a, j = units[u]
                g2, r = t // 4, t % 4
                h = (2 * g2 + a) * 4 + r
                W = 128 * (j + 1)
                P, s, x = live[u]
                v = dve.do(lambda e, s=s: e.reciprocal(s.ap[:, 6:8], s.ap[:, 4:6]), x)
                gv = gate[:, j, 16 + h:48:16]
                v = dve.do(lambda e, gv=gv, s=s: e.tensor_tensor(s.ap[:, 6:8], s.ap[:, 6:8], gv, ALU.mult), v, tgate)
                g_ = []
                for br in range(2):
                    g_.append(gp.do(lambda e, br=br, P=P, s=s, W=W: e.tensor_scalar(
                        P.ap[:, br, 0:W], P.ap[:, br, 0:W], s.ap[:, 6 + br:7 + br], 1.0, ALU.mult, ALU.mult), v, x))
                stp.give(s, g_[1])
                live[u] = (P, g_)

            def stage_c(u):
                t, a, j = units[u]
                g2, r = t // 4, t % 4
                g = 2 * g2 + a
                P, g_ = live[u]
                if (t, a, j) == (t, 0, 0):
                    ob[t] = banks.take()
                o = ob[t]
                oap = o.ap[a * 64:a * 64 + 64, j * 128:j * 128 + 128]
                pe.do(lambda e, oap=oap, vc=vc, pcT=pcT, r=r, g=g, j=j: e.matmul(oap, vc[32 * g:32 * g + 31, :], pcT[32 * g:32 * g + 31, r, j * 128:j * 128 + 128],
                                         start=True, stop=False, skip_group_check=True), tvc, tpc[j], o.free)
                hold = []
                for br in range(2):
                    b = banks.take()
                    for k in range(j + 1):
                        tok = pe.do(lambda e, b=b, br=br, k=k, P=P, c=c: e.transpose(
                            b.ap[:, k * 128:k * 128 + 128], P.ap[:, br, k * 128:k * 128 + 128], c.ident[:, :]),
                            g_[br], b.free)
                    p = pT.take()
                    n = (j + 1) * 128
                    dst = p.ap.rearrange("p k q -> p (k q)")[:, 0:n]
                    if br:
                        x = act.do(lambda e, b=b, dst=dst, n=n: e.activation(dst, b.ap[:, 0:n], ACT.Copy), tok, p.free)
                    else:
                        x = dve.do(lambda e, b=b, dst=dst, n=n: e.tensor_copy(dst, b.ap[:, 0:n]), tok, p.free)
                    banks.give(b, x)
                    hold.append((p, x))
                Pb.give(P, tok)
                for br in range(2):
                    p, x = hold[br]
                    for k in range(j + 1):
                        tok = pe.do(lambda e, br=br, k=k, p=p, oap=oap, vsw=vsw, j=j, g=g: e.matmul(
                            oap, vsw[:, k, br * 256 + g * 64:br * 256 + g * 64 + 64], p.ap[:, k, :], start=False,
                            stop=(br == 1 and k == j), skip_group_check=True), x, tv)
                    pT.give(p, tok)
                if (a, j) == (1, 3):
                    s = c.sq.take()
                    v = dve.do(lambda e, s=s, o=o, zs=zs, t=t: e.tensor_tensor(s.ap, o.ap, zs[:, t, :], ALU.mult), tok, tz[t], s.free)
                    banks.give(o, v)
                    h2 = split(c, s.ap, c.hhi(t), c.hlo(t), v, hdone)
                    c.sq.give(s, *h2)
                    htoks.append(h2)

            n = len(units)
            for i in range(n + 2):
                if i < n:
                    stage_a(i)
                if 1 <= i <= n:
                    stage_b(i - 1)
                if i >= 2:
                    stage_c(i - 2)
            out = []
            for t in range(8):
                b, tok = gemm(c, "w_o0", t, KT, c.hhi, c.hlo, htoks)
                v = dve.do(lambda e, b=b, t=t, X=X: e.tensor_tensor(X[:, t, :], X[:, t, :], b.ap, ALU.add), tok, xtoks[t])
                banks.give(b, v)
                out.append(v)
            c.hfree = tok
    barrier(c)
    return out


def s5(c, X, xtoks):
    pe, act, dve, gp, banks = c.pe, c.act, c.dve, c.gp, c.banks
    I = c.ins
    M, A_, S_ = ALU.mult, ALU.add, ALU.subtract
    with ExitStack() as ctx:
        def sb(name, shape, dt=F32):
            return ctx.enter_context(c.nc.sbuf_tensor(name, shape, dt))

        par = sb("par", [128, 3, 32])
        sm = sb("sm", [128, 20, 32])
        pw = sb("pw", [128, 2, 9, 32])
        pr = sb("pr", [128, 2, 8, 32])
        e8 = sb("e8", [128, 2, 32])
        Bq = sb("Bq", [128, 2, 8, 16])
        Cq = sb("Cq", [128, 2, 8, 16])
        Bb = sb("Bb", [128, 2, 8, 16])
        Bd = sb("Bd", [128, 2, 8, 32])
        CA = sb("CA", [128, 2, 8, 9, 16])
        WT = sb("WT", [128, 8, 8, 16])
        Wm = sb("Wm", [128, 2, 8, 128])
        Kp = sb("Kp", [64, 4, 16, 16])
        Tm = sb("Tm", [128, 16, 128])
        Rt = sb("Rt", [128, 2, 8, 64])
        D0 = sb("D0", [128, 8, 64])
        tA = sb("tA", [128, 8, 144])
        wre = sb("wre", [128, 8, 64])
        wim = sb("wim", [128, 8, 64])
        Xs = sb("Xs", [128, 2, 8, 64])
        U = sb("U", [128, 16, 64])
        Yt = sb("Yt", [128, 16, 64])
        up = Pool([sb(f"up{i}", [128, S])[:, :] for i in range(4)])
        zs = sb("zs5", [128, 8, S])
        yt = c.sq
        Y = sb("Y5", [128, 8, S])

        dp = load(c, par[:, :, :], I["s5_par"])
        H = norm(c, X, xtoks, c.g_l1, c.hhi, c.hlo, c.hfree, perm=True)

        def V(fn, *t):
            return dve.do(fn, *t, dve.now())

        def tt(o, a, b, op, *t):
            return V(lambda e, o=o, a=a, b=b, op=op: e.tensor_tensor(o, a, b, op), *t)

        def ts(o, a, s1, op, s2=None, op2=None, *t):
            if op2 is None:
                return V(lambda e, o=o, a=a, s1=s1, op=op: e.tensor_scalar(o, a, s1, None, op), *t)
            return V(lambda e, o=o, a=a, s1=s1, s2=s2, op=op, op2=op2: e.tensor_scalar(o, a, s1, s2, op, op2), *t)

        def cmul(ore, oim, xr, xi, yr, yi, t1, t2, *t):
            tt(t1, xr, yr, M, *t)
            tt(t2, xi, yi, M, *t)
            tt(ore, t1, t2, S_)
            tt(t1, xr, yi, M)
            tt(t2, xi, yr, M)
            return tt(oim, t1, t2, A_)

        s = lambda i: sm[:, i, :]
        lre, lim, ldt = par[:, 0, :], par[:, 1, :], par[:, 2, :]
        a = act.do(lambda e, ldt=ldt, s=s: e.activation(s(0), ldt, ACT.Exp), dp)
        ts(s(1), lre, -1e-4, ALU.min, None, None, dp, a)
        tt(s(2), s(1), s(0), M)
        v = tt(s(3), lim, s(0), M)
        a = act.do(lambda e, s=s: e.activation(s(4), s(2), ACT.Exp), v)
        a8 = act.do(lambda e, s=s: e.activation(s(17), s(2), ACT.Exp, scale=8.0), v)
        big = float(np.float32(1.5 * 2 ** 23))
        ts(s(5), s(3), float(np.float32(1 / (2 * np.pi))), M, big, A_)
        ts(s(5), s(5), big, S_)
        c1 = 6.28125
        c2 = float(np.float32(np.round((2 * np.pi - c1) * 2 ** 20) / 2 ** 20))
        c3 = float(np.float32(2 * np.pi - c1 - c2))
        cur = s(3)
        for cc in (c1, c2, c3):
            ts(s(6), s(5), cc, M)
            tt(s(7), cur, s(6), S_)
            cur = s(7)
        lim_ = 3.1415925
        ts(s(7), s(7), lim_, ALU.min, -lim_, ALU.max)
        ts(s(8), s(7), -1.0, M)
        tt(s(8), s(7), s(8), ALU.max)
        v = ts(s(8), s(8), -1.0, M, float(np.float32(np.pi / 2)), A_)
        a1 = act.do(lambda e, s=s: e.activation(s(9), s(8), ACT.Sin), v)
        a2 = act.do(lambda e, s=s: e.activation(s(10), s(7), ACT.Sin), v)
        cos, sin = s(9), s(10)
        P = lambda i, k: pw[:, i, k, :]
        V(lambda e, P=P: e.memset(P(0, 0), 1.0))
        V(lambda e, P=P: e.memset(P(1, 0), 0.0))
        tt(P(0, 1), s(4), cos, M, a, a1)
        tt(P(1, 1), s(4), sin, M, a2)
        t1, t2 = s(11), s(12)
        cmul(P(0, 2), P(1, 2), P(0, 1), P(1, 1), P(0, 1), P(1, 1), t1, t2)
        for k in (3, 4):
            cmul(P(0, k), P(1, k), P(0, k - 2), P(1, k - 2), P(0, 2), P(1, 2), t1, t2)
        for k in (5, 6, 7, 8):
            cmul(P(0, k), P(1, k), P(0, k - 4), P(1, k - 4), P(0, 4), P(1, 4), t1, t2)
        for k in range(8):
            V(lambda e, k=k, pr=pr, pw=pw: e.tensor_copy(pr[:, :, k, :], pw[:, :, 7 - k, :]))
        E = (s(13), s(14))
        cmul(E[0], E[1], cos, sin, cos, sin, t1, t2)
        cmul(s(15), s(16), E[0], E[1], E[0], E[1], t1, t2)
        cmul(e8[:, 0, :], e8[:, 1, :], s(15), s(16), s(15), s(16), t1, t2)
        tt(s(11), s(1), s(1), M)
        tt(s(12), lim, lim, M)
        tt(s(11), s(11), s(12), A_)
        V(lambda e, s=s: e.reciprocal(s(11), s(11)))
        ts(s(12), P(0, 1), -1.0, A_)
        tt(s(13), s(12), s(1), M)
        tt(s(14), P(1, 1), lim, M)
        tt(s(13), s(13), s(14), A_)
        tt(s(18), s(13), s(11), M)
        tt(s(13), P(1, 1), s(1), M)
        tt(s(14), s(12), lim, M)
        tt(s(13), s(13), s(14), S_)
        tt(s(19), s(13), s(11), M)
        V(lambda e, Bd=Bd: e.memset(Bd[:, :, :, :], 0.0))
        V(lambda e, D0=D0: e.memset(D0[:, :, 0:1], 0.0))
        V(lambda e, Xs=Xs: e.memset(Xs[:, :, :, 0:1], 0.0))
        V(lambda e, Kp=Kp: e.memset(Kp[:, :, 0:8, :], 0.0))
        zero = dve.now()

        def u_tile(k):
            b, tok = gemm(c, "w_s5", k, KT, c.hhi, c.hlo, H)
            u = up.take()
            a_ = act.do(lambda e, u=u, b=b: e.activation(u.ap, b.ap, ACT.Copy), tok, u.free)
            banks.give(b, a_)
            return u, a_

        tz = []

        def z_tile(k):
            b, tok = gemm(c, "w_s5", 8 + k, KT, c.hhi, c.hlo, H)
            a_ = act.do(lambda e, zs=zs, b=b, k=k: e.activation(zs[:, k, :], b.ap, ACT.Silu), tok)
            banks.give(b, a_)
            tz.append(a_)

        yfree = kfree = cafree = tmfree = wmfree = ufree = None
        ytoks = []
        us = [u_tile(0), u_tile(1)]
        for b4 in range(4):
            p8 = slice(8 * b4, 8 * b4 + 8)
            dB = load(c, Bq[:, :, :, :], I["s5_B"][b4], dve.now())
            dC = load(c, Cq[:, :, :, :], I["s5_C"][b4], dve.now())
            bc = lambda ap, n: ap.unsqueeze(2).broadcast_to([128, 8, n])
            x1 = tA[:, :, 0:16]
            x2 = tA[:, :, 16:32]
            cmul(Bb[:, 0, :, :], Bb[:, 1, :, :], Bq[:, 0, :, :], Bq[:, 1, :, :], bc(sm[:, 18, p8], 16),
                 bc(sm[:, 19, p8], 16), x1, x2, dB, pe.now())
            for i in range(2):
                for h in range(2):
                    vb = V(lambda e, i=i, h=h, Bd=Bd, Bb=Bb: e.tensor_copy(Bd[h * 64:h * 64 + 64, i, :, h * 16:h * 16 + 16],
                                                             Bb[h * 64:h * 64 + 64, i, :, :]))
            x3 = tA[:, :, :].rearrange("p q (k n) -> p q k n", k=9)
    
            def cplx(w, n, y, i, o, *t):
                wk = lambda i: w[:, i, 0:n, p8].rearrange("p k q -> p q k").unsqueeze(3).broadcast_to([128, 8, n, 16])
                yk = lambda i: y[:, i, :, :].unsqueeze(2).broadcast_to([128, 8, n, 16])
                x = x3[:, :, 0:n, :]
                tt(o, yk(0), wk(i), M, dC, *t)
                tt(x, yk(1), wk(1 - i), M)
                return tt(o, o, x, A_ if i else S_)
            cplx(pw, 9, Cq, 0, CA[:, 0, :, :, :], cafree)
            cplx(pw, 9, Cq, 1, CA[:, 1, :, :, :])
            vca = ts(CA[:, 1, :, :, :], CA[:, 1, :, :, :], -1.0, M)
            for hf in range(2):
                bk = banks.take()
                for q in range(4):
                    p = 4 * hf + q
                    for i in range(2):
                        tok = pe.do(lambda e, bk=bk, p=p, q=q, i=i, hf=hf, Bd=Bd, CA=CA: e.matmul(
                            bk.ap[hf * 32:hf * 32 + 32, q * 128:q * 128 + 128], Bd[:, i, p, :],
                            CA[:, i, p, 0:8, :].rearrange("p k n -> p (k n)"), start=(i == 0), stop=(i == 1)),
                            vca, vb, bk.free)
                ak = act.do(lambda e, bk=bk, hf=hf, Kp=Kp: e.activation(
                    Kp[hf * 32:hf * 32 + 32, :, 8:16, :].rearrange("p q k n -> p q (k n)"),
                    bk.ap[hf * 32:hf * 32 + 32, :].rearrange("p (q n) -> p q n", q=4), ACT.Copy), tok, zero, kfree)
                banks.give(bk, ak)
            tds = Sem(c.tsems[b4])
            for st in range(8):
                for hf in range(2):
                    for h in range(2):
                        dst = Tm[st * 16:st * 16 + 16, 8 * hf:8 * hf + 8, :].rearrange(
                            "p (q h) n -> p q h n", h=2)[:, :, h, :]
                        src = Kp[hf * 32 + h * 16:hf * 32 + h * 16 + 16, :, 8 - st:16 - st, :].rearrange(
                            "p q k n -> p q (k n)")
                        dt_ = c.sp.dma(lambda e, dst=dst, src=src: e.dma_start(dst, src), tds, ak, tmfree)
            kfree = dt_
            for i in range(2):
                vwt = cplx(pr, 8, Bb, i, WT[:, :, :, :], pe.now())
                for hf in range(2):
                    bk = banks.take()
                    for q in range(4):
                        p = 4 * hf + q
                        tok = pe.do(lambda e, bk=bk, p=p, q=q, c=c, WT=WT: e.transpose(
                            bk.ap[:, q * 128:q * 128 + 128], WT[:, p, :, :].rearrange("p k n -> p (k n)"),
                            c.ident[:, :]), vwt, bk.free)
                    aw = act.do(lambda e, bk=bk, i=i, hf=hf, Wm=Wm: e.activation(
                        Wm[:, i, 4 * hf:4 * hf + 4, :].rearrange("p q n -> p (q n)"), bk.ap, ACT.Copy), tok, wmfree)
                    banks.give(bk, aw)
            R = lambda i, n0, n1: Rt[:, i, :, n0:n1]
            V(lambda e, p8=p8, Rt=Rt, e8=e8: e.tensor_copy(Rt[:, :, :, 0], e8[:, :, p8]))
            n = 1
            while n < 64:
                bl = lambda i, n=n: Rt[:, i, :, n - 1:n].broadcast_to([128, 8, n])
                cmul(R(0, n, 2 * n), R(1, n, 2 * n), R(0, 0, n), R(1, 0, n), bl(0), bl(1),
                     tA[:, :, 0:n], tA[:, :, 64:64 + n])
                n *= 2
            V(lambda e, p8=p8, D0=D0, sm=sm: e.tensor_copy(D0[:, :, 1:64], sm[:, 17, p8].unsqueeze(2).broadcast_to([128, 8, 63])), a8)
            uds = Sem(c.tsems[4 + b4])
            for kk in range(2):
                u, ut = us[kk]
                dw = c.sp.dma(lambda e, u=u, kk=kk, b4=b4, c=c: e.dma_start(c.du[b4, kk], u.ap), uds, ut)
            for st in range(8):
                dst = U[st * 16:st * 16 + 16, :, :]
                src = c.du[b4].rearrange("k (g c) (s n) -> s c (k g) n", c=16, s=8)[st]
                du = c.sp.dma(lambda e, dst=dst, src=src: e.dma_start(dst, src), uds, dw, ufree)
            vb_ = [banks.take(), banks.take()]
            for i in range(2):
                for g in range(16):
                    p, h = g // 2, g % 2
                    tok = pe.do(lambda e, i=i, g=g, p=p, h=h, vb_=vb_, Wm=Wm, U=U: e.matmul(
                        vb_[i].ap[h * 64:h * 64 + 64, p * 64:p * 64 + 64], Wm[:, i, p, h * 64:h * 64 + 64],
                        U[:, g, :], start=True, stop=True), aw, du, vb_[i].free)
            vr = vb_[0].ap.rearrange("p (q n) -> p q n", q=8)
            vi = vb_[1].ap.rearrange("p (q n) -> p q n", q=8)
            xt = tA[:, :, 0:64]
            tt(wre[:, :, :], vr, Rt[:, 0, :, :], M, tok)
            tt(xt, vi, Rt[:, 1, :, :], M)
            tt(wre[:, :, :], wre[:, :, :], xt, A_)
            tt(wim[:, :, :], vi, Rt[:, 0, :, :], M)
            v = tt(xt, vr, Rt[:, 1, :, :], M)
            banks.give(vb_[0], v)
            banks.give(vb_[1], v)
            tt(wim[:, :, :], wim[:, :, :], xt, S_)
            for w_ in (wre, wim):
                fl = w_[:, :, :].rearrange("p q n -> p (q n)")
                V(lambda e, fl=fl, M=M, A_=A_, D0=D0: e.tensor_tensor_scan(fl, D0[:, :, :].rearrange("p q n -> p (q n)"), fl, 0.0, M, A_))
            lo_ = lambda ap: ap[:, :, 0:63]
            x63 = tA[:, :, 64:127]
            tt(Xs[:, 0, :, 1:64], lo_(wre), lo_(Rt[:, 0, :, :]), M)
            tt(x63, lo_(wim), lo_(Rt[:, 1, :, :]), M)
            tt(Xs[:, 0, :, 1:64], Xs[:, 0, :, 1:64], x63, S_)
            tt(Xs[:, 1, :, 1:64], lo_(wre), lo_(Rt[:, 1, :, :]), M)
            tt(x63, lo_(wim), lo_(Rt[:, 0, :, :]), M)
            vx = tt(Xs[:, 1, :, 1:64], Xs[:, 1, :, 1:64], x63, A_)
            z_tile(2 * b4)
            if b4 < 3:
                nus = [u_tile(2 * b4 + 2), u_tile(2 * b4 + 3)]
            z_tile(2 * b4 + 1)
            for h in range(2):
                yb = banks.take()
                for q in range(8):
                    g = 2 * q + h
                    o = yb.ap[:, q * 64:q * 64 + 64]
                    pe.do(lambda e, o=o, g=g, Tm=Tm, U=U: e.matmul(o, Tm[:, g, :], U[:, g, :], start=True, stop=False),
                          dt_, du, yb.free, pe.now())
                    for i in range(2):
                        tok = pe.do(lambda e, o=o, q=q, h=h, i=i, Xs=Xs, CA=CA: e.matmul(
                            o, CA[h * 64:h * 64 + 64, i, q, 1:9, :].rearrange("p k n -> p (k n)"),
                            Xs[h * 64:h * 64 + 64, i, q, :], start=False, stop=(i == 1)), vx, pe.now() if i == 0 else None)
                ay = act.do(lambda e, yb=yb, h=h, Yt=Yt: e.activation(
                    Yt[:, :, :].rearrange("p (q h) n -> p q h n", h=2)[:, :, h, :],
                    yb.ap.rearrange("p (q n) -> p q n", q=8), ACT.Copy), tok, yfree)
                banks.give(yb, ay)
            yds = Sem(c.tsems[8 + b4])
            for st in range(8):
                dst = c.dy[b4].rearrange("k (g c) (s n) -> s c (k g) n", c=16, s=8)[st]
                src = Yt[st * 16:st * 16 + 16, :, :]
                dyw = c.sp.dma(lambda e, dst=dst, src=src: e.dma_start(dst, src), yds, ay)
            for kk in range(2):
                y = Y[:, 2 * b4 + kk, :]
                dy = c.sp.dma(lambda e, y=y, kk=kk, b4=b4, c=c: e.dma_start(y, c.dy[b4, kk]), yds, dyw)
            for kk in range(2):
                k = 2 * b4 + kk
                y = Y[:, k, :]
                u, ut = us[kk]
                v = dve.do(lambda e, y=y, u=u, k=k, M=M, A_=A_, c=c: e.scalar_tensor_tensor(
                    y, u.ap, c.g_d[:, k:k + 1], y, M, A_), dy, ut)
                up.give(u, v, dw)
                ytoks.append(act.do(lambda e, y=y: e.activation(y, y, ACT.Gelu_apprx_tanh), v))
            yfree = dyw
            cafree = tmfree = wmfree = ufree = tok
            if b4 < 3:
                us = nus
        hd = pe.now()
        ytoks = [split(c, Y[:, k, :], c.hhi(k), c.hlo(k), ytoks[k], hd) for k in range(8)]
        gv = []
        for k in range(8):
            ba, ta = gemm(c, "w_glu", k, KT, c.hhi, c.hlo, ytoks)
            bb, tb = gemm(c, "w_glu", 8 + k, KT, c.hhi, c.hlo, ytoks)
            y = yt.take()
            a = act.do(lambda e, y=y, bb=bb: e.activation(y.ap, bb.ap, ACT.Sigmoid), tb, y.free)
            banks.give(bb, a)
            v = dve.do(lambda e, k=k, M=M, zs=zs, y=y: e.tensor_tensor(zs[:, k, :], zs[:, k, :], y.ap, M), a, tz[k])
            yt.give(y, v)
            v = dve.do(lambda e, k=k, ba=ba, M=M, zs=zs: e.tensor_tensor(zs[:, k, :], zs[:, k, :], ba.ap, M), ta, v)
            banks.give(ba, v)
            gv.append(v)
        hd = pe.now()
        g2 = [split(c, zs[:, k, :], c.hhi(k), c.hlo(k), gv[k], hd) for k in range(8)]
        out = []
        for k in range(8):
            b, tok = gemm(c, "w_o1", k, KT, c.hhi, c.hlo, g2)
            x = X[:, k, :].rearrange("p (n s) -> p s n", s=8)
            v = dve.do(lambda e, b=b, x=x, A_=A_: e.tensor_tensor(x, x, b.ap.rearrange("p (s n) -> p s n", s=8), A_),
                       tok, xtoks[k])
            banks.give(b, v)
            out.append(v)
        c.hfree = tok
    barrier(c)
    return out


def add_normed(c, X, xtoks, Y, ytoks, g):
    r = inv_rms(c, [Y[:, k, :] for k in range(KT)], ytoks, D, 0, 1.0 / D)
    out = []
    for k in range(KT):
        v = c.dve.do(lambda e, Y=Y, g=g, k=k, c=c: e.scalar_tensor_tensor(
            Y[:, k, :], Y[:, k, :], g[:, k:k + 1], c.rs[:, :], ALU.mult, ALU.mult), r)
        out.append(v)
    for k in range(KT):
        out[k] = c.dve.do(lambda e, X=X, Y=Y, k=k: e.tensor_tensor(X[:, k, :], X[:, k, :], Y[:, k, :], ALU.add), out[k], xtoks[k])
    c.nfree = out[-1]
    return out


def branch(c, n, bhi, blo, btoks, H, mg, mtoks):
    out = []
    for k in range(8):
        bg, tg = gemm(c, "w_bgate", 8 * n + k, KT, c.hhi, c.hlo, H)
        s = c.sq.take()
        a = c.act.do(lambda e, s=s, bg=bg: e.activation(s.ap, bg.ap, ACT.Sigmoid), tg, s.free)
        c.banks.give(bg, a)
        bp, tp = gemm(c, "w_branch", 8 * n + k, KT, bhi, blo, btoks)
        if n == 0:
            v = c.dve.do(lambda e, mg=mg, s=s, bp=bp, k=k: e.tensor_tensor(mg[:, k, :], s.ap, bp.ap, ALU.mult), a, tp)
        else:
            v = c.dve.do(lambda e, s=s, bp=bp: e.tensor_tensor(s.ap, s.ap, bp.ap, ALU.mult), a, tp)
        c.banks.give(bp, v)
        if n:
            v = c.dve.do(lambda e, mg=mg, s=s, k=k: e.tensor_tensor(mg[:, k, :], mg[:, k, :], s.ap, ALU.add), v, mtoks[k])
        c.sq.give(s, v)
        out.append(v)
    return out, c.pe.now()


def evacuate(c, name, col, hi, lo, H, dst, func=ACT.Copy, scale=1.0, M=128, free=None):
    b, tok = gemm(c, name, col, KT, hi, lo, H, M=M)
    a = c.act.do(lambda e, dst=dst, func=func, scale=scale, b=b, M=M: e.activation(dst, b.ap[0:M, :], func, scale=scale), tok, free)
    c.banks.give(b, a)
    return a


def second(c, X, xtoks):
    pe, act, dve, gp, banks = c.pe, c.act, c.dve, c.gp, c.banks
    I = c.ins
    r = inv_rms(c, [X[:, k, :] for k in range(KT)], xtoks, D, 0, 1.0 / D)
    xt = [dve.do(lambda e, X=X, k=k, c=c: e.scalar_tensor_tensor(X[:, k, :], X[:, k, :], c.g_fin[:, k:k + 1], c.rs[:, :],
                                                  ALU.mult, ALU.mult), r) for k in range(KT)]
    c.nfree = xt[-1]
    H = norm(c, X, xt, c.g_pre, c.hhi, c.hlo, c.hfree)
    ev = lambda name, col, dst, **kw: evacuate(c, name, col, c.hhi, c.hlo, H, dst, **kw)
    QS = float(128 ** -0.5)

    with ExitStack() as ctx:
        def sb(name, shape, dt=F32):
            return ctx.enter_context(c.nc.sbuf_tensor(name, shape, dt))
        Bh = sb("Bh", [128, 8, S], F32R)
        Bl = sb("Bl", [128, 8, S], F32R)
        bhi = lambda k: Bh[:, k, :]
        blo = lambda k: Bl[:, k, :]
        mg = sb("mg", [128, 8, S])

        def rows_v(name, dst):
            toks = []
            for m in range(2):
                for t, b in enumerate(gemm_tok(c, name, m, 512, 2, c.hhi, c.hlo, H)):
                    a = act.do(lambda e, dst=dst, b=b, t=t, m=m: e.activation(dst[:, t, m * 512:m * 512 + 512], b.ap, ACT.Copy), b.tok)
                    banks.give(b, a)
                    toks.append(a)
            return toks

        def head_rs(tiles, tok, rs, eps):
            s0, s1 = c.sq.take(), c.sq.take()
            a0 = act.do(lambda e, s0=s0, tiles=tiles: e.activation(s0.ap, tiles[0], ACT.Square), tok, s0.free)
            a1 = act.do(lambda e, s1=s1, tiles=tiles: e.activation(s1.ap, tiles[1], ACT.Square), tok, s1.free)
            v = dve.do(lambda e, s0=s0, s1=s1: e.tensor_tensor(s0.ap, s0.ap, s1.ap, ALU.add), a0, a1)
            c.sq.give(s1, v)
            b = banks.take()
            p = pe.do(lambda e, b=b, s0=s0, c=c: e.matmul(b.ap, c.ones[:, :], s0.ap, start=True, stop=True), v, b.free)
            c.sq.give(s0, p)
            a = act.do(lambda e, rs=rs, b=b, c=c, eps=eps: e.activation(rs, b.ap, ACT.Sqrt, bias=c.epst[:, eps:eps + 1], scale=1.0 / 256), p)
            banks.give(b, a)
            return dve.do(lambda e, rs=rs: e.reciprocal(rs, rs), a)

        with ExitStack() as cx:
            def sc(name, shape, dt=F32):
                return cx.enter_context(c.nc.sbuf_tensor(name, shape, dt))
            q = sc("rq", [128, 4, S])
            kk = sc("rk", [128, 4, S])
            v_ = sc("rv", [128, 4, 1024])
            dec = sc("dec", [128, 4, S])
            sT = Pool([sc(f"sT{i}", [128, S])[:, :] for i in range(3)])
            ot = Pool([sc(f"ro{i}", [128, 2, S])[:, :, :] for i in range(2)])
            sg = Pool([sc(f"rg{i}", [128, S])[:, :] for i in range(2)])
            hr = sc("hr", [128, S])
            dd = load(c, dec[:, :, :], I["c_decay"])
            tq = [ev("w_r", h, q[:, h, :], scale=QS) for h in range(4)]
            tk = [ev("w_r", 4 + h, kk[:, h, :]) for h in range(4)]
            tv = rows_v("w_rv", v_)
            btoks = []
            hrfree = None
            for h in range(4):
                ob = [banks.take(), banks.take()]
                for kt in range(4):
                    W = S - 128 * kt
                    b = banks.take()
                    tok = pe.do(lambda e, kk=kk, q=q, b=b, h=h, W=W, kt=kt: e.matmul(b.ap[:, 0:W], kk[:, h, kt * 128:kt * 128 + 128],
                                                   q[:, h, kt * 128:S], start=True, stop=True), tq[h], tk[h], b.free)
                    s = sT.take()
                    v = dve.do(lambda e, dec=dec, s=s, b=b, h=h, W=W: e.tensor_tensor(s.ap[:, 0:W], b.ap[:, 0:W], dec[:, h, 0:W], ALU.mult),
                               tok, dd, s.free)
                    banks.give(b, v)
                    for e2 in range(2):
                        col = h * 256 + e2 * 128
                        tok = pe.do(lambda e, v_=v_, kt=kt, s=s, ob=ob, e2=e2, col=col, W=W: e.matmul(ob[e2].ap[:, kt * 128:S], v_[:, kt, col:col + 128],
                                                       s.ap[:, 0:W], start=(kt == 0), stop=(kt == 3)),
                                    v, tv, ob[e2].free)
                    sT.give(s, tok)
                o = ot.take()
                for e2 in range(2):
                    a = act.do(lambda e, o=o, e2=e2, ob=ob: e.activation(o.ap[:, e2, :], ob[e2].ap, ACT.Copy), tok, o.free)
                    banks.give(ob[e2], a)
                b = banks.take()
                for e2 in range(2):
                    tok = pe.do(lambda e, b=b, c=c, o=o, e2=e2: e.matmul(b.ap, c.ones[:, :], o.ap[:, e2, :], start=(e2 == 0),
                                                   stop=(e2 == 1)), a, b.free)
                for e2 in range(2):
                    v = dve.do(lambda e, b=b, o=o, e2=e2: e.scalar_tensor_tensor(o.ap[:, e2, :], b.ap, -1.0 / 256, o.ap[:, e2, :],
                                                                ALU.mult, ALU.add), tok)
                banks.give(b, v)
                r = head_rs([o.ap[:, 0, :], o.ap[:, 1, :]], [v, hrfree], hr[:, :], 1)
                for e2 in range(2):
                    k = 2 * h + e2
                    g = sg.take()
                    a = ev("w_rg", k, g.ap, func=ACT.Silu, free=g.free)
                    x = o.ap[:, e2, :]
                    v = dve.do(lambda e, x=x, hr=hr, c=c, k=k: e.scalar_tensor_tensor(x, x, c.g_retw[:, k:k + 1], hr[:, :],
                                                                ALU.mult, ALU.mult), r)
                    hrfree = v
                    v = dve.do(lambda e, x=x, g=g, c=c, k=k: e.scalar_tensor_tensor(x, x, c.g_retb[:, k:k + 1], g.ap,
                                                                ALU.add, ALU.mult), v, a)
                    sg.give(g, v)
                    btoks.append(split(c, x, bhi(k), blo(k), v))
                ot.give(o, *btoks[-1])
            done = [x.now() for x in (pe, act, dve, gp)]
        mt, bfree = branch(c, 0, bhi, blo, btoks, H, mg, None)

        with ExitStack() as cx:
            def sc(name, shape, dt=F32):
                return cx.enter_context(c.nc.sbuf_tensor(name, shape, dt))
            for x in (pe, act, dve, gp, c.sp):
                x.wait(done)
            q = sc("gq", [128, 4, S])
            kk = sc("gk", [128, 4, S])
            v_ = sc("gv", [128, 4, 1024])
            ga = sc("ga", [16, S])
            al = sc("al", [16, 512])
            kd = sc("kd", [128, 4, 128])
            St = sc("St", [128, 7, 256])
            At = sc("At", [128, 4, 64])
            mk = sc("mk", [128, 4, 64])
            rm = sc("rm", [128, S])
            ta, tb, tc = [sc(f"gt{i}", [128, S]) for i in range(3)]
            cd = sc("cd", [128, 8])
            o = sc("go", [128, 2, S])
            sg = Pool([sc(f"gg{i}", [128, S])[:, :] for i in range(2)])
            hr = sc("ghr", [128, S])
            d1 = load(c, al[:, :], I["alpha2"])
            d2 = load(c, mk[:, :, :], I["c_tri"])
            d3 = load(c, rm[:, :], I["c_reset"])
            tga = ev("w_ga", 0, ga[:, :], M=16)
            tq = [ev("w_g", h, q[:, h, :], scale=QS) for h in range(4)]
            tk = [ev("w_g", 4 + h, kk[:, h, :]) for h in range(4)]
            tv = rows_v("w_gv", v_)
            z = dve.do(lambda e, At=At: e.memset(At[:, :, :], 0.0))
            btoks = []
            pfree = gfree = None
            for h in range(4):
                b = banks.take()
                tok = pe.do(lambda e, b=b, al=al, ga=ga, h=h: e.matmul(b.ap, al[:, h * 128:h * 128 + 128], ga[:, :], start=True, stop=True),
                            d1, tga, b.free)
                v = dve.do(lambda e, ta=ta, b=b, c=c, h=h: e.tensor_scalar(ta[:, :], b.ap, c.galpha[:, h:h + 1], None, ALU.add), tok, gfree)
                banks.give(b, v)
                a = act.do(lambda e, tb=tb, ta=ta: e.activation(tb[:, :], ta[:, :], ACT.Abs), v, gfree)
                a = act.do(lambda e, tb=tb: e.activation(tb[:, :], tb[:, :], ACT.Exp, scale=-1.0), a)
                a = act.do(lambda e, tb=tb, c=c: e.activation(tb[:, :], tb[:, :], ACT.Ln, bias=c.ones[:, 0:1]), a)
                v = dve.do(lambda e, ta=ta, tb=tb: e.scalar_tensor_tensor(ta[:, :], ta[:, :], 0.0, tb[:, :], ALU.min,
                                                            ALU.subtract), a, v)
                v = dve.do(lambda e, ta=ta: e.tensor_scalar(ta[:, :], ta[:, :], 1.0 / 16, -1.0, ALU.mult, ALU.max), v)
                v = dve.do(lambda e, tb=tb, rm=rm, ta=ta: e.tensor_tensor_scan(tb[:, :], rm[:, :], ta[:, :], 0.0, ALU.mult, ALU.add),
                           v, d3)
                a1 = act.do(lambda e, ta=ta, tb=tb: e.activation(ta[:, :], tb[:, :], ACT.Exp), v)
                a2 = act.do(lambda e, tc=tc, tb=tb: e.activation(tc[:, :], tb[:, :], ACT.Exp, scale=-1.0), v, gfree)
                t3 = tb[:, :].rearrange("p (n s) -> p n s", s=64)
                a3 = act.do(lambda e, cd=cd, t3=t3: e.activation(cd[:, :], t3[:, :, 63], ACT.Exp), v, gfree)
                vq = dve.do(lambda e, q=q, ta=ta, h=h: e.tensor_tensor(q[:, h, :], q[:, h, :], ta[:, :], ALU.mult), a1, tq[h])
                v = dve.do(lambda e, t3=t3, ta=ta: e.tensor_tensor(
                    ta[:, :].rearrange("p (n s) -> p n s", s=64), t3[:, :, 63:64].broadcast_to([128, 8, 64]), t3,
                    ALU.subtract), vq, a2, a3)
                a = act.do(lambda e, ta=ta: e.activation(ta[:, :], ta[:, :], ACT.Exp), v)
                v = dve.do(lambda e, ta=ta, kk=kk, h=h: e.tensor_tensor(ta[:, :], ta[:, :], kk[:, h, :], ALU.mult), a, tk[h])
                vk = dve.do(lambda e, kk=kk, tc=tc, h=h: e.tensor_tensor(kk[:, h, :], kk[:, h, :], tc[:, :], ALU.mult), v)
                b = banks.take()
                for t in range(4):
                    tok = pe.do(lambda e, ta=ta, b=b, c=c, t=t: e.transpose(b.ap[:, t * 128:t * 128 + 128], ta[:, t * 128:t * 128 + 128],
                                                      c.ident[:, :]), v, b.free)
                gfree = tok
                akd = act.do(lambda e, b=b, kd=kd: e.activation(kd[:, :, :].rearrange("p t d -> p (t d)"), b.ap, ACT.Copy),
                             tok, pfree)
                banks.give(b, akd)
                b = banks.take()
                for n in range(8):
                    p, t = 64 * (n % 2), n // 2
                    tok = pe.do(lambda e, kk=kk, q=q, b=b, h=h, p=p, t=t, n=n: e.matmul(b.ap[p:p + 64, t * 64:t * 64 + 64], kk[:, h, n * 64:n * 64 + 64],
                                                   q[:, h, n * 64:n * 64 + 64], start=True, stop=True), vk, b.free)
                va = dve.do(lambda e, At=At, mk=mk, b=b: e.copy_predicated(At[:, :, :], mk[:, :, :].bitcast(U32),
                                                        b.ap[:, 0:256].rearrange("p (t i) -> p t i", t=4)),
                            tok, d2, z, pfree)
                banks.give(b, va)
                last = None
                for n in range(7):
                    p, t = 64 * (n % 2), n // 2
                    b = banks.take()
                    tok = pe.do(lambda e, kd=kd, v_=v_, b=b, t=t, p=p, h=h: e.matmul(b.ap[:, 0:256], kd[p:p + 64, t, :],
                                                   v_[p:p + 64, t, h * 256:h * 256 + 256], start=True, stop=True),
                                akd, tv, b.free)
                    if n == 0:
                        last = dve.do(lambda e, St=St, b=b: e.tensor_copy(St[:, 0, :], b.ap[:, 0:256]), tok, pfree)
                    else:
                        last = dve.do(lambda e, St=St, cd=cd, n=n, b=b: e.scalar_tensor_tensor(
                            St[:, n, :], St[:, n - 1, :], cd[:, n:n + 1], b.ap[:, 0:256], ALU.mult, ALU.add),
                            tok, last, a3)
                    banks.give(b, last)
                ao = None
                for e2 in range(2):
                    col = h * 256 + e2 * 128
                    bb = [banks.take(), banks.take()]
                    for n in range(8):
                        p, t = 64 * (n % 2), n // 2
                        o_ = bb[n % 2].ap[:, t * 64:t * 64 + 64]
                        tok = pe.do(lambda e, o_=o_, v_=v_, At=At, t=t, n=n, p=p, col=col: e.matmul(o_, v_[p:p + 64, t, col:col + 128], At[p:p + 64, t, :],
                                                       start=True, stop=(n == 0)), va, bb[n % 2].free)
                        if n:
                            tok = pe.do(lambda e, o_=o_, St=St, q=q, h=h, n=n, e2=e2: e.matmul(o_, St[:, n - 1, e2 * 128:e2 * 128 + 128],
                                                           q[:, h, n * 64:n * 64 + 64], start=False, stop=True), last)
                    for i in range(2):
                        ao = act.do(lambda e, i=i, o=o, e2=e2, bb=bb: e.activation(
                            o[:, e2, :].rearrange("p (t i s) -> p t i s", i=2, s=64)[:, :, i, :],
                            bb[i].ap[:, 0:256].rearrange("p (t s) -> p t s", t=4), ACT.Copy), tok, pfree)
                        banks.give(bb[i], ao)
                r = head_rs([o[:, 0, :], o[:, 1, :]], [ao, pfree], hr[:, :], 0)
                for e2 in range(2):
                    k = 2 * h + e2
                    g = sg.take()
                    a = ev("w_gg", k, g.ap, func=ACT.Silu, free=g.free)
                    x = o[:, e2, :]
                    v = dve.do(lambda e, x=x, hr=hr, c=c, k=k: e.scalar_tensor_tensor(x, x, c.g_gla[:, k:k + 1], hr[:, :],
                                                                ALU.mult, ALU.mult), r)
                    v = dve.do(lambda e, x=x, g=g: e.tensor_tensor(x, x, g.ap, ALU.mult), v, a)
                    sg.give(g, v)
                    btoks.append(split(c, x, bhi(k), blo(k), v, bfree))
                pfree = [tok, gfree, btoks[-1]]
                gfree = [gfree, last, vk]
            done = [x.now() for x in (pe, act, dve, gp)]
        mt, bfree = branch(c, 1, bhi, blo, btoks, H, mg, mt)

        with ExitStack() as cx:
            def sc(name, shape, dt=F32):
                return cx.enter_context(c.nc.sbuf_tensor(name, shape, dt))
            for x in (pe, act, dve, gp, c.sp):
                x.wait(done)
            q = sc("sq_", [128, 8, S])
            kk = sc("sk_", [128, 2, S])
            v_ = sc("sv_", [128, 4, 256])
            dist = sc("dist2", [128, 256])
            sink = sc("sink", [128, 16])
            Pb = Pool([sc(f"Ps{i}", [128, 4, 256])[:, :, :] for i in range(3)])
            pT = Pool([sc(f"pTs{i}", [128, 8, 128])[:, :, :] for i in range(2)])
            bias = Pool([sc(f"bs{i}", [128, 256])[:, :] for i in range(3)])
            stp = Pool([sc(f"ss{i}", [128, 5, 4])[:, :, :] for i in range(4)])
            dd = load(c, dist[:, :], I["c_dist2"])
            ds = load(c, sink[:, :], I["sinks"])
            tq = [ev("w_sq", t, q[:, t, :], scale=0.125) for t in range(8)]
            tk = [ev("w_sk", t, kk[:, t, :]) for t in range(2)]
            tv = []
            for t, b in enumerate(gemm_tok(c, "w_sv", 0, 256, 4, c.hhi, c.hlo, H)):
                a = act.do(lambda e, v_=v_, t=t, b=b: e.activation(v_[:, t, :], b.ap[:, 0:256], ACT.Copy), b.tok)
                banks.give(b, a)
                tv.append(a)
            live, ob, btoks = {}, {}, []
            units = [(t, a) for t in range(8) for a in range(2)]
            span = [(0, 128)] + [(128 * (j - 1), 256) for j in (1, 2, 3)]

            def stage_a(u):
                t, a = units[u]
                g2, r = t // 4, t % 4
                h = (2 * g2 + a) * 4 + r
                bs = bias.take()
                slope = -float(np.exp2(np.float32(-8.0 * (h + 1) / 16)))
                bt = gp.do(lambda e, slope=slope, bs=bs, dist=dist: e.tensor_scalar(bs.ap, dist[:, :], slope, 1.0, ALU.mult, ALU.mult), dd, bs.free)
                P = Pb.take()
                s = stp.take()
                for jj in range(2):
                    b = banks.take()
                    for j in (2 * jj, 2 * jj + 1):
                        k0, W = span[j]
                        col = (j % 2) * 256
                        tok = pe.do(lambda e, q=q, kk=kk, b=b, t=t, g2=g2, col=col, k0=k0, W=W, a=a, j=j: e.matmul(
                            b.ap[:, col:col + W], q[a * 64:a * 64 + 64, t, j * 128:j * 128 + 128],
                            kk[a * 64:a * 64 + 64, g2, k0:k0 + W], start=True, stop=True), tq[t], tk[g2], b.free)
                    for j in (2 * jj, 2 * jj + 1):
                        k0, W = span[j]
                        col = (j % 2) * 256
                        v = dve.do(lambda e, P=P, j=j, b=b, bs=bs, s=s, W=W, col=col: e.tensor_tensor_reduce(
                            out=P.ap[:, j, 0:W], in0=b.ap[:, col:col + W], in1=bs.ap[:, 256 - W:256], scale=1.0,
                            scalar=-3.0e38, op0=ALU.add, op1=ALU.max, accum_out=s.ap[:, 0, j:j + 1]),
                            tok, bt, P.free, s.free)
                    banks.give(b, v)
                bias.give(bs, v)
                hs = sink[:, h:h + 1]
                v = dve.do(lambda e, hs=hs, s=s: e.tensor_scalar(s.ap[:, 1, :], s.ap[:, 0, :], hs, -1.0, ALU.max, ALU.mult), v, ds)
                for j in range(4):
                    k0, W = span[j]
                    x = act.do(lambda e, P=P, j=j, W=W, s=s: e.activation(P.ap[:, j, 0:W], P.ap[:, j, 0:W], ACT.Exp,
                                                      bias=s.ap[:, 1, j:j + 1], accum_out=s.ap[:, 2, j:j + 1]), v)
                x = act.do(lambda e, hs=hs, s=s: e.activation(s.ap[:, 3, :], s.ap[:, 1, :], ACT.Exp, bias=hs), v)
                live[u] = (P, s, x)

            def stage_b(u):
                P, s, x = live[u]
                v = dve.do(lambda e, s=s: e.tensor_tensor(s.ap[:, 2, :], s.ap[:, 2, :], s.ap[:, 3, :], ALU.add), x)
                v = dve.do(lambda e, s=s: e.reciprocal(s.ap[:, 4, :], s.ap[:, 2, :]), v)
                for j in range(4):
                    W = span[j][1]
                    g_ = gp.do(lambda e, P=P, j=j, s=s, W=W: e.tensor_scalar(P.ap[:, j, 0:W], P.ap[:, j, 0:W], s.ap[:, 4, j:j + 1], 1.0,
                                                         ALU.mult, ALU.mult), v, x)
                stp.give(s, g_)
                live[u] = (P, g_)

            def stage_c(u):
                t, a = units[u]
                g = 2 * (t // 4) + a
                P, g_ = live[u]
                if a == 0:
                    ob[t] = banks.take()
                o = ob[t]
                p = pT.take()
                blocks = [(j, k) for j in range(4) for k in range(span[j][1] // 128)]
                x = None
                for i in range(2):
                    b = banks.take()
                    part = blocks[4 * i:4 * i + 4]
                    for n, (j, k) in enumerate(part):
                        tok = pe.do(lambda e, b=b, P=P, j=j, c=c, n=n, k=k: e.transpose(b.ap[:, n * 128:n * 128 + 128],
                                                          P.ap[:, j, k * 128:k * 128 + 128], c.ident[:, :]), g_, b.free)
                    w = len(part) * 128
                    dst = p.ap.rearrange("p k q -> p (k q)")[:, i * 512:i * 512 + w]
                    if i:
                        y = act.do(lambda e, dst=dst, b=b, w=w: e.activation(dst, b.ap[:, 0:w], ACT.Copy), tok, p.free)
                    else:
                        y = dve.do(lambda e, dst=dst, b=b, w=w: e.tensor_copy(dst, b.ap[:, 0:w]), tok, p.free)
                    banks.give(b, y)
                    x = [x, y]
                Pb.give(P, tok)
                for n, (j, k) in enumerate(blocks):
                    nb = span[j][1] // 128
                    kt = span[j][0] // 128 + k
                    tok = pe.do(lambda e, v_=v_, o=o, kt=kt, p=p, n=n, k=k, nb=nb, a=a, j=j, g=g: e.matmul(
                        o.ap[a * 64:a * 64 + 64, j * 128:j * 128 + 128], v_[:, kt, g * 64:g * 64 + 64], p.ap[:, n, :],
                        start=(k == 0), stop=(k == nb - 1), skip_group_check=True), x, tv, o.free)
                pT.give(p, tok)
                if a == 1:
                    s = c.sq.take()
                    y = act.do(lambda e, s=s, o=o: e.activation(s.ap, o.ap, ACT.Copy), tok, s.free)
                    banks.give(o, y)
                    h2 = split(c, s.ap, bhi(t), blo(t), y, bfree)
                    c.sq.give(s, *h2)
                    btoks.append(h2)

            n = len(units)
            for i in range(n + 2):
                if i < n:
                    stage_a(i)
                if 1 <= i <= n:
                    stage_b(i - 1)
                if i >= 2:
                    stage_c(i - 2)
        mt, bfree = branch(c, 2, bhi, blo, btoks, H, mg, mt)
        mt = [split(c, mg[:, k, :], bhi(k), blo(k), mt[k], bfree) for k in range(8)]
        yt = []
        for k in range(8):
            b, tok = gemm(c, "w_o2", k, KT, bhi, blo, mt)
            a = act.do(lambda e, mg=mg, b=b, k=k: e.activation(mg[:, k, :], b.ap, ACT.Copy), tok, mt)
            banks.give(b, a)
            yt.append(a)
        xt = add_normed(c, X, xt, mg, yt, c.g_post)
    H = norm(c, X, xt, c.g_fpre, c.hhi, c.hlo, bfree)
    barrier(c)
    with ExitStack() as ctx:
        def sb(name, shape, dt=F32):
            return ctx.enter_context(c.nc.sbuf_tensor(name, shape, dt))
        Fh = sb("Fh", [128, 22, S], F32R)
        Fl = sb("Fl", [128, 22, S], F32R)
        y = sb("fy", [128, 8, S])
        ft = Pool([sb(f"ft{i}", [128, S])[:, :] for i in range(3)])
        ftoks = []
        for k in range(22):
            bg, tg = gemm(c, "w_fg", k, KT, c.hhi, c.hlo, H)
            s = ft.take()
            a = act.do(lambda e, s=s, bg=bg: e.activation(s.ap, bg.ap, ACT.Silu), tg, s.free)
            banks.give(bg, a)
            bu, tu = gemm(c, "w_fu", k, KT, c.hhi, c.hlo, H)
            v = dve.do(lambda e, s=s, bu=bu: e.tensor_tensor(s.ap, s.ap, bu.ap, ALU.mult), a, tu)
            banks.give(bu, v)
            h2 = split(c, s.ap, Fh[:, k, :], Fl[:, k, :], v)
            ft.give(s, *h2)
            ftoks.append(h2)
        yt = []
        for k in range(8):
            b, tok = gemm(c, "w_fd", k, 22, lambda i: Fh[:, i, :], lambda i: Fl[:, i, :], ftoks)
            a = act.do(lambda e, y=y, b=b, k=k: e.activation(y[:, k, :], b.ap, ACT.Copy), tok)
            banks.give(b, a)
            yt.append(a)
        xt = add_normed(c, X, xt, y, yt, c.g_fpost)
        so = Sem(c.osem)
        for k in range(8):
            t = c.sp.dma(lambda e, k=k, X=X, c=c: e.dma_start(c.out[k], X[:, k, :]), so, xt[k])
        c.sp.wait(t)
    return xt


def more(x, A, f, tiles, rows):
    A["w_s5"] = tiles(x["l1_w_in"])
    A["w_glu"] = tiles(x["l1_w_glu"])
    A["w_o1"] = tiles(x["l1_w_out"])
    pair = lambda v: v.reshape(32, 2, 64, *v.shape[2:]).transpose(1, 2, 0, *range(3, v.ndim + 1)).reshape(
        128, 32, *v.shape[2:])
    dt = np.broadcast_to(x["l1_log_dt"][:, None], (64, 64))
    A["s5_par"] = f(np.stack([pair(x["l1_lambda_re"]), pair(x["l1_lambda_im"]), pair(dt)], 1))
    cut = lambda r, i: f(np.stack([r, i], 1).reshape(128, 2, 4, 8, 16).transpose(2, 0, 1, 3, 4))
    A["s5_B"] = cut(pair(x["l1_b_re"]), pair(x["l1_b_im"]))
    A["s5_C"] = cut(pair(x["l1_c_re"].transpose(0, 2, 1)), pair(x["l1_c_im"].transpose(0, 2, 1)))
    w = x["w_in_2"][0]
    at = np.concatenate([[0], np.cumsum([512, 512, 1024, 1024, 512, 512, 1024, 1024, 16, 1024, 256, 256, 3072])])
    s = lambda i, j=None: w[:, at[i]:at[(j or i) + 1]]
    hd = np.arange(64)
    order = np.concatenate([((2 * (t // 4) + a) * 4 + t % 4) * 64 + hd for t in range(8) for a in range(2)])
    A["w_r"] = tiles(s(0, 1))
    A["w_rv"] = rows(s(2), 512, 2)
    A["w_rg"] = tiles(s(3))
    A["w_g"] = tiles(s(4, 5))
    A["w_gv"] = rows(s(6), 512, 2)
    A["w_gg"] = tiles(s(7))
    A["w_ga"] = tiles(s(8), 16)
    A["w_sq"] = tiles(s(9)[:, order])
    A["w_sk"] = tiles(s(10))
    A["w_sv"] = rows(s(11), 256, 4)
    A["w_bgate"] = tiles(s(12))
    wb = x["w_branch_2"][0]
    A["w_branch"] = tiles(np.concatenate([wb[0], wb[1], wb[2][order]], 1))
    A["w_o2"] = tiles(x["w_out_2"][0])
    A["w_fg"] = tiles(x["ffn_w_gate_2"][0])
    A["w_fu"] = tiles(x["ffn_w_up_2"][0])
    A["w_fd"] = tiles(x["ffn_w_down_2"][0])
    A["alpha2"] = f(x["gla_w_alpha2_2"][0])
    A["sinks"] = f(np.broadcast_to(x["attn_sinks_2"], (128, 16)))
    p, m = np.arange(128)[:, None], np.arange(512)[None, :]
    lg = np.log1p(-np.exp2(-5.0 - np.arange(4)))
    rel = (m - p)[:, None, :]
    A["c_decay"] = f(np.where(rel >= 0, np.exp(np.maximum(rel, 0) * lg[None, :, None]), 0.0))
    j, i = np.arange(128)[:, None] % 64, np.arange(64)[None, :]
    A["c_tri"] = f(np.broadcast_to((j <= i)[:, None, :], (128, 4, 64)))
    A["c_reset"] = f(np.broadcast_to(np.arange(512) % 64 != 0, (128, 512)))
    d = 128 + p - np.arange(256)[None, :]
    A["c_dist2"] = f(np.where((d >= 0) & (d < 128), d, np.float32(MASKED)))


def program(nc, ins, out, plan, tap=None):
    c = Core()
    c.nc, c.ins, c.out, c.tap = nc, ins, out, tap
    with ExitStack() as ctx:
        def sb(name, shape, dt=F32):
            return ctx.enter_context(nc.sbuf_tensor(name, shape, dt))

        def sem(name):
            return ctx.enter_context(nc.semaphore(name))

        c.pe, c.act, c.dve, c.gp, c.sp = [Queue(sem(n)) for n in ("s_pe", "s_act", "s_dve", "s_gp", "s_sp")]
        c.queues = [c.pe, c.act, c.dve, c.gp, c.sp]
        c.sems = [Sem(sem(f"s_d{i}")) for i in range(64)]
        c.tsems = [sem(f"s_t{i}") for i in range(12)]
        c.osem = sem("s_out")
        c.sem_at = 0
        c.dma_toks = []

        def dsem():
            s = c.sems[c.sem_at]
            c.sem_at += 1
            return s
        c.dsem = dsem
        c.du = nc.dram_tensor("scratch_u", [4, 2, 128, S], F32, kind="Internal").ap()
        c.dy = nc.dram_tensor("scratch_y", [4, 2, 128, S], F32, kind="Internal").ap()
        raw = [sb(f"wraw{i}", [128, 1024]) for i in range(RR)]
        hi = [sb(f"whi{i}", [128, 1024], F32R) for i in range(RH)]
        lo = [sb(f"wlo{i}", [128, 1024], F32R) for i in range(RH)]
        c.w = Weights(ins, c.sp, c.act, c.dve, raw, hi, lo, [Sem(sem(f"s_w{i}")) for i in range(RR)], plan)
        c.banks = Pool([ctx.enter_context(nc.psum_tensor(f"bank{i}", [128, 512], F32))[:, :] for i in range(8)])
        X = sb("X", [128, 8, S])
        Hh = sb("Hh", [128, 8, S], F32R)
        Hl = sb("Hl", [128, 8, S], F32R)
        c.hhi = lambda k: Hh[:, k, :]
        c.hlo = lambda k: Hl[:, k, :]
        c.nacc = sb("nacc", [128, S])
        c.rs = sb("rs", [128, S])
        c.nfree = None
        c.sq = Pool([sb(f"sq{i}", [128, S])[:, :] for i in range(2)])
        c.ones = sb("ones", [128, 128])
        c.ident = sb("ident", [128, 128])
        c.epst = sb("epst", [128, 2])
        vecs = sb("vecs", [128, 16, 8])
        c.g_l0, c.g_l1, c.g_fin, c.g_pre, c.g_post, c.g_fpre, c.g_fpost, c.g_retw, c.g_retb, c.g_gla, c.g_d = [
            vecs[:, i, :] for i in range(11)]
        c.galpha = vecs[:, 11, 0:4]
        xt = []
        for k in range(8):
            xt.append(load(c, X[:, k, :], ins["xT"][k]))
        dv = load(c, vecs[:, 0:12, :], ins["vecs"])
        di = load(c, c.ident[:, :], ins["c_ident"])
        m1 = c.dve.do(lambda e, c=c: e.memset(c.ones[:, :], 1.0))
        m2 = c.dve.do(lambda e, c=c: e.memset(c.epst[:, 0:1], 1e-6))
        m3 = c.dve.do(lambda e, c=c: e.memset(c.epst[:, 1:2], 1e-5))
        c.gtok = dv
        for q in (c.pe, c.act, c.dve):
            q.wait(dv, di, m3)
        r = nsa(c, X, xt)
        taps = {}
        if tap is None or tap not in ("proj", "nsa"):
            r = s5(c, X, r)
            if tap != "s5":
                r = second(c, X, r)
        if tap:
            if isinstance(r, dict):
                taps = {n: t for n, t in r.items()}
            else:
                taps = {"X": X}
        if taps:
            end = [q.now() for q in c.queues]
            fs = Sem(sem("s_fin"))
            for n, t in taps.items():
                o = nc.dram_tensor("tap_" + n, list(t.shape), F32, kind="ExternalOutput").ap()
                c.sp.dma(lambda e, o=o, t=t: e.dma_start(o, t[tuple(slice(None) for _ in t.shape)]), fs, end)
            c.sp.wait((fs, fs.n))
        if plan is None:
            return c.w.asked
        block = ctx.enter_context(nc.Block())
        block.tensor(lambda e, c=c: c.pe.play(e))
        block.scalar(lambda e, c=c: c.act.play(e))
        block.vector(lambda e, c=c: c.dve.play(e))
        block.gpsimd(lambda e, c=c: c.gp.play(e))
        block.sync(lambda e, c=c: c.sp.play(e))


SHAPES = {}


def build(nc, arrays, tap=None):
    def declare(n):
        return {k: n.dram_tensor("in_" + k, list(a.shape), F32, kind="ExternalInput").ap() for k, a in arrays.items()}

    def result(n):
        return n.dram_tensor("out_0", [8, 128, S], F32, kind="ExternalOutput").ap()
    scratch = bass.Bass()
    plan = program(scratch, declare(scratch), result(scratch), None, tap)
    program(nc, declare(nc), result(nc), plan, tap)


def layout(x):
    f = lambda a: np.ascontiguousarray(a, dtype=np.float32)

    def tiles(w, M=128):
        K, C = w.shape
        return f(w.reshape(K // 128, 128, C // M, M).transpose(2, 1, 0, 3).reshape(C // M, 128, K // 128 * M))

    def rows(w, n, kper):
        K, C = w.shape
        return f(w.reshape(K // 128 // kper, kper, 128, C // n, n).transpose(3, 0, 2, 1, 4).reshape(
            C // n, K // 128 // kper, 128, kper * n))

    def vec(v):
        return f(v.reshape(-1, 128).T)

    A = {}
    A["xT"] = f(x["x"][0].T.reshape(8, 128, S))
    w = x["l0_w_in"]
    hd = np.arange(64)
    order = np.concatenate([((2 * (t // 4) + a) * 4 + t % 4) * 64 + hd for t in range(8) for a in range(2)])
    A["w_kvc"] = tiles(w[:, 1024:1536])
    A["w_gate"] = tiles(w[:, 2560:2608], 48)
    A["w_q"] = tiles(w[:, order])
    A["w_ksw"] = tiles(np.concatenate([w[:, 1536:1792], w[:, 2048:2304]], 1))
    A["w_vsw"] = rows(np.concatenate([w[:, 1792:2048], w[:, 2304:2560]], 1), 512, 2)
    A["w_z0"] = tiles(w[:, 2608 + order])
    A["w_o0"] = tiles(x["l0_w_out"][order])
    p = [x["l0_cmp_k_pe"].T, x["l0_cmp_v_pe"].T]
    A["cmp_pe"] = f(np.stack([np.concatenate([q, q]) for q in p], 1))
    A["cmp_w1"] = f(np.stack([x[n].reshape(2, 8, 128, 2, 128).transpose(3, 0, 2, 1, 4).reshape(2, 2, 128, 1024)
                              for n in ("l0_cmp_k_w1", "l0_cmp_v_w1")]))
    A["cmp_w2"] = f(np.stack([x[n].reshape(2, 128, 64).transpose(1, 0, 2)
                              for n in ("l0_cmp_k_w2", "l0_cmp_v_w2")], 1))
    t = np.arange(512).reshape(4, 128).T
    n = np.arange(32)
    slopes = np.exp2(-8.0 * np.arange(1, 17, dtype=np.float32) / np.float32(16)).astype(np.float32).reshape(4, 4)
    seen = (16 * n + 31)[None, None, :] <= t[:, :, None]
    seen &= n < 31
    gap = (t[:, :, None] - (16 * n + 15.5)).astype(np.float32)
    b = -slopes.T[None, None, :, :, None] * gap[:, :, None, None, :]
    b = np.where(seen[:, :, None, None, :], b, np.float32(NEG))
    A["c_biasc"] = f(b.reshape(128, 4, 512))
    A["c_maskc"] = f(seen)
    d = 384 + np.arange(128)[:, None] - np.arange(512)[None, :]
    A["c_dist"] = f(np.where(d >= 0, d, np.float32(MASKED)))
    A["c_ident"] = f(np.eye(128))
    V = [vec(x[k]) for k in ("l0_norm", "l1_norm", "final_norm", "norm_mix_pre_2", "norm_mix_post_2",
                             "norm_ffn_pre_2", "norm_ffn_post_2", "ret_norm_w_2", "ret_norm_b_2", "gla_norm_w_2")]
    V.append(vec(x["l1_d"]))
    V.append(np.concatenate([vec(x["gla_b_alpha_2"]), np.zeros((128, 4), np.float32)], 1))
    A["vecs"] = f(np.stack(V, 1))
    more(x, A, f, tiles, rows)
    return A


def kernel(**inputs):
    import concourse.bacc as bacc
    from concourse.bass_utils import run_bass_kernel_spmd as run

    x = {k: np.asarray(v) for k, v in inputs.items()}
    A = layout(x)
    nc = bacc.Bacc("TRN2", target_bir_lowering=False, num_devices=1)
    build(nc, A)
    r = run(nc, [{"in_" + k: a for k, a in A.items()}], core_ids=[0])
    return r.results[0]["out_0"].reshape(1024, S).T.reshape(1, S, 1024)
```

```python
from contextlib import ExitStack

import numpy as np

import concourse.bass as bass
from concourse import mybir

F32 = mybir.dt.float32
F32R = mybir.dt.float32r
U32 = mybir.dt.uint32
ALU = mybir.AluOpType
ACT = mybir.ActivationFunctionType
AX = mybir.AxisListType.X

S = 512
D = 1024
KT = 8
NEG = -1.0e30
MASKED = 3.0e33
RR = 3
RH = 3
LOOK = 2
RING = 1024
TICKS = 3


class Sem:

    def __init__(self, handle):
        self.handle = handle
        self.n = 0


class Queue:

    def __init__(self, sem):
        self.sem = Sem(sem)
        self.items = []
        self.seen = {}

    def wait(self, *toks):
        for t in toks:
            if t is None:
                continue
            if isinstance(t, list):
                self.wait(*t)
                continue
            s, n = t
            if self.seen.get(s, 0) < n:
                self.seen[s] = n
                self.items.append((0, s.handle, n))

    def do(self, fn, *toks):
        self.wait(*toks)
        self.sem.n += 1
        self.items.append((1, fn, self.sem.handle, 1))
        return (self.sem, self.sem.n)

    def quiet(self, fn, *toks):
        self.wait(*toks)
        self.items.append((2, fn))

    def dma(self, fn, sem, *toks):
        self.wait(*toks)
        sem.n += 16
        self.items.append((1, fn, sem.handle, 16))
        return (sem, sem.n)

    def now(self):
        return (self.sem, self.sem.n) if self.sem.n else None

    def play(self, eng):
        for it in self.items:
            if it[0] == 0:
                eng.wait_ge(it[1], it[2])
            elif it[0] == 1:
                it[1](eng).then_inc(it[2], it[3])
            else:
                it[1](eng)


class Slot:
    def __init__(self, ap):
        self.ap = ap
        self.free = None


class Pool:

    def __init__(self, aps):
        self.slots = [Slot(a) for a in aps]
        self.idle = list(self.slots)

    def take(self):
        return self.idle.pop(0)

    def give(self, slot, *toks):
        slot.free = list(toks)
        self.idle.append(slot)


class Weights:

    def __init__(self, ins, sp, act, dve, raw, hi, lo, sems, plan):
        self.ins = ins
        self.sp, self.act, self.dve = sp, act, dve
        self.raw, self.hi, self.lo = raw, hi, lo
        self.sems = sems
        self.plan = plan
        self.asked = []
        self.rawfree = [None] * RR
        self.rawuser = [-1] * RR
        self.ringfree = [None] * RH
        self.ringuser = [-1] * RH
        self.loaded = {}
        self.ready = {}
        self.done = set()
        self.nsplit = 0
        self.splits = 0

    def pump(self, upto):
        if self.plan is None:
            return
        while True:
            moved = False
            i = len(self.loaded)
            if i < len(self.plan) and i <= upto + RR:
                r = i % RR
                u = self.rawuser[r]
                if u < 0 or u in self.done:
                    _, (name, at, lo), n, _ = self.plan[i]
                    dst = self.raw[r][:, 0:n]
                    src = self.ins[name][at][:, lo:lo + n]
                    self.loaded[i] = self.sp.dma(
                        lambda e, dst=dst, src=src: e.dma_start(dst, src), self.sems[r], self.rawfree[r])
                    self.rawuser[r] = i
                    moved = True
            j = self.nsplit
            if j < len(self.plan) and j <= upto and j in self.loaded:
                _, _, n, split = self.plan[j]
                if not split:
                    self.ready[j] = (self.raw[j % RR], None, [self.loaded[j]], None)
                    self.nsplit += 1
                    moved = True
                else:
                    q = self.splits % RH
                    u = self.ringuser[q]
                    if u < 0 or u in self.done:
                        raw = self.raw[j % RR][:, 0:n]
                        hi = self.hi[q][:, 0:n]
                        lo = self.lo[q][:, 0:n]
                        a = self.act.do(lambda e, o=hi, i_=raw: e.activation(o, i_, ACT.Copy),
                                        self.loaded[j], self.ringfree[q])
                        v = self.dve.do(lambda e, o=lo, i_=raw, h=hi: e.tensor_tensor(
                            o, i_, h.bitcast(F32), ALU.subtract), a, self.ringfree[q])
                        self.rawfree[j % RR] = [a, v]
                        self.done.add(("raw", j))
                        self.rawuser[j % RR] = -1
                        self.ringuser[q] = j
                        self.ready[j] = (self.hi[q], self.lo[q], [a, v], q)
                        self.splits += 1
                        self.nsplit += 1
                        moved = True
            if not moved:
                return

    def get(self, key, src, n, split=True):
        i = len(self.asked)
        self.asked.append((key, src, n, split))
        if self.plan is None:
            return i, self.hi[0] if split else self.raw[0], self.lo[0], []
        assert self.plan[i][0] == key
        self.pump(i + LOOK)
        hi, lo, toks, _ = self.ready[i]
        return i, hi, lo, toks

    def release(self, i, tok):
        if self.plan is None:
            return
        if self.asked[i][3]:
            q = self.ready[i][3]
            self.ringfree[q] = tok
            self.ringuser[q] = -1
        else:
            self.rawfree[i % RR] = tok
            self.rawuser[i % RR] = -1


class Core:
    pass


def gemm_steps(c, w, col, K, hi, lo, toks, M=128):
    bank = c.banks.take()
    k0 = 0
    while k0 < K:
        nk = min(8, K - k0)
        i, wh, wl, wt = c.w.get((w, col, k0), (w, (col,), k0 * M), nk * M)
        for k in range(k0, k0 + nk):
            for p, (a, b) in enumerate(((wh, hi), (wh, lo), (wl, hi))):
                st = k == 0 and p == 0
                sp = k == K - 1 and p == 2
                lhs = a[:, (k - k0) * M:(k - k0 + 1) * M]
                fn = lambda e, o=bank.ap[0:M, :], l=lhs, r=b(k), st=st, sp=sp: e.matmul(o, l, r, start=st, stop=sp)
                if k == k0 + nk - 1 and p == 2:
                    tok = c.pe.do(fn, wt, toks[k], bank.free)
                else:
                    c.pe.quiet(fn, wt, toks[k], bank.free)
            if k % 4 == 3 and k < K - 1:
                yield None
        c.w.release(i, tok)
        k0 += nk
    yield bank, tok


def gemm(c, *args, **kw):
    for r in gemm_steps(c, *args, **kw):
        pass
    return r


def gemm_pair(c, cols, hi, lo, toks):
    banks = [c.banks.take() for _ in cols]
    ws = [c.w.get((w, col, 0), (w, (col,), 0), 1024) for w, col in cols]
    out = []
    for k in range(KT):
        for bank, (i, wh, wl, wt) in zip(banks, ws):
            for p, (a, b) in enumerate(((wh, hi), (wh, lo), (wl, hi))):
                st = k == 0 and p == 0
                sp = k == KT - 1 and p == 2
                fn = lambda e, o=bank.ap, l=a[:, k * 128:(k + 1) * 128], r=b(k), st=st, sp=sp: e.matmul(
                    o, l, r, start=st, stop=sp)
                if sp:
                    tok = c.pe.do(fn, wt, toks[k], bank.free)
                    c.w.release(i, tok)
                    out.append((bank, tok))
                else:
                    c.pe.quiet(fn, wt, toks[k], bank.free)
    return out


def pair_or_two(c, pair, a, b, toks):
    if pair:
        return gemm_pair(c, [a, b], c.hhi, c.hlo, toks)
    return [gemm(c, w, col, KT, c.hhi, c.hlo, toks) for w, col in (a, b)]


def gemm_tok(c, w, m, n, kper, hi, lo, toks):
    banks = [c.banks.take() for _ in range(4)]
    for j in range(KT // kper):
        i, wh, wl, wt = c.w.get((w, m, j), (w, (m, j), 0), kper * n)
        for t in range(4):
            for kk in range(kper):
                k = j * kper + kk
                for p, (a, b) in enumerate(((hi, wh), (lo, wh), (hi, wl))):
                    st = k == 0 and p == 0
                    sp = k == KT - 1 and p == 2
                    fn = lambda e, o=banks[t].ap[:, 0:n], l=a(k)[:, t * 128:(t + 1) * 128], \
                        r=b[:, kk * n:(kk + 1) * n], st=st, sp=sp: e.matmul(o, l, r, start=st, stop=sp)
                    if kk == kper - 1 and p == 2:
                        tok = c.pe.do(fn, wt, toks[k], banks[t].free)
                    else:
                        c.pe.quiet(fn, wt, toks[k], banks[t].free)
            if j == KT // kper - 1:
                banks[t].tok = tok
        c.w.release(i, tok)
    return banks


def split(c, src, hi, lo, *toks):
    a = c.act.do(lambda e, hi=hi, src=src: e.activation(hi, src, ACT.Copy), *toks)
    v = c.dve.do(lambda e, lo=lo, src=src, hi=hi: e.tensor_tensor(lo, src, hi.bitcast(F32), ALU.subtract), a, *toks)
    return [a, v]


class Squares:

    def __init__(self, c):
        self.c = c
        self.last = None

    def start(self):
        self.last = None

    def add(self, t, *toks):
        c = self.c
        acc = c.nacc
        if self.last is None:
            self.last = c.act.do(lambda e, t=t, acc=acc: e.activation(acc[:, :], t, ACT.Square), *toks, c.nfree)
        else:
            s = c.sq2.take()
            a = c.act.do(lambda e, t=t, s=s: e.activation(s.ap, t, ACT.Square), *toks, s.free)
            self.last = c.dve.do(lambda e, acc=acc, s=s: e.tensor_tensor(acc[:, :], acc[:, :], s.ap, ALU.add), a, self.last)
            c.sq2.give(s, self.last)

    def inv(self, eps, scale):
        c = self.c
        b = c.banks.take()
        p = c.pe.do(lambda e, b=b, c=c: e.matmul(b.ap, c.ones[:, :], c.nacc[:, :], start=True, stop=True), self.last, b.free)
        return rsqrt(c, c.rs[:, :], b, scale, eps, p, c.nfree)


def rsqrt(c, dst, b, scale, eps, *toks):
    a = c.act.do(lambda e, dst=dst, b=b, scale=scale, c=c, eps=eps: e.activation(dst, b.ap, ACT.Ln, bias=c.epst[:, eps:eps + 1], scale=scale), *toks)
    c.banks.give(b, a)
    return c.act.do(lambda e, dst=dst: e.activation(dst, dst, ACT.Exp, scale=-0.5), a)


def norm(c, X, xtoks, g, hi, lo, hfree, perm=False):
    r = c.ss.inv(0, 1.0 / D)
    out = []
    for k in range(KT):
        s = c.sq.take()
        x = X[:, k, :]
        rs = c.rs[:, :]
        o = s.ap
        if perm:
            x = x.rearrange("p (n s) -> p s n", s=8)
            rs = rs.rearrange("p (n s) -> p s n", s=8)
            o = o.rearrange("p (s n) -> p s n", s=8)
        v = c.dve.do(lambda e, x=x, o=o, k=k, rs=rs, g=g: e.scalar_tensor_tensor(
            o, x, g[:, k:k + 1], rs, ALU.mult, ALU.mult), r, s.free, c.gtok)
        a = c.act.do(lambda e, s=s, k=k, hi=hi: e.activation(hi(k), s.ap, ACT.Copy), v, hfree)
        v2 = c.dve.do(lambda e, s=s, k=k, lo=lo, hi=hi: e.tensor_tensor(lo(k), s.ap, hi(k).bitcast(F32), ALU.subtract), a, hfree)
        c.sq.give(s, v2)
        out.append([a, v2])
    c.nfree = v2
    return out


def barrier(c):
    toks = [q.now() for q in c.queues] + c.dma_toks
    for q in c.queues:
        q.wait(*toks)
    c.dma_toks = []


def load(c, dst, src, *toks):
    t = c.sp.dma(lambda e, dst=dst, src=src: e.dma_start(dst, src), c.dsem(), *toks)
    return t


def nsa(c, X, xtoks):
    pe, act, dve, gp, banks = c.pe, c.act, c.dve, c.gp, c.banks
    I = c.ins
    with ExitStack() as ctx:
        def sb(name, shape, dt=F32):
            return ctx.enter_context(c.nc.sbuf_tensor(name, shape, dt))

        qT = sb("qT", [128, 8, S])
        ksT = sb("ksT", [128, 2, S])
        kwT = sb("kwT", [128, 2, S])
        vsw = sb("vsw", [128, 4, 512])
        zs = sb("zs", [128, 8, S])
        gT = sb("gT", [48, S])
        gate = sb("gate", [128, 4, 48])
        kcT = sb("kcT", [128, 2, 32])
        vc = sb("vc", [128, 64])
        pcT = sb("pcT", [128, 4, S])
        dist = sb("dist", [128, S])
        st = sb("st", [128, 64])

        d_dist = load(c, dist[:, :], I["c_dist"])
        H = norm(c, X, xtoks, c.g_l0, c.hhi, c.hlo, None)
        proj = lambda w, col, **kw: gemm(c, w, col, KT, c.hhi, c.hlo, H, **kw)

        with ExitStack() as cx:
            def sc(name, shape, dt=F32):
                return cx.enter_context(c.nc.sbuf_tensor(name, shape, dt))
            blk = [sc(f"blk{i}", [128, 16, 128]) for i in range(2)]
            pe2 = sc("pe2", [128, 2, 32])
            w2 = sc("w2", [128, 2, 2, 64])
            hid = sc("hid", [128, 2, 2, 128])
            biasc = sc("biasc", [128, 4, 512])
            maskc = sc("maskc", [128, 4, 32])
            sC = sc("sC", [128, 512])
            cs = sc("cs", [128, 3, 16])
            d_pe = load(c, pe2[:, :, :], I["cmp_pe"])
            d_w2 = load(c, w2[:, :, :, :], I["cmp_w2"])
            d_bc = load(c, biasc[:, :, :], I["c_biasc"])
            d_mc = load(c, maskc[:, :, :], I["c_maskc"])
            zt = [gp.do(lambda e, i=i, blk=blk: e.memset(blk[i][:, :, :], 0.0)) for i in range(2)]
            btoks = []
            for i in range(2):
                bt = []
                pair = gemm_pair(c, [("w_kvc", 2 * i), ("w_kvc", 2 * i + 1)], c.hhi, c.hlo, H)
                for gpair in range(2):
                    b, tok = pair[gpair]
                    src = b.ap.rearrange("p (n q two) -> p two q n", q=8, two=2)
                    for a in range(2):
                        for par in range(2):
                            for hf in range(2):
                                o = blk[i][par * 64:par * 64 + 64, hf * 8:hf * 8 + 8, :].rearrange(
                                    "p q (g n) -> p q g n", g=4)[:, :, 2 * gpair + a, 0:31]
                                i0 = src[a * 64:a * 64 + 64, par, :, hf:hf + 31]
                                i1 = pe2[a * 64:a * 64 + 64, i, :].rearrange("p (q two) -> p two q", two=2)[
                                    :, par, hf * 8:hf * 8 + 8].unsqueeze(2).broadcast_to([64, 8, 31])
                                v = dve.do(lambda e, o=o, i0=i0, i1=i1: e.tensor_tensor(o, i0, i1, ALU.add),
                                           tok, d_pe, zt[i])
                    banks.give(b, v)
                    bt.append(v)
                btoks.append(bt)
            b, tok = proj("w_gate", 0, M=48)
            tg = act.do(lambda e, b=b, gT=gT: e.activation(gT[:, :], b.ap[0:48, :], ACT.Sigmoid), tok)
            banks.give(b, tg)
            b = banks.take()
            for t in range(4):
                tok = pe.do(lambda e, t=t, b=b, gT=gT, c=c: e.transpose(b.ap[:, t * 48:t * 48 + 48], gT[:, t * 128:t * 128 + 128],
                                                            c.ident[0:48, 0:48]), tg, b.free)
            tgate = dve.do(lambda e, b=b, gate=gate: e.tensor_copy(gate[:, :, :].rearrange("p a b -> p (a b)"), b.ap[:, 0:192]), tok)
            banks.give(b, tgate)
            for i in range(2):
                b = banks.take()
                for m in range(2):
                    for hf in range(2):
                        j, w1, _, wt = c.w.get(("cmp_w1", i, m, hf), ("cmp_w1", (i, m, hf), 0), 1024, split=False)
                        for q in range(8):
                            fn = lambda e, b=b, m=m, q=q, hf=hf, i=i, w1=w1, blk=blk: e.matmul(
                                b.ap[:, m * 128:m * 128 + 128], w1[:, q * 128:q * 128 + 128],
                                blk[i][:, hf * 8 + q, :], start=(hf == 0 and q == 0), stop=(hf == 1 and q == 7))
                            tok = pe.do(fn, wt, btoks[i], b.free)
                        c.w.release(j, tok)
                th = act.do(lambda e, b=b, i=i, hid=hid: e.activation(hid[:, i, :, :].rearrange("p a b -> p (a b)"),
                                                             b.ap[:, 0:256], ACT.Silu), tok)
                banks.give(b, th)
                b = banks.take()
                if i == 0:
                    for g in range(4):
                        for m in range(2):
                            fn = lambda e, g=g, m=m, b=b, w2=w2, hid=hid: e.matmul(
                                b.ap[(g % 2) * 64:(g % 2) * 64 + 64, (g // 2) * 32:(g // 2) * 32 + 32],
                                w2[:, 0, m, :], hid[:, 0, m, g * 32:g * 32 + 32], start=(m == 0), stop=(m == 1))
                            tok = pe.do(fn, th, d_w2, b.free)
                    tkc = act.do(lambda e, b=b, kcT=kcT: e.activation(kcT[:, :, :].rearrange("p a b -> p (a b)"),
                                                             b.ap[:, 0:64], ACT.Copy), tok)
                    banks.give(b, tkc)
                else:
                    for m in range(2):
                        fn = lambda e, m=m, b=b, hid=hid, w2=w2: e.matmul(b.ap[:, 0:64], hid[:, 1, m, :], w2[:, 1, m, :],
                                                          start=(m == 0), stop=(m == 1))
                        tok = pe.do(fn, th, d_w2, b.free)
                    tvc = act.do(lambda e, b=b, vc=vc: e.activation(vc[:, :], b.ap[:, 0:64], ACT.Copy), tok)
                    banks.give(b, tvc)
            tq = []
            for t in range(8):
                b, tok = proj("w_q", t)
                a = act.do(lambda e, b=b, t=t, qT=qT: e.activation(qT[:, t, :], b.ap, ACT.Copy, scale=0.125), tok)
                banks.give(b, a)
                tq.append(a)
            tk = []
            for i, dst in enumerate((ksT, kwT)):
                for g2 in range(2):
                    b, tok = proj("w_ksw", 2 * i + g2)
                    a = act.do(lambda e, b=b, dst=dst, g2=g2: e.activation(dst[:, g2, :], b.ap, ACT.Copy), tok)
                    banks.give(b, a)
                    tk.append(a)
            tv = []
            for t, b in enumerate(gemm_tok(c, "w_vsw", 0, 512, 2, c.hhi, c.hlo, H)):
                a = act.do(lambda e, b=b, t=t, vsw=vsw: e.activation(vsw[:, t, :], b.ap, ACT.Copy), b.tok)
                banks.give(b, a)
                tv.append(a)

            tz = []

            def z_tiles():
                for t in range(8):
                    for r in gemm_steps(c, "w_z0", t, KT, c.hhi, c.hlo, H):
                        yield
                    b, tok = r
                    a = act.do(lambda e, zs=zs, b=b, t=t: e.activation(zs[:, t, :], b.ap, ACT.Silu), tok)
                    banks.give(b, a)
                    tz.append(a)
                    yield
            c.side = z_tiles()
            tpc = []
            prev = None
            for j in range(4):
                for a in range(2):
                    b = banks.take()
                    for t in range(8):
                        r, g2 = t % 4, t // 4
                        col = (r * 2 + g2) * 32
                        fn = lambda e, b=b, t=t, a=a, j=j, col=col, qT=qT, kcT=kcT: e.matmul(
                            b.ap[:, col:col + 32], qT[a * 64:a * 64 + 64, t, j * 128:j * 128 + 128],
                            kcT[a * 64:a * 64 + 64, t // 4, :], start=True, stop=True)
                        tok = pe.do(fn, tq, tkc, b.free)
                    view = lambda ap, a=a: ap.rearrange("p (h a n) -> p h a n", a=2, n=32)[:, :, a, :]
                    v = dve.do(lambda e, b=b, j=j, view=view, sC=sC, biasc=biasc: e.tensor_tensor(
                        view(sC[:, :]), b.ap[:, 0:256].rearrange("p (h n) -> p h n", n=32), view(biasc[:, j, :]),
                        ALU.add), tok, d_bc, prev)
                    banks.give(b, v)
                c.tick(2)
                s3 = sC[:, :].rearrange("p (h n) -> p h n", n=32)
                bc = lambda ap: ap.unsqueeze(2).broadcast_to([128, 16, 32])
                v = dve.do(lambda e, s3=s3, cs=cs: e.tensor_reduce(cs[:, 0, :], s3, axis=AX, op=ALU.max), v)
                v = dve.do(lambda e, s3=s3, bc=bc, cs=cs: e.tensor_tensor(s3, s3, bc(cs[:, 0, :]), ALU.subtract), v)
                a = act.do(lambda e, sC=sC: e.activation(sC[:, :], sC[:, :], ACT.Exp), v)
                v = dve.do(lambda e, j=j, s3=s3, maskc=maskc: e.tensor_tensor(s3, s3, maskc[:, j, :].unsqueeze(1).broadcast_to(
                    [128, 16, 32]), ALU.mult), a, d_mc)
                v = dve.do(lambda e, s3=s3, cs=cs: e.tensor_reduce(cs[:, 1, :], s3, axis=AX, op=ALU.add), v)
                v = dve.do(lambda e, cs=cs: e.tensor_scalar(cs[:, 1, :], cs[:, 1, :], 1e-30, None, ALU.max), v)
                v = dve.do(lambda e, cs=cs: e.reciprocal(cs[:, 2, :], cs[:, 1, :]), v)
                v = dve.do(lambda e, j=j, cs=cs, gate=gate: e.tensor_tensor(
                    cs[:, 0, :].rearrange("p (r g) -> p r g", g=4), cs[:, 2, :].rearrange("p (r g) -> p r g", g=4),
                    gate[:, j, 0:16].rearrange("p (g r) -> p r g", g=4), ALU.mult), v, tgate)
                v = dve.do(lambda e, s3=s3, bc=bc, cs=cs: e.tensor_tensor(s3, s3, bc(cs[:, 0, :]), ALU.mult), v)
                c.tick(4)
                b = banks.take()
                for r in range(4):
                    tok = pe.do(lambda e, b=b, r=r, sC=sC, c=c: e.transpose(b.ap[:, r * 128:r * 128 + 128],
                                                                sC[:, r * 128:r * 128 + 128], c.ident[:, :]), v, b.free)
                prev = tok
                a = act.do(lambda e, b=b, j=j, pcT=pcT: e.activation(pcT[:, :, j * 128:j * 128 + 128],
                                                            b.ap.rearrange("p (r q) -> p r q", r=4), ACT.Copy), tok)
                banks.give(b, a)
                tpc.append(a)
            c.drain()
            cmpdone = [pe.now(), act.now(), dve.now(), gp.now()]
        if c.tap == "proj":
            return dict(qT=qT, ksT=ksT, vsw=vsw, gate=gate, kcT=kcT, vc=vc, pcT=pcT, zs=zs)

        with ExitStack() as cx:
            def sc(name, shape, dt=F32):
                return cx.enter_context(c.nc.sbuf_tensor(name, shape, dt))
            for q in (pe, act, dve, gp):
                q.wait(cmpdone)
            c.sp.wait(cmpdone)
            c.side = s5_prep(c, cx)
            Pb = Pool([sc(f"Pb{i}", [128, 2, 512])[:, :, :] for i in range(4)])
            pT = Pool([sc(f"pT{i}", [128, 4, 128])[:, :, :] for i in range(6)])
            bias = Pool([sc(f"bias{i}", [128, 512])[:, :] for i in range(2)])
            stp = Pool([sc(f"stp{i}", [128, 8])[:, :] for i in range(4)])
            units = [(t, a, j) for t in range(8) for a in range(2) for j in range(4)]
            live = {}
            ob = {}
            otok = []
            htoks = []

            def head_bias(t, a):
                h = (2 * (t // 4) + a) * 4 + t % 4
                bs = bias.take()
                slope = -float(np.exp2(np.float32(-8.0 * (h + 1) / 16)))
                bt = gp.do(lambda e, slope=slope, bs=bs, dist=dist: e.tensor_scalar(bs.ap, dist[:, :], slope, 1.0, ALU.mult, ALU.mult),
                           d_dist, bs.free)
                live["bias", t, a] = (bs, bt)

            head_bias(0, 0)

            def stage_a(u):
                t, a, j = units[u]
                g2, r = t // 4, t % 4
                h = (2 * g2 + a) * 4 + r
                W = 128 * (j + 1)
                bs, bt = live["bias", t, a]
                if j == 1 and u + 3 < len(units):
                    head_bias(*units[u + 3][0:2])
                P = Pb.take()
                s = stp.take()
                vs_ = []
                for br, K in enumerate((ksT, kwT)):
                    b = banks.take()
                    tok = pe.do(lambda e, b=b, K=K, qT=qT, t=t, g2=g2, W=W, a=a, j=j: e.matmul(
                        b.ap[:, 0:W], qT[a * 64:a * 64 + 64, t, j * 128:j * 128 + 128],
                        K[a * 64:a * 64 + 64, g2, 0:W], start=True, stop=True), tq[t], tk[2 * br + g2], b.free)
                    v = dve.do(lambda e, b=b, br=br, P=P, bs=bs, s=s, W=W: e.tensor_tensor_reduce(
                        out=P.ap[:, br, 0:W], in0=b.ap[:, 0:W], in1=bs.ap[:, 512 - W:512], scale=1.0, scalar=-3.0e38,
                        op0=ALU.add, op1=ALU.max, accum_out=s.ap[:, br:br + 1]), tok, bt, P.free, s.free)
                    banks.give(b, v)
                if j == 3:
                    bias.give(bs, v)
                v = dve.do(lambda e, s=s: e.tensor_scalar(s.ap[:, 2:4], s.ap[:, 0:2], -1.0, None, ALU.mult), v)
                for br in range(2):
                    x = act.do(lambda e, br=br, P=P, W=W, s=s: e.activation(P.ap[:, br, 0:W], P.ap[:, br, 0:W], ACT.Exp,
                                                            bias=s.ap[:, 2 + br:3 + br],
                                                            accum_out=s.ap[:, 4 + br:5 + br]), v)
                live[u] = (P, s, x)

            def stage_b(u):
                t, a, j = units[u]
                g2, r = t // 4, t % 4
                h = (2 * g2 + a) * 4 + r
                W = 128 * (j + 1)
                P, s, x = live[u]
                v = dve.do(lambda e, s=s: e.reciprocal(s.ap[:, 6:8], s.ap[:, 4:6]), x)
                gv = gate[:, j, 16 + h:48:16]
                v = dve.do(lambda e, gv=gv, s=s: e.tensor_tensor(s.ap[:, 6:8], s.ap[:, 6:8], gv, ALU.mult), v, tgate)
                g_ = [gp.do(lambda e, P=P, s=s, W=W: e.tensor_scalar(
                    P.ap[:, 0, 0:W], P.ap[:, 0, 0:W], s.ap[:, 6:7], 1.0, ALU.mult, ALU.mult), v, x)]
                g_.append(act.do(lambda e, P=P, W=W, s=s: e.activation(P.ap[:, 1, 0:W], P.ap[:, 1, 0:W], ACT.Copy,
                                                        scale=s.ap[:, 7:8]), v, x))
                stp.give(s, *g_)
                live[u] = (P, g_)

            def stage_c(u):
                t, a, j = units[u]
                g2, r = t // 4, t % 4
                g = 2 * g2 + a
                P, g_ = live[u]
                if (t, a, j) == (t, 0, 0):
                    ob[t] = banks.take()
                hold = []
                for br in range(2):
                    b = banks.take()
                    for k in range(j + 1):
                        tok = pe.do(lambda e, b=b, br=br, k=k, P=P, c=c: e.transpose(
                            b.ap[:, k * 128:k * 128 + 128], P.ap[:, br, k * 128:k * 128 + 128], c.ident[:, :]),
                            g_[br], b.free)
                    p = pT.take()
                    n = (j + 1) * 128
                    dst = p.ap.rearrange("p k q -> p (k q)")[:, 0:n]
                    if br:
                        x = act.do(lambda e, b=b, dst=dst, n=n: e.activation(dst, b.ap[:, 0:n], ACT.Copy), tok, p.free)
                    else:
                        x = dve.do(lambda e, b=b, dst=dst, n=n: e.tensor_copy(dst, b.ap[:, 0:n]), tok, p.free)
                    banks.give(b, x)
                    hold.append((p, x))
                Pb.give(P, tok)
                live[u] = hold

            def stage_d(u):
                t, a, j = units[u]
                g2, r = t // 4, t % 4
                g = 2 * g2 + a
                hold = live[u]
                o = ob[t]
                oap = o.ap[a * 64:a * 64 + 64, j * 128:j * 128 + 128]
                pe.do(lambda e, oap=oap, vc=vc, pcT=pcT, r=r, g=g, j=j: e.matmul(oap, vc[32 * g:32 * g + 31, :], pcT[32 * g:32 * g + 31, r, j * 128:j * 128 + 128],
                                         start=True, stop=False, skip_group_check=True), tvc, tpc[j], o.free)
                for br in range(2):
                    p, x = hold[br]
                    for k in range(j + 1):
                        tok = pe.do(lambda e, br=br, k=k, p=p, oap=oap, vsw=vsw, j=j, g=g: e.matmul(
                            oap, vsw[:, k, br * 256 + g * 64:br * 256 + g * 64 + 64], p.ap[:, k, :], start=False,
                            stop=(br == 1 and k == j), skip_group_check=True), x, tv)
                    pT.give(p, tok)
                if (a, j) == (1, 3):
                    v = dve.do(lambda e, zs=zs, o=o, t=t: e.tensor_tensor(zs[:, t, :], zs[:, t, :], o.ap, ALU.mult), tok, tz[t])
                    banks.give(o, v)
                    htoks.append(v)

            n = len(units)
            for i in range(n + 5):
                if i < n:
                    stage_a(i)
                c.tick()
                if 1 <= i <= n:
                    stage_b(i - 1)
                c.tick()
                if i >= 5:
                    stage_d(i - 5)
                if 3 <= i <= n + 2:
                    stage_c(i - 3)
                c.tick()
            c.drain()
            free = [list(c.s5t.values()), pe.now(), gp.now(), act.now()]
            free[0] = [x for y in free[0] for x in (y if isinstance(y, list) else [y])]
            htoks = [split(c, zs[:, t, :], c.hhi(t), c.hlo(t), htoks[t], free) for t in range(8)]
            out = []
            c.ss.start()
            pair = gemm_pair(c, [("w_o0", 0), ("w_o0", 1)], c.hhi, c.hlo, htoks)
            for t in range(8):
                b, tok = pair[t] if t < 2 else gemm(c, "w_o0", t, KT, c.hhi, c.hlo, htoks)
                v = dve.do(lambda e, b=b, t=t, X=X: e.tensor_tensor(X[:, t, :], X[:, t, :], b.ap, ALU.add), tok, xtoks[t])
                banks.give(b, v)
                out.append(v)
                c.ss.add(X[:, t, :], v)
            c.hfree = tok
    barrier(c)
    return out


HOLD = 4


def s5_prep(c, ctx):
    pe, act, dve, gp, banks = c.pe, c.act, c.dve, c.gp, c.banks
    I = c.ins
    M, A_, S_ = ALU.mult, ALU.add, ALU.subtract

    def sb(name, shape, dt=F32):
        return ctx.enter_context(c.nc.sbuf_tensor(name, shape, dt))

    par = sb("par", [128, 3, 32])
    sm = sb("sm", [128, 19, 32])
    pw = sb("pw", [128, 2, 9, 32])
    pr = sb("pr", [128, 2, 8, 32])
    e8 = sb("e8", [128, 2, 32])
    Bq = c.at("Bq", [128, 2, 8, 16], 30208)
    Cq = c.at("Cq", [128, 2, 8, 16], 31232)
    Bb = sb("Bb", [128, 2, 8, 16])
    Bd = sb("Bd", [128, 2, 8, 32])
    CA = c.at("CA", [128, 2, 8, 9, 16], 0)
    WT = c.at("WT", [128, 8, 8, 16], 9216)
    Ws = sb("Ws", [128, 4, 128])
    Kp = c.at("Kp", [64, 4, 16, 16], 13312)
    Rt = c.at("Rt", [128, 2, 8, 64], 17408)
    tA = c.at("tA", [128, 8, 144], 21504)
    tG = c.at("tG", [128, 8, 128], 26112)
    dp = load(c, par[:, :, :], I["s5_par"])

    def V(fn, *t):
        return dve.do(fn, *t, dve.now())

    def tt(o, a, b, op, *t):
        return V(lambda e, o=o, a=a, b=b, op=op: e.tensor_tensor(o, a, b, op), *t)

    def ts(o, a, s1, op, s2=None, op2=None, *t):
        if op2 is None:
            return V(lambda e, o=o, a=a, s1=s1, op=op: e.tensor_scalar(o, a, s1, None, op), *t)
        return V(lambda e, o=o, a=a, s1=s1, s2=s2, op=op, op2=op2: e.tensor_scalar(o, a, s1, s2, op, op2), *t)

    def cmul(ore, oim, xr, xi, yr, yi, t1, t2, *t):
        tt(t1, xr, yr, M, *t)
        tt(t2, xi, yi, M, *t)
        tt(ore, t1, t2, S_)
        tt(t1, xr, yi, M)
        tt(t2, xi, yr, M)
        return tt(oim, t1, t2, A_)

    s = lambda i: sm[:, i, :]
    lre, lim, ldt = par[:, 0, :], par[:, 1, :], par[:, 2, :]
    a = act.do(lambda e, ldt=ldt, s=s: e.activation(s(0), ldt, ACT.Exp), dp)
    ts(s(1), lre, -1e-4, ALU.min, None, None, dp, a)
    tt(s(2), s(1), s(0), M)
    v = tt(s(3), lim, s(0), M)
    a = act.do(lambda e, s=s: e.activation(s(4), s(2), ACT.Exp), v)
    c.mag8_tok = act.do(lambda e, s=s, c=c: e.activation(c.mag8[:, :], s(2), ACT.Exp, scale=8.0), v)
    yield
    big = float(np.float32(1.5 * 2 ** 23))
    ts(s(5), s(3), float(np.float32(1 / (2 * np.pi))), M, big, A_)
    ts(s(5), s(5), big, S_)
    c1 = 6.28125
    c2 = float(np.float32(np.round((2 * np.pi - c1) * 2 ** 20) / 2 ** 20))
    c3 = float(np.float32(2 * np.pi - c1 - c2))
    cur = s(3)
    for cc in (c1, c2, c3):
        ts(s(6), s(5), cc, M)
        tt(s(7), cur, s(6), S_)
        cur = s(7)
    lim_ = 3.1415925
    ts(s(7), s(7), lim_, ALU.min, -lim_, ALU.max)
    ts(s(8), s(7), -1.0, M)
    tt(s(8), s(7), s(8), ALU.max)
    v = ts(s(8), s(8), -1.0, M, float(np.float32(np.pi / 2)), A_)
    a1 = act.do(lambda e, s=s: e.activation(s(9), s(8), ACT.Sin), v)
    a2 = act.do(lambda e, s=s: e.activation(s(10), s(7), ACT.Sin), v)
    yield
    cos, sin = s(9), s(10)
    P = lambda i, k: pw[:, i, k, :]
    V(lambda e, P=P: e.memset(P(0, 0), 1.0))
    V(lambda e, P=P: e.memset(P(1, 0), 0.0))
    tt(P(0, 1), s(4), cos, M, a, a1)
    tt(P(1, 1), s(4), sin, M, a2)
    t1, t2 = s(11), s(12)
    cmul(P(0, 2), P(1, 2), P(0, 1), P(1, 1), P(0, 1), P(1, 1), t1, t2)
    yield
    for k in (3, 4):
        cmul(P(0, k), P(1, k), P(0, k - 2), P(1, k - 2), P(0, 2), P(1, 2), t1, t2)
    yield
    for k in (5, 6, 7, 8):
        cmul(P(0, k), P(1, k), P(0, k - 4), P(1, k - 4), P(0, 4), P(1, 4), t1, t2)
        yield
    for k in range(8):
        vpr = V(lambda e, pr=pr, pw=pw, k=k: e.tensor_copy(pr[:, :, k, :], pw[:, :, 7 - k, :]))
    yield
    E = (s(13), s(14))
    cmul(E[0], E[1], cos, sin, cos, sin, t1, t2)
    cmul(s(15), s(16), E[0], E[1], E[0], E[1], t1, t2)
    cmul(e8[:, 0, :], e8[:, 1, :], s(15), s(16), s(15), s(16), t1, t2)
    yield
    tt(s(11), s(1), s(1), M)
    tt(s(12), lim, lim, M)
    tt(s(11), s(11), s(12), A_)
    V(lambda e, s=s: e.reciprocal(s(11), s(11)))
    ts(s(12), P(0, 1), -1.0, A_)
    tt(s(13), s(12), s(1), M)
    tt(s(14), P(1, 1), lim, M)
    tt(s(13), s(13), s(14), A_)
    tt(s(17), s(13), s(11), M)
    tt(s(13), P(1, 1), s(1), M)
    tt(s(14), s(12), lim, M)
    tt(s(13), s(13), s(14), S_)
    tt(s(18), s(13), s(11), M)
    V(lambda e, Bd=Bd: e.memset(Bd[:, :, :, :], 0.0))
    zero = V(lambda e, Kp=Kp: e.memset(Kp[:, :, 0:8, :], 0.0))
    yield
    cafree = wsfree = kfree = rfree = bfree = None
    dB = load(c, Bq[:, :, :, :], I["s5_B"][0])
    dC = load(c, Cq[:, :, :, :], I["s5_C"][0])
    for b4 in range(4):
        p8 = slice(8 * b4, 8 * b4 + 8)
        bc = lambda ap, n: ap.unsqueeze(2).broadcast_to([128, 8, n])
        vbb = cmul(Bb[:, 0, :, :], Bb[:, 1, :, :], Bq[:, 0, :, :], Bq[:, 1, :, :], bc(sm[:, 17, p8], 16),
                   bc(sm[:, 18, p8], 16), tA[:, :, 0:16], tA[:, :, 16:32], dB, bfree)
        for i in range(2):
            for h in range(2):
                vb = V(lambda e, Bd=Bd, Bb=Bb, i=i, h=h: e.tensor_copy(Bd[h * 64:h * 64 + 64, i, :, h * 16:h * 16 + 16],
                                               Bb[h * 64:h * 64 + 64, i, :, :]))
        yield
        x3 = tA[:, :, :].rearrange("p q (k n) -> p q k n", k=9)
        g3 = tG[:, :, :].rearrange("p q (k n) -> p q k n", k=8)

        def cplx(eng, x, w, n, y, i, o, *t):
            wk = lambda i: w[:, i, 0:n, p8].rearrange("p k q -> p q k").unsqueeze(3).broadcast_to([128, 8, n, 16])
            yk = lambda i: y[:, i, :, :].unsqueeze(2).broadcast_to([128, 8, n, 16])
            op = A_ if i else S_
            for hf in (slice(0, 4), slice(4, 8)):
                y0, y1, w0, w1, oo, xx = [ap[:, hf] for ap in (yk(0), yk(1), wk(i), wk(1 - i), o, x)]
                eng.do(lambda e, oo=oo, y0=y0, w0=w0, M=M: e.tensor_tensor(oo, y0, w0, M), *t, eng.now())
                yield
                eng.do(lambda e, xx=xx, y1=y1, w1=w1, M=M: e.tensor_tensor(xx, y1, w1, M), eng.now())
                yield
                eng.do(lambda e, oo=oo, xx=xx, op=op: e.tensor_tensor(oo, oo, xx, op), eng.now())
                yield
        yield from cplx(dve, x3, pw, 9, Cq, 0, CA[:, 0, :, :, :], cafree, dC)
        yield from cplx(dve, x3, pw, 9, Cq, 1, CA[:, 1, :, :, :])
        vc_ = dve.now()
        if b4 < 3:
            dB = load(c, Bq[:, :, :, :], I["s5_B"][b4 + 1], vbb)
            dC = load(c, Cq[:, :, :, :], I["s5_C"][b4 + 1], vc_)
        yield
        vca = ts(CA[:, 1, :, :, :], CA[:, 1, :, :, :], -1.0, M)
        d = c.sp.dma(lambda e, b4=b4, c=c, CA=CA: e.dma_start(c.dCA[b4], CA[:, :, :, :, :].rearrange("p i q k n -> p (i q k n)")),
                     c.dsem(), vca)
        c.s5t["CA", b4] = d
        for _ in range(HOLD):
            yield
        ak = []
        for hf in range(2):
            bk = banks.take()
            for q in range(4):
                p = 4 * hf + q
                for i in range(2):
                    tok = pe.do(lambda e, Bd=Bd, bk=bk, i=i, p=p, CA=CA, hf=hf, q=q: e.matmul(
                        bk.ap[hf * 32:hf * 32 + 32, q * 128:q * 128 + 128], Bd[:, i, p, :],
                        CA[:, i, p, 0:8, :].rearrange("p k n -> p (k n)"), start=(i == 0), stop=(i == 1)),
                        vca, vb, bk.free)
            a = act.do(lambda e, Kp=Kp, bk=bk, hf=hf: e.activation(
                Kp[hf * 32:hf * 32 + 32, :, 8:16, :].rearrange("p q k n -> p q (k n)"),
                bk.ap[hf * 32:hf * 32 + 32, :].rearrange("p (q n) -> p q n", q=4), ACT.Copy), tok, zero, kfree)
            banks.give(bk, a)
            yield
        cafree = [d, tok]
        bfree = tok
        ks = Sem(c.tsems[b4])
        for hf in range(2):
            for h in range(2):
                dst = c.dK[b4][:, 8 * hf:8 * hf + 8, :].rearrange("c (q h) n -> c q h n", h=2)[:, :, h, :]
                src = Kp[hf * 32 + h * 16:hf * 32 + h * 16 + 16, :, :, :].rearrange("p q k n -> p q (k n)")
                kfree = c.sp.dma(lambda e, dst=dst, src=src: e.dma_start(dst, src), ks, a)
        c.s5t["K", b4] = kfree
        yield
        for i in range(2):
            yield from cplx(gp, g3, pr, 8, Bb, i, WT[:, :, :, :], pe.now(), vbb, vpr)
            vwt = gp.now()
            for _ in range(HOLD):
                yield
            for hf in range(2):
                bk = banks.take()
                for q in range(4):
                    p = 4 * hf + q
                    tok = pe.do(lambda e, bk=bk, c=c, WT=WT, q=q, p=p: e.transpose(
                        bk.ap[:, q * 128:q * 128 + 128], WT[:, p, :, :].rearrange("p k n -> p (k n)"),
                        c.ident[:, :]), vwt, bk.free)
                aw = act.do(lambda e, bk=bk, Ws=Ws: e.activation(Ws[:, :, :].rearrange("p q n -> p (q n)"), bk.ap, ACT.Copy),
                            tok, wsfree)
                banks.give(bk, aw)
                o = 1024 * i + 512 * hf
                wsfree = c.sp.dma(lambda e, b4=b4, c=c, o=o, Ws=Ws: e.dma_start(c.dW[b4][:, o:o + 512],
                                                        Ws[:, :, :].rearrange("p q n -> p (q n)")), c.dsem(), aw)
                c.s5t["W", b4] = c.s5t.get(("W", b4), []) + [wsfree]
                yield
        bfree = [bfree, vwt]
        R = lambda i, n0, n1: Rt[:, i, :, n0:n1]
        V(lambda e, Rt=Rt, e8=e8, p8=p8: e.tensor_copy(Rt[:, :, :, 0], e8[:, :, p8]), rfree)
        n = 1
        while n < 64:
            bl = lambda i: Rt[:, i, :, n - 1:n].broadcast_to([128, 8, n])
            vr = cmul(R(0, n, 2 * n), R(1, n, 2 * n), R(0, 0, n), R(1, 0, n), bl(0), bl(1),
                      tA[:, :, 0:n], tA[:, :, 64:64 + n])
            n *= 2
            yield
        rfree = c.sp.dma(lambda e, b4=b4, c=c, Rt=Rt: e.dma_start(c.dR[b4], Rt[:, :, :, :].rearrange("p i q n -> p (i q n)")),
                         c.dsem(), vr)
        c.s5t["R", b4] = rfree
        yield


def s5(c, X, xtoks, H):
    pe, act, dve, gp, banks = c.pe, c.act, c.dve, c.gp, c.banks
    M, A_, S_ = ALU.mult, ALU.add, ALU.subtract
    with ExitStack() as ctx:
        def sb(name, shape, dt=F32):
            return ctx.enter_context(c.nc.sbuf_tensor(name, shape, dt))

        mats = Pool([(sb(f"mCA{i}", [128, 2, 8, 9, 16]), sb(f"mT{i}", [128, 16, 128])) for i in range(2)])
        turns = Pool([(sb("mW", [128, 2, 8, 128]), sb("mR", [128, 2, 8, 64]))])
        D0 = sb("D0", [128, 8, 64])
        wre = sb("wre", [128, 8, 64])
        wim = sb("wim", [128, 8, 64])
        xt = sb("xt", [128, 8, 64])
        Xs = Pool([sb(f"Xs{i}", [128, 2, 8, 64]) for i in range(2)])
        Us = Pool([sb(f"U{i}", [128, 16, 64]) for i in range(2)])
        Yt = sb("Yt", [128, 16, 64])
        zy = sb("zy", [128, 8, S])
        yt = c.sq
        Y = sb("Y5", [128, 8, S])
        z0 = dve.do(lambda e, D0=D0: e.memset(D0[:, :, 0:1], 0.0))
        for x in Xs.slots:
            z1 = dve.do(lambda e, x=x: e.memset(x.ap[:, :, :, 0:1], 0.0))

        def V(fn, *t):
            return dve.do(fn, *t, dve.now())

        def tt(o, a, b, op, *t):
            return V(lambda e, o=o, a=a, b=b, op=op: e.tensor_tensor(o, a, b, op), *t)

        fl = lambda t, n: t[tuple(slice(None) for _ in t.shape)].rearrange(n)

        def fetch_turn(b4):
            m = turns.take()
            W, R = m.ap
            sm = Sem(c.tsems[4 + b4])
            c.sp.dma(lambda e, fl=fl, W=W, b4=b4, c=c: e.dma_start(fl(W, "p i q n -> p (i q n)"), c.dW[b4]), sm, c.s5t["W", b4], m.free)
            d = c.sp.dma(lambda e, fl=fl, R=R, b4=b4, c=c: e.dma_start(fl(R, "p i q n -> p (i q n)"), c.dR[b4]), sm, c.s5t["R", b4])
            return m, d

        def fetch(b4):
            m = mats.take()
            CA, T = m.ap
            sm = Sem(c.tsems[16 + b4])
            c.sp.dma(lambda e, fl=fl, CA=CA, b4=b4, c=c: e.dma_start(fl(CA, "p i q k n -> p (i q k n)"), c.dCA[b4]), sm, c.s5t["CA", b4], m.free)
            for st in range(8):
                dst = T[st * 16:st * 16 + 16, :, :]
                src = c.dK[b4][:, :, (8 - st) * 16:(16 - st) * 16]
                d = c.sp.dma(lambda e, dst=dst, src=src: e.dma_start(dst, src), sm, c.s5t["K", b4])
            return m, d

        uts = {}

        def u_tile(k):
            b, tok = first[k] if k < 2 else gemm(c, "w_s5", k, KT, c.hhi, c.hlo, H)
            a_ = act.do(lambda e, Y=Y, b=b, k=k: e.activation(Y[:, k, :], b.ap, ACT.Copy), tok)
            banks.give(b, a_)
            uts[k] = (Y[:, k, :], a_)

        def z_tile(k):
            b, tok = gemm(c, "w_s5", 8 + k, KT, c.hhi, c.hlo, H)
            a_ = act.do(lambda e, zy=zy, b=b, k=k: e.activation(zy[:, k, :], b.ap, ACT.Silu), tok)
            banks.give(b, a_)
            tz.append(a_)

        tz, ytoks = [], []
        mfetch, live = {}, {}
        mturn = {0: fetch_turn(0)}
        mfetch[0] = fetch(0)
        mfetch[1] = fetch(1)
        first = gemm_pair(c, [("w_s5", 0), ("w_s5", 1)], c.hhi, c.hlo, H)

        def rows(b4):
            uds = Sem(c.tsems[8 + b4])
            for kk in range(2):
                u, ut = uts[2 * b4 + kk]
                dw = c.sp.dma(lambda e, u=u, c=c, b4=b4, kk=kk: e.dma_start(c.du[b4, kk], u), uds, ut)
            U = Us.take()
            for st in range(8):
                dst = U.ap[st * 16:st * 16 + 16, :, :]
                src = c.du[b4].rearrange("k (g c) (s n) -> s c (k g) n", c=16, s=8)[st]
                du = c.sp.dma(lambda e, dst=dst, src=src: e.dma_start(dst, src), uds, dw, U.free)
            live[b4] = (U, du)

        def states(b4):
            U, du = live[b4]
            m, dm = mturn[b4]
            W, R = m.ap
            vb_ = [banks.take(), banks.take()]
            for i in range(2):
                for g in range(16):
                    p, h = g // 2, g % 2
                    tok = pe.do(lambda e, W=W, i=i, p=p, U=U, g=g, vb_=vb_, h=h: e.matmul(
                        vb_[i].ap[h * 64:h * 64 + 64, p * 64:p * 64 + 64], W[:, i, p, h * 64:h * 64 + 64],
                        U.ap[:, g, :], start=True, stop=True), dm, du, vb_[i].free)
            p8 = slice(8 * b4, 8 * b4 + 8)
            X_ = Xs.take()
            V(lambda e, D0=D0, c=c, p8=p8: e.tensor_copy(D0[:, :, 1:64], c.mag8[:, p8].unsqueeze(2).broadcast_to([128, 8, 63])),
              c.mag8_tok, z0)
            vr = vb_[0].ap.rearrange("p (q n) -> p q n", q=8)
            vi = vb_[1].ap.rearrange("p (q n) -> p q n", q=8)
            tt(wre[:, :, :], vr, R[:, 0, :, :], M, tok, dm)
            tt(xt[:, :, :], vi, R[:, 1, :, :], M)
            tt(wre[:, :, :], wre[:, :, :], xt[:, :, :], A_)
            tt(wim[:, :, :], vi, R[:, 0, :, :], M)
            v = tt(xt[:, :, :], vr, R[:, 1, :, :], M)
            banks.give(vb_[0], v)
            banks.give(vb_[1], v)
            tt(wim[:, :, :], wim[:, :, :], xt[:, :, :], S_)
            for w_ in (wre, wim):
                fl = w_[:, :, :].rearrange("p q n -> p (q n)")
                V(lambda e, fl=fl, M=M, A_=A_, D0=D0: e.tensor_tensor_scan(fl, D0[:, :, :].rearrange("p q n -> p (q n)"), fl, 0.0, M, A_))
            lo_ = lambda ap: ap[:, :, 0:63]
            x63 = xt[:, :, 0:63]
            xs = X_.ap
            tt(xs[:, 0, :, 1:64], lo_(wre), lo_(R[:, 0, :, :]), M, X_.free, z1)
            tt(x63, lo_(wim), lo_(R[:, 1, :, :]), M)
            tt(xs[:, 0, :, 1:64], xs[:, 0, :, 1:64], x63, S_)
            tt(xs[:, 1, :, 1:64], lo_(wre), lo_(R[:, 1, :, :]), M)
            tt(x63, lo_(wim), lo_(R[:, 0, :, :]), M)
            vx = tt(xs[:, 1, :, 1:64], xs[:, 1, :, 1:64], x63, A_)
            turns.give(m, tok, vx)
            if b4 < 3:
                mturn[b4 + 1] = fetch_turn(b4 + 1)
            live[b4] = (U, du, X_, vx)

        yfree = [None]

        def outputs(b4):
            U, du, X_, vx = live[b4]
            m, dm = mfetch[b4]
            CA, T = m.ap
            for h in range(2):
                yb = banks.take()
                for q in range(8):
                    g = 2 * q + h
                    o = yb.ap[:, q * 64:q * 64 + 64]
                    pe.do(lambda e, o=o, T=T, g=g, U=U: e.matmul(o, T[:, g, :], U.ap[:, g, :], start=True, stop=False), dm, du, yb.free)
                    for i in range(2):
                        tok = pe.do(lambda e, o=o, X_=X_, i=i, q=q, CA=CA, h=h: e.matmul(
                            o, CA[h * 64:h * 64 + 64, i, q, 1:9, :].rearrange("p k n -> p (k n)"),
                            X_.ap[h * 64:h * 64 + 64, i, q, :], start=False, stop=(i == 1)), vx)
                ay = act.do(lambda e, h=h, yb=yb, Yt=Yt: e.activation(
                    Yt[:, :, :].rearrange("p (q h) n -> p q h n", h=2)[:, :, h, :],
                    yb.ap.rearrange("p (q n) -> p q n", q=8), ACT.Copy), tok, yfree[0])
                banks.give(yb, ay)
            mats.give(m, tok, vx)
            Us.give(U, tok)
            Xs.give(X_, tok)
            if b4 + 2 < 4:
                mfetch[b4 + 2] = fetch(b4 + 2)
            yds = Sem(c.tsems[12 + b4])
            for st in range(8):
                dst = c.dy[b4].rearrange("k (g c) (s n) -> s c (k g) n", c=16, s=8)[st]
                src = Yt[st * 16:st * 16 + 16, :, :]
                dyw = c.sp.dma(lambda e, dst=dst, src=src: e.dma_start(dst, src), yds, ay)
            ys = [yt.take(), yt.take()]
            for kk in range(2):
                y = ys[kk]
                dy = c.sp.dma(lambda e, y=y, c=c, b4=b4, kk=kk: e.dma_start(y.ap, c.dy[b4, kk]), yds, dyw, y.free)
            yfree[0] = dyw
            live[b4] = (ys, dy)

        def finish(b4):
            ys, dy = live[b4]
            for kk in range(2):
                k = 2 * b4 + kk
                y = ys[kk]
                u, ut = uts[k]
                v = dve.do(lambda e, u=u, M=M, A_=A_, y=y, c=c, k=k: e.scalar_tensor_tensor(u, u, c.g_d[:, k:k + 1], y.ap, M, A_), dy, ut)
                yt.give(y, v)
                ytoks.append(act.do(lambda e, u=u: e.activation(u, u, ACT.Gelu_apprx_tanh), v))

        order = "u0 u1 r0 u2 u3 r1 s0 u4 u5 o0 r2 s1 u6 f0 u7 o1 r3 s2 z0 f1 z1 z2 o2 s3 z3 f2 z4 z5 o3 z6 z7 f3"
        fns = dict(u=u_tile, r=rows, s=states, o=outputs, z=z_tile, f=finish)
        Us.slots[0].free = Us.slots[1].free = None
        for step in order.split():
            fns[step[0]](int(step[1]))
        hd = pe.now()
        ytoks = [split(c, Y[:, k, :], c.hhi(k), c.hlo(k), ytoks[k], hd) for k in range(8)]
        gv = []
        for k in range(8):
            (ba, ta), (bb, tb) = pair_or_two(c, k == 0, ("w_glu", k), ("w_glu", 8 + k), ytoks)
            y = yt.take()
            a = act.do(lambda e, y=y, bb=bb: e.activation(y.ap, bb.ap, ACT.Sigmoid), tb, y.free)
            banks.give(bb, a)
            v = dve.do(lambda e, M=M, zy=zy, y=y, k=k: e.tensor_tensor(zy[:, k, :], zy[:, k, :], y.ap, M), a, tz[k])
            yt.give(y, v)
            v = dve.do(lambda e, M=M, zy=zy, ba=ba, k=k: e.tensor_tensor(zy[:, k, :], zy[:, k, :], ba.ap, M), ta, v)
            banks.give(ba, v)
            gv.append(v)
        hd = pe.now()
        g2 = [split(c, zy[:, k, :], c.hhi(k), c.hlo(k), gv[k], hd) for k in range(8)]
        out = []
        c.ss.start()
        pair = gemm_pair(c, [("w_o1", 0), ("w_o1", 1)], c.hhi, c.hlo, g2)
        for k in range(8):
            b, tok = pair[k] if k < 2 else gemm(c, "w_o1", k, KT, c.hhi, c.hlo, g2)
            x = X[:, k, :].rearrange("p (n s) -> p s n", s=8)
            v = dve.do(lambda e, x=x, A_=A_, b=b: e.tensor_tensor(x, x, b.ap.rearrange("p (s n) -> p s n", s=8), A_),
                       tok, xtoks[k])
            banks.give(b, v)
            out.append(v)
            c.ss.add(X[:, k, :], v)
        c.hfree = tok
    barrier(c)
    return out


def add_normed(c, X, xtoks, Y, ytoks, g, after):
    r = c.ss.inv(0, 1.0 / D)
    c.nfree = c.pe.now()
    c.ss.start()
    out = []
    for k in range(KT + 1):
        if k < KT:
            v = c.dve.do(lambda e, Y=Y, g=g, k=k, c=c: e.scalar_tensor_tensor(
                Y[:, k, :], Y[:, k, :], g[:, k:k + 1], c.rs[:, :], ALU.mult, ALU.mult), r, ytoks[k])
            out.append(v)
        if k:
            j = k - 1
            out[j] = c.dve.do(lambda e, X=X, Y=Y, j=j: e.tensor_tensor(X[:, j, :], X[:, j, :], Y[:, j, :], ALU.add), out[j], xtoks[j])
            after(j, out[j])
    c.nfree = out[-1]
    return out


def split_scaled(c, x, g, hi, lo, *toks):
    a = c.act.do(lambda e, hi=hi, x=x, g=g: e.activation(hi, x, ACT.Copy, scale=g), *toks)
    v = c.dve.do(lambda e, lo=lo, x=x, g=g, hi=hi: e.scalar_tensor_tensor(lo, x, g, hi.bitcast(F32), ALU.mult, ALU.subtract), a, *toks)
    return [a, v]


def branch(c, n, bhi, blo, btoks, H, mg, mtoks, out):
    for k in range(8):
        for r in gemm_steps(c, "w_bgate", 8 * n + k, KT, c.hhi, c.hlo, H):
            yield
        bg, tg = r
        s = c.sq.take()
        a = c.act.do(lambda e, s=s, bg=bg: e.activation(s.ap, bg.ap, ACT.Sigmoid), tg, s.free)
        c.banks.give(bg, a)
        for r in gemm_steps(c, "w_branch", 8 * n + k, KT, bhi, blo, btoks):
            yield
        bp, tp = r
        if n == 0:
            v = c.dve.do(lambda e, mg=mg, s=s, bp=bp, k=k: e.tensor_tensor(mg[:, k, :], s.ap, bp.ap, ALU.mult), a, tp)
        else:
            v = c.dve.do(lambda e, s=s, bp=bp: e.tensor_tensor(s.ap, s.ap, bp.ap, ALU.mult), a, tp)
        c.banks.give(bp, v)
        if n:
            v = c.dve.do(lambda e, mg=mg, s=s, k=k: e.tensor_tensor(mg[:, k, :], mg[:, k, :], s.ap, ALU.add), v, mtoks[k])
        c.sq.give(s, v)
        out.append(v)
        yield
    c.bfree = c.pe.now()


def gate_tiles(c, name, dst, toks, free, H):
    for k in range(8):
        for r in gemm_steps(c, name, k, KT, c.hhi, c.hlo, H):
            yield
        b, tok = r
        toks[k] = c.act.do(lambda e, dst=dst, b=b, k=k: e.activation(dst[:, k, :], b.ap, ACT.Silu), tok, free)
        c.banks.give(b, toks[k])
        yield


def both(*steps):
    for s in steps:
        yield from s


def evacuate(c, name, col, hi, lo, H, dst, func=ACT.Copy, scale=1.0, M=128, free=None, made=None):
    b, tok = made or gemm(c, name, col, KT, hi, lo, H, M=M)
    a = c.act.do(lambda e, dst=dst, func=func, scale=scale, b=b, M=M: e.activation(dst, b.ap[0:M, :], func, scale=scale), tok, free)
    c.banks.give(b, a)
    return a


def second(c, X, xtoks):
    pe, act, dve, gp, banks = c.pe, c.act, c.dve, c.gp, c.banks
    I = c.ins
    r = c.ss.inv(0, 1.0 / D)
    c.nfree = pe.now()
    c.ss.start()
    xt = []
    for k in range(KT):
        xt.append(dve.do(lambda e, X=X, k=k, c=c: e.scalar_tensor_tensor(X[:, k, :], X[:, k, :], c.g_fin[:, k:k + 1], c.rs[:, :],
                                                          ALU.mult, ALU.mult), r))
        if k:
            c.ss.add(X[:, k - 1, :], xt[k - 1])
    c.ss.add(X[:, 7, :], xt[7])
    c.nfree = xt[-1]
    H = norm(c, X, xt, c.g_pre, c.hhi, c.hlo, c.hfree)
    ev = lambda name, col, dst, **kw: evacuate(c, name, col, c.hhi, c.hlo, H, dst, **kw)
    QS = float(128 ** -0.5)

    with ExitStack() as ctx:
        def sb(name, shape, dt=F32):
            return ctx.enter_context(c.nc.sbuf_tensor(name, shape, dt))
        Bh = sb("Bh", [128, 8, S], F32R)
        Bl = sb("Bl", [128, 8, S], F32R)
        bhi = lambda k: Bh[:, k, :]
        blo = lambda k: Bl[:, k, :]
        mg = sb("mg", [128, 8, S])
        of = sb("of", [128, 8, S])

        def rows_v(name, dst):
            toks = []
            for m in range(2):
                for t, b in enumerate(gemm_tok(c, name, m, 512, 2, c.hhi, c.hlo, H)):
                    a = act.do(lambda e, dst=dst, b=b, t=t, m=m: e.activation(dst[:, t, m * 512:m * 512 + 512], b.ap, ACT.Copy), b.tok)
                    banks.give(b, a)
                    toks.append(a)
            return toks

        def head_rs(tiles, tok, rs, eps):
            s0, s1 = c.sq2.take(), c.sq2.take()
            a0 = act.do(lambda e, s0=s0, tiles=tiles: e.activation(s0.ap, tiles[0], ACT.Square), tok, s0.free)
            a1 = act.do(lambda e, s1=s1, tiles=tiles: e.activation(s1.ap, tiles[1], ACT.Square), tok, s1.free)
            v = dve.do(lambda e, s0=s0, s1=s1: e.tensor_tensor(s0.ap, s0.ap, s1.ap, ALU.add), a0, a1)
            c.sq2.give(s1, v)
            c.tick()
            b = banks.take()
            p = pe.do(lambda e, b=b, s0=s0, c=c: e.matmul(b.ap, c.ones[:, :], s0.ap, start=True, stop=True), v, b.free)
            c.sq2.give(s0, p)
            return rsqrt(c, rs, b, 1.0 / 256, eps, p)

        with ExitStack() as cx:
            def sc(name, shape, dt=F32):
                return cx.enter_context(c.nc.sbuf_tensor(name, shape, dt))
            q = sc("rq", [128, 4, S])
            kk = sc("rk", [128, 4, S])
            v_ = sc("rv", [128, 4, 1024])
            dec = sc("dec", [128, 4, S])
            sT = Pool([sc(f"sT{i}", [128, S])[:, :] for i in range(3)])
            ot = Pool([sc(f"ro{i}", [128, 2, S])[:, :, :] for i in range(2)])
            hr = sc("hr", [128, S])
            dd = load(c, dec[:, :, :], I["c_decay"])
            pair = gemm_pair(c, [("w_r", 0), ("w_r", 1)], c.hhi, c.hlo, H)
            tq = [ev("w_r", h, q[:, h, :], scale=QS, made=pair[h] if h < 2 else None) for h in range(4)]
            tk = [ev("w_r", 4 + h, kk[:, h, :]) for h in range(4)]
            tv = rows_v("w_rv", v_)
            btoks = []
            hrfree = None
            gt = {}
            c.side = gate_tiles(c, "w_rg", of, gt, None, H)
            for h in range(4):
                ob = [banks.take(), banks.take()]
                for kt in range(4):
                    W = S - 128 * kt
                    b = banks.take()
                    tok = pe.do(lambda e, kk=kk, q=q, b=b, h=h, W=W, kt=kt: e.matmul(b.ap[:, 0:W], kk[:, h, kt * 128:kt * 128 + 128],
                                                   q[:, h, kt * 128:S], start=True, stop=True), tq[h], tk[h], b.free)
                    s = sT.take()
                    v = dve.do(lambda e, dec=dec, s=s, b=b, h=h, W=W: e.tensor_tensor(s.ap[:, 0:W], b.ap[:, 0:W], dec[:, h, 0:W], ALU.mult),
                               tok, dd, s.free)
                    banks.give(b, v)
                    c.tick()
                    for e2 in range(2):
                        col = h * 256 + e2 * 128
                        tok = pe.do(lambda e, v_=v_, kt=kt, s=s, ob=ob, e2=e2, col=col, W=W: e.matmul(ob[e2].ap[:, kt * 128:S], v_[:, kt, col:col + 128],
                                                       s.ap[:, 0:W], start=(kt == 0), stop=(kt == 3)),
                                    v, tv, ob[e2].free)
                    sT.give(s, tok)
                o = ot.take()
                for e2 in range(2):
                    a = act.do(lambda e, o=o, e2=e2, ob=ob: e.activation(o.ap[:, e2, :], ob[e2].ap, ACT.Copy), tok, o.free)
                    banks.give(ob[e2], a)
                c.tick()
                b = banks.take()
                for e2 in range(2):
                    tok = pe.do(lambda e, b=b, c=c, o=o, e2=e2: e.matmul(b.ap, c.ones[:, :], o.ap[:, e2, :], start=(e2 == 0),
                                                   stop=(e2 == 1)), a, b.free)
                for e2 in range(2):
                    v = dve.do(lambda e, b=b, o=o, e2=e2: e.scalar_tensor_tensor(o.ap[:, e2, :], b.ap, -1.0 / 256, o.ap[:, e2, :],
                                                                ALU.mult, ALU.add), tok)
                banks.give(b, v)
                r = head_rs([o.ap[:, 0, :], o.ap[:, 1, :]], [v, hrfree], hr[:, :], 1)
                for e2 in range(2):
                    k = 2 * h + e2
                    while k not in gt:
                        c.tick()
                    x = o.ap[:, e2, :]
                    v = dve.do(lambda e, x=x, hr=hr, c=c, k=k: e.scalar_tensor_tensor(x, x, c.g_retw[:, k:k + 1], hr[:, :],
                                                                ALU.mult, ALU.mult), r)
                    hrfree = v
                    v = dve.do(lambda e, x=x, of=of, c=c, k=k: e.scalar_tensor_tensor(x, x, c.g_retb[:, k:k + 1], of[:, k, :],
                                                                ALU.add, ALU.mult), v, gt[k])
                    btoks.append(split(c, x, bhi(k), blo(k), v))
                ot.give(o, *btoks[-1])
            c.drain()
            done = [x.now() for x in (pe, act, dve, gp)]
        mt = []
        gt = {}
        c.side = both(gate_tiles(c, "w_gg", of, gt, done, H), branch(c, 0, bhi, blo, btoks, H, mg, None, mt))

        with ExitStack() as cx:
            def sc(name, shape, dt=F32):
                return cx.enter_context(c.nc.sbuf_tensor(name, shape, dt))
            for x in (pe, act, dve, gp, c.sp):
                x.wait(done)
            qs = Pool([sc(f"gq{i}", [128, S])[:, :] for i in range(2)])
            ks = Pool([sc(f"gk{i}", [128, S])[:, :] for i in range(2)])
            v_ = sc("gv", [128, 4, 1024])
            ga = sc("ga", [16, S])
            al = sc("al", [16, 512])
            kd = sc("kd", [128, 4, 128])
            St = sc("St", [128, 7, 256])
            At = sc("At", [128, 4, 64])
            mk = sc("mk", [128, 4, 64])
            rm = sc("rm", [128, S])
            ta, tb, tc = [sc(f"gt{i}", [128, S]) for i in range(3)]
            cd = sc("cd", [128, 8])
            o = sc("go", [128, 2, S])
            hr = sc("ghr", [128, S])
            d1 = load(c, al[:, :], I["alpha2"])
            d2 = load(c, mk[:, :, :], I["c_tri"])
            d3 = load(c, rm[:, :], I["c_reset"])
            tga = ev("w_ga", 0, ga[:, :], M=16)
            def heads(h):
                q, k = qs.take(), ks.take()
                a = ev("w_g", h, q.ap, scale=QS, free=q.free)
                b = ev("w_g", 4 + h, k.ap, free=k.free)
                return q, a, k, b
            nxt = heads(0)
            tv = rows_v("w_gv", v_)
            z = dve.do(lambda e, At=At: e.memset(At[:, :, :], 0.0))
            btoks = []
            pfree = gfree = None
            for h in range(4):
                qslot, tq, kslot, tk = nxt
                q, kk = qslot.ap, kslot.ap
                b = banks.take()
                tok = pe.do(lambda e, b=b, al=al, ga=ga, h=h: e.matmul(b.ap, al[:, h * 128:h * 128 + 128], ga[:, :], start=True, stop=True),
                            d1, tga, b.free)
                v = dve.do(lambda e, ta=ta, b=b, c=c, h=h: e.tensor_scalar(ta[:, :], b.ap, c.galpha[:, h:h + 1], None, ALU.add), tok, gfree)
                banks.give(b, v)
                a = act.do(lambda e, tb=tb, ta=ta: e.activation(tb[:, :], ta[:, :], ACT.Abs), v, gfree)
                a = act.do(lambda e, tb=tb: e.activation(tb[:, :], tb[:, :], ACT.Exp, scale=-1.0), a)
                a = act.do(lambda e, tb=tb, c=c: e.activation(tb[:, :], tb[:, :], ACT.Ln, bias=c.ones[:, 0:1]), a)
                v = dve.do(lambda e, ta=ta, tb=tb: e.scalar_tensor_tensor(ta[:, :], ta[:, :], 0.0, tb[:, :], ALU.min,
                                                            ALU.subtract), a, v)
                v = dve.do(lambda e, ta=ta: e.tensor_scalar(ta[:, :], ta[:, :], 1.0 / 16, -1.0, ALU.mult, ALU.max), v)
                c.tick(2)
                v = dve.do(lambda e, tb=tb, rm=rm, ta=ta: e.tensor_tensor_scan(tb[:, :], rm[:, :], ta[:, :], 0.0, ALU.mult, ALU.add),
                           v, d3)
                a1 = act.do(lambda e, ta=ta, tb=tb: e.activation(ta[:, :], tb[:, :], ACT.Exp), v)
                a2 = act.do(lambda e, tc=tc, tb=tb: e.activation(tc[:, :], tb[:, :], ACT.Exp, scale=-1.0), v, gfree)
                t3 = tb[:, :].rearrange("p (n s) -> p n s", s=64)
                a3 = act.do(lambda e, cd=cd, t3=t3: e.activation(cd[:, :], t3[:, :, 63], ACT.Exp), v, gfree)
                vq = dve.do(lambda e, q=q, ta=ta: e.tensor_tensor(q, q, ta[:, :], ALU.mult), a1, tq)
                v = dve.do(lambda e, t3=t3, ta=ta: e.tensor_tensor(
                    ta[:, :].rearrange("p (n s) -> p n s", s=64), t3[:, :, 63:64].broadcast_to([128, 8, 64]), t3,
                    ALU.subtract), vq, a2, a3)
                a = act.do(lambda e, ta=ta: e.activation(ta[:, :], ta[:, :], ACT.Exp), v)
                v = dve.do(lambda e, kk=kk, ta=ta: e.tensor_tensor(ta[:, :], ta[:, :], kk, ALU.mult), a, tk)
                vk = dve.do(lambda e, kk=kk, tc=tc: e.tensor_tensor(kk, kk, tc[:, :], ALU.mult), v)
                c.tick(4)
                b = banks.take()
                for t in range(4):
                    tok = pe.do(lambda e, ta=ta, b=b, c=c, t=t: e.transpose(b.ap[:, t * 128:t * 128 + 128], ta[:, t * 128:t * 128 + 128],
                                                      c.ident[:, :]), v, b.free)
                gfree = tok
                akd = act.do(lambda e, b=b, kd=kd: e.activation(kd[:, :, :].rearrange("p t d -> p (t d)"), b.ap, ACT.Copy),
                             tok, pfree)
                banks.give(b, akd)
                b = banks.take()
                for n in range(8):
                    p, t = 64 * (n % 2), n // 2
                    tok = pe.do(lambda e, kk=kk, q=q, b=b, p=p, t=t, n=n: e.matmul(b.ap[p:p + 64, t * 64:t * 64 + 64], kk[:, n * 64:n * 64 + 64],
                                                   q[:, n * 64:n * 64 + 64], start=True, stop=True), vk, b.free)
                va = dve.do(lambda e, At=At, mk=mk, b=b: e.copy_predicated(At[:, :, :], mk[:, :, :].bitcast(U32),
                                                        b.ap[:, 0:256].rearrange("p (t i) -> p t i", t=4)),
                            tok, d2, z, pfree)
                banks.give(b, va)
                c.tick()
                last = None
                for n in range(7):
                    p, t = 64 * (n % 2), n // 2
                    b = banks.take()
                    tok = pe.do(lambda e, kd=kd, v_=v_, b=b, t=t, p=p, h=h: e.matmul(b.ap[:, 0:256], kd[p:p + 64, t, :],
                                                   v_[p:p + 64, t, h * 256:h * 256 + 256], start=True, stop=True),
                                akd, tv, b.free)
                    if n == 0:
                        last = dve.do(lambda e, St=St, b=b: e.tensor_copy(St[:, 0, :], b.ap[:, 0:256]), tok, pfree)
                    else:
                        last = dve.do(lambda e, St=St, cd=cd, n=n, b=b: e.scalar_tensor_tensor(
                            St[:, n, :], St[:, n - 1, :], cd[:, n:n + 1], b.ap[:, 0:256], ALU.mult, ALU.add),
                            tok, last, a3)
                    banks.give(b, last)
                if h < 3:
                    nxt = heads(h + 1)
                c.tick(3)
                ao = None
                for e2 in range(2):
                    col = h * 256 + e2 * 128
                    bb = [banks.take(), banks.take()]
                    for n in range(8):
                        p, t = 64 * (n % 2), n // 2
                        o_ = bb[n % 2].ap[:, t * 64:t * 64 + 64]
                        tok = pe.do(lambda e, o_=o_, v_=v_, At=At, t=t, n=n, p=p, col=col: e.matmul(o_, v_[p:p + 64, t, col:col + 128], At[p:p + 64, t, :],
                                                       start=True, stop=(n == 0)), va, bb[n % 2].free)
                        if n:
                            tok = pe.do(lambda e, o_=o_, St=St, q=q, n=n, e2=e2: e.matmul(o_, St[:, n - 1, e2 * 128:e2 * 128 + 128],
                                                           q[:, n * 64:n * 64 + 64], start=False, stop=True), last)
                    for i in range(2):
                        ao = act.do(lambda e, i=i, o=o, e2=e2, bb=bb: e.activation(
                            o[:, e2, :].rearrange("p (t i s) -> p t i s", i=2, s=64)[:, :, i, :],
                            bb[i].ap[:, 0:256].rearrange("p (t s) -> p t s", t=4), ACT.Copy), tok, pfree)
                        banks.give(bb[i], ao)
                qs.give(qslot, tok, vk)
                ks.give(kslot, tok, vk)
                c.tick(2)
                r = head_rs([o[:, 0, :], o[:, 1, :]], [ao, pfree], hr[:, :], 0)
                for e2 in range(2):
                    k = 2 * h + e2
                    while k not in gt:
                        c.tick()
                    x = o[:, e2, :]
                    v = dve.do(lambda e, x=x, hr=hr, c=c, k=k: e.scalar_tensor_tensor(x, x, c.g_gla[:, k:k + 1], hr[:, :],
                                                                ALU.mult, ALU.mult), r)
                    btoks.append(dve.do(lambda e, x=x, of=of, k=k: e.tensor_tensor(of[:, k, :], of[:, k, :], x, ALU.mult), v, gt[k]))
                pfree = [tok, gfree, btoks[-1]]
                gfree = [gfree, last, vk]
            c.drain()
            done = [x.now() for x in (pe, act, dve, gp)]
        btoks = [split(c, of[:, k, :], bhi(k), blo(k), btoks[k], c.bfree) for k in range(8)]
        done = done + btoks
        m2 = []
        c.side = branch(c, 1, bhi, blo, btoks, H, mg, mt, m2)

        with ExitStack() as cx:
            def sc(name, shape, dt=F32):
                return cx.enter_context(c.nc.sbuf_tensor(name, shape, dt))
            for x in (pe, act, dve, gp, c.sp):
                x.wait(done)
            q = sc("sq_", [128, 8, S])
            kk = sc("sk_", [128, 2, S])
            v_ = sc("sv_", [128, 4, 256])
            dist = sc("dist2", [128, 256])
            sink = sc("sink", [128, 16])
            Pb = Pool([sc(f"Ps{i}", [128, 4, 256])[:, :, :] for i in range(3)])
            pT = Pool([sc(f"pTs{i}", [128, 8, 128])[:, :, :] for i in range(2)])
            bias = Pool([sc(f"bs{i}", [128, 256])[:, :] for i in range(3)])
            stp = Pool([sc(f"ss{i}", [128, 5, 4])[:, :, :] for i in range(4)])
            dd = load(c, dist[:, :], I["c_dist2"])
            ds = load(c, sink[:, :], I["sinks"])
            tq = [ev("w_sq", t, q[:, t, :], scale=0.125) for t in range(8)]
            tk = [ev("w_sk", t, kk[:, t, :]) for t in range(2)]
            tv = []
            for t, b in enumerate(gemm_tok(c, "w_sv", 0, 256, 4, c.hhi, c.hlo, H)):
                a = act.do(lambda e, v_=v_, t=t, b=b: e.activation(v_[:, t, :], b.ap[:, 0:256], ACT.Copy), b.tok)
                banks.give(b, a)
                tv.append(a)
            live, ob, btoks = {}, {}, []
            units = [(t, a) for t in range(8) for a in range(2)]
            span = [(0, 128)] + [(128 * (j - 1), 256) for j in (1, 2, 3)]

            def stage_a(u):
                t, a = units[u]
                g2, r = t // 4, t % 4
                h = (2 * g2 + a) * 4 + r
                bs = bias.take()
                slope = -float(np.exp2(np.float32(-8.0 * (h + 1) / 16)))
                bt = gp.do(lambda e, slope=slope, bs=bs, dist=dist: e.tensor_scalar(bs.ap, dist[:, :], slope, 1.0, ALU.mult, ALU.mult), dd, bs.free)
                P = Pb.take()
                s = stp.take()
                for jj in range(2):
                    b = banks.take()
                    for j in (2 * jj, 2 * jj + 1):
                        k0, W = span[j]
                        col = (j % 2) * 256
                        tok = pe.do(lambda e, q=q, kk=kk, b=b, t=t, g2=g2, col=col, k0=k0, W=W, a=a, j=j: e.matmul(
                            b.ap[:, col:col + W], q[a * 64:a * 64 + 64, t, j * 128:j * 128 + 128],
                            kk[a * 64:a * 64 + 64, g2, k0:k0 + W], start=True, stop=True), tq[t], tk[g2], b.free)
                    for j in (2 * jj, 2 * jj + 1):
                        k0, W = span[j]
                        col = (j % 2) * 256
                        v = dve.do(lambda e, P=P, j=j, b=b, bs=bs, s=s, W=W, col=col: e.tensor_tensor_reduce(
                            out=P.ap[:, j, 0:W], in0=b.ap[:, col:col + W], in1=bs.ap[:, 256 - W:256], scale=1.0,
                            scalar=-3.0e38, op0=ALU.add, op1=ALU.max, accum_out=s.ap[:, 0, j:j + 1]),
                            tok, bt, P.free, s.free)
                    banks.give(b, v)
                bias.give(bs, v)
                hs = sink[:, h:h + 1]
                v = dve.do(lambda e, hs=hs, s=s: e.tensor_scalar(s.ap[:, 1, :], s.ap[:, 0, :], hs, -1.0, ALU.max, ALU.mult), v, ds)
                for j in range(4):
                    k0, W = span[j]
                    x = act.do(lambda e, P=P, j=j, W=W, s=s: e.activation(P.ap[:, j, 0:W], P.ap[:, j, 0:W], ACT.Exp,
                                                      bias=s.ap[:, 1, j:j + 1], accum_out=s.ap[:, 2, j:j + 1]), v)
                x = act.do(lambda e, hs=hs, s=s: e.activation(s.ap[:, 3, :], s.ap[:, 1, :], ACT.Exp, bias=hs), v)
                live[u] = (P, s, x)

            def stage_b(u):
                P, s, x = live[u]
                v = dve.do(lambda e, s=s: e.tensor_tensor(s.ap[:, 2, :], s.ap[:, 2, :], s.ap[:, 3, :], ALU.add), x)
                v = dve.do(lambda e, s=s: e.reciprocal(s.ap[:, 4, :], s.ap[:, 2, :]), v)
                for j in range(4):
                    W = span[j][1]
                    g_ = gp.do(lambda e, P=P, j=j, s=s, W=W: e.tensor_scalar(P.ap[:, j, 0:W], P.ap[:, j, 0:W], s.ap[:, 4, j:j + 1], 1.0,
                                                         ALU.mult, ALU.mult), v, x)
                stp.give(s, g_)
                live[u] = (P, g_)

            def stage_c(u):
                t, a = units[u]
                g = 2 * (t // 4) + a
                P, g_ = live[u]
                if a == 0:
                    ob[t] = banks.take()
                p = pT.take()
                blocks = [(j, k) for j in range(4) for k in range(span[j][1] // 128)]
                x = None
                for i in range(2):
                    b = banks.take()
                    part = blocks[4 * i:4 * i + 4]
                    for n, (j, k) in enumerate(part):
                        tok = pe.do(lambda e, b=b, P=P, j=j, c=c, n=n, k=k: e.transpose(b.ap[:, n * 128:n * 128 + 128],
                                                          P.ap[:, j, k * 128:k * 128 + 128], c.ident[:, :]), g_, b.free)
                    w = len(part) * 128
                    dst = p.ap.rearrange("p k q -> p (k q)")[:, i * 512:i * 512 + w]
                    if i:
                        y = act.do(lambda e, dst=dst, b=b, w=w: e.activation(dst, b.ap[:, 0:w], ACT.Copy), tok, p.free)
                    else:
                        y = dve.do(lambda e, dst=dst, b=b, w=w: e.tensor_copy(dst, b.ap[:, 0:w]), tok, p.free)
                    banks.give(b, y)
                    x = [x, y]
                Pb.give(P, tok)
                live[u] = (p, x, blocks)

            def stage_d(u):
                t, a = units[u]
                g = 2 * (t // 4) + a
                p, x, blocks = live[u]
                o = ob[t]
                for n, (j, k) in enumerate(blocks):
                    nb = span[j][1] // 128
                    kt = span[j][0] // 128 + k
                    tok = pe.do(lambda e, v_=v_, o=o, kt=kt, p=p, n=n, k=k, nb=nb, a=a, j=j, g=g: e.matmul(
                        o.ap[a * 64:a * 64 + 64, j * 128:j * 128 + 128], v_[:, kt, g * 64:g * 64 + 64], p.ap[:, n, :],
                        start=(k == 0), stop=(k == nb - 1), skip_group_check=True), x, tv, o.free)
                pT.give(p, tok)
                if a == 1:
                    y = act.do(lambda e, of=of, o=o, t=t: e.activation(of[:, t, :], o.ap, ACT.Copy), tok, done)
                    banks.give(o, y)
                    btoks.append(y)

            n = len(units)
            for i in range(n + 3):
                if i < n:
                    stage_a(i)
                c.tick()
                if 1 <= i <= n:
                    stage_b(i - 1)
                c.tick()
                if i >= 3:
                    stage_d(i - 3)
                if 2 <= i <= n + 1:
                    stage_c(i - 2)
                c.tick()
        c.drain()
        btoks = [split(c, of[:, k, :], bhi(k), blo(k), btoks[k], c.bfree) for k in range(8)]
        mt = []
        c.side = branch(c, 2, bhi, blo, btoks, H, mg, m2, mt)
        c.drain()
        mt = [split(c, mg[:, k, :], bhi(k), blo(k), mt[k], c.bfree) for k in range(8)]
        yt = []
        c.ss.start()
        for k in range(8):
            b, tok = gemm(c, "w_o2", k, KT, bhi, blo, mt)
            a = act.do(lambda e, mg=mg, b=b, k=k: e.activation(mg[:, k, :], b.ap, ACT.Copy), tok, mt)
            banks.give(b, a)
            yt.append(a)
            c.ss.add(mg[:, k, :], a)
        hd = pe.now()
        H = []

        def after(k, tok):
            H.append(split_scaled(c, X[:, k, :], c.g_fpre[:, k:k + 1], c.hhi(k), c.hlo(k), tok, hd))
            c.ss.add(X[:, k, :], tok)
        xt = add_normed(c, X, xt, mg, yt, c.g_post, after)
        done = [x.now() for x in (pe, act, dve, gp)]
    with ExitStack() as ctx:
        def sb(name, shape, dt=F32):
            return ctx.enter_context(c.nc.sbuf_tensor(name, shape, dt))
        for x in (pe, act, dve, gp):
            x.wait(done)
        Fh = sb("Fh", [128, 22, S], F32R)
        Fl = sb("Fl", [128, 22, S], F32R)
        y = sb("fy", [128, 8, S])
        ft = Pool([sb(f"ft{i}", [128, S])[:, :] for i in range(3)])
        ftoks = []
        rt = None
        for k in range(22):
            (bg, tg), (bu, tu) = pair_or_two(c, k == 0, ("w_fg", k), ("w_fu", k), H)
            if k == 0:
                rt = c.ss.inv(0, 1.0 / D)
            s = ft.take()
            v = dve.do(lambda e, s=s, bg=bg, c=c: e.tensor_tensor(s.ap, bg.ap, c.rs[:, :], ALU.mult), tg, s.free, rt)
            banks.give(bg, v)
            a = act.do(lambda e, s=s: e.activation(s.ap, s.ap, ACT.Silu), v)
            v = dve.do(lambda e, s=s, bu=bu: e.tensor_tensor(s.ap, s.ap, bu.ap, ALU.mult), a, tu)
            banks.give(bu, v)
            v = gp.do(lambda e, s=s, c=c: e.tensor_tensor(s.ap, s.ap, c.rs[:, :], ALU.mult), v)
            h2 = split(c, s.ap, Fh[:, k, :], Fl[:, k, :], v)
            ft.give(s, *h2)
            ftoks.append(h2)
        c.nfree = [pe.now(), v]
        yt = []
        c.ss.start()
        for k in range(8):
            b, tok = gemm(c, "w_fd", k, 22, lambda i: Fh[:, i, :], lambda i: Fl[:, i, :], ftoks)
            a = act.do(lambda e, y=y, b=b, k=k: e.activation(y[:, k, :], b.ap, ACT.Copy), tok)
            banks.give(b, a)
            yt.append(a)
            c.ss.add(y[:, k, :], a)
        so = Sem(c.osem)
        sent = []

        def send(k, tok):
            sent.append(c.sp.dma(lambda e, k=k, X=X, c=c: e.dma_start(c.out[k], X[:, k, :]), so, tok))
        xt = add_normed(c, X, xt, y, yt, c.g_fpost, send)
        t = sent[-1]
        c.sp.wait(t)
    return xt


def more(x, A, f, tiles, rows):
    A["w_s5"] = tiles(x["l1_w_in"])
    A["w_glu"] = tiles(x["l1_w_glu"])
    A["w_o1"] = tiles(x["l1_w_out"])
    pair = lambda v: v.reshape(32, 2, 64, *v.shape[2:]).transpose(1, 2, 0, *range(3, v.ndim + 1)).reshape(
        128, 32, *v.shape[2:])
    dt = np.broadcast_to(x["l1_log_dt"][:, None], (64, 64))
    A["s5_par"] = f(np.stack([pair(x["l1_lambda_re"]), pair(x["l1_lambda_im"]), pair(dt)], 1))
    cut = lambda r, i: f(np.stack([r, i], 1).reshape(128, 2, 4, 8, 16).transpose(2, 0, 1, 3, 4))
    A["s5_B"] = cut(pair(x["l1_b_re"]), pair(x["l1_b_im"]))
    A["s5_C"] = cut(pair(x["l1_c_re"].transpose(0, 2, 1)), pair(x["l1_c_im"].transpose(0, 2, 1)))
    w = x["w_in_2"][0]
    at = np.concatenate([[0], np.cumsum([512, 512, 1024, 1024, 512, 512, 1024, 1024, 16, 1024, 256, 256, 3072])])
    s = lambda i, j=None: w[:, at[i]:at[(j or i) + 1]]
    hd = np.arange(64)
    order = np.concatenate([((2 * (t // 4) + a) * 4 + t % 4) * 64 + hd for t in range(8) for a in range(2)])
    A["w_r"] = tiles(s(0, 1))
    A["w_rv"] = rows(s(2), 512, 2)
    A["w_rg"] = tiles(s(3))
    A["w_g"] = tiles(s(4, 5))
    A["w_gv"] = rows(s(6), 512, 2)
    A["w_gg"] = tiles(s(7))
    A["w_ga"] = tiles(s(8), 16)
    A["w_sq"] = tiles(s(9)[:, order])
    A["w_sk"] = tiles(s(10))
    A["w_sv"] = rows(s(11), 256, 4)
    A["w_bgate"] = tiles(s(12))
    wb = x["w_branch_2"][0]
    A["w_branch"] = tiles(np.concatenate([wb[0], wb[1], wb[2][order]], 1))
    A["w_o2"] = tiles(x["w_out_2"][0])
    A["w_fg"] = tiles(x["ffn_w_gate_2"][0])
    A["w_fu"] = tiles(x["ffn_w_up_2"][0])
    A["w_fd"] = tiles(x["ffn_w_down_2"][0])
    A["alpha2"] = f(x["gla_w_alpha2_2"][0])
    A["sinks"] = f(np.broadcast_to(x["attn_sinks_2"], (128, 16)))
    p, m = np.arange(128)[:, None], np.arange(512)[None, :]
    lg = np.log1p(-np.exp2(-5.0 - np.arange(4)))
    rel = (m - p)[:, None, :]
    A["c_decay"] = f(np.where(rel >= 0, np.exp(np.maximum(rel, 0) * lg[None, :, None]), 0.0))
    j, i = np.arange(128)[:, None] % 64, np.arange(64)[None, :]
    A["c_tri"] = f(np.broadcast_to((j <= i)[:, None, :], (128, 4, 64)))
    A["c_reset"] = f(np.broadcast_to(np.arange(512) % 64 != 0, (128, 512)))
    d = 128 + p - np.arange(256)[None, :]
    A["c_dist2"] = f(np.where((d >= 0) & (d < 128), d, np.float32(MASKED)))


def program(nc, ins, out, plan, tap=None):
    c = Core()
    c.nc, c.ins, c.out, c.tap = nc, ins, out, tap
    with ExitStack() as ctx:
        def sb(name, shape, dt=F32):
            return ctx.enter_context(nc.sbuf_tensor(name, shape, dt))

        def sem(name):
            return ctx.enter_context(nc.semaphore(name))

        c.pe, c.act, c.dve, c.gp, c.sp = [Queue(sem(n)) for n in ("s_pe", "s_act", "s_dve", "s_gp", "s_sp")]
        c.queues = [c.pe, c.act, c.dve, c.gp, c.sp]
        c.sems = [Sem(sem(f"s_d{i}")) for i in range(64)]
        c.tsems = [sem(f"s_t{i}") for i in range(20)]
        c.osem = sem("s_out")
        c.sem_at = 0
        c.dma_toks = []

        def dsem():
            s = c.sems[c.sem_at]
            c.sem_at += 1
            return s
        c.dsem = dsem
        c.du = nc.dram_tensor("scratch_u", [4, 2, 128, S], F32, kind="Internal").ap()
        c.dy = nc.dram_tensor("scratch_y", [4, 2, 128, S], F32, kind="Internal").ap()
        base = (nc.sbuf_base + 31) // 32 * 32
        sb("hspan", [128, 8192])
        c.at = lambda name, shape, off, dt=F32: nc.alloc_sbuf_tensor_at(name, shape, dt, offset=base + off)
        raw = [sb(f"wraw{i}", [128, 1024]) for i in range(RR)]
        hi = [sb(f"whi{i}", [128, 1024], F32R) for i in range(RH)]
        lo = [sb(f"wlo{i}", [128, 1024], F32R) for i in range(RH)]
        c.w = Weights(ins, c.sp, c.act, c.dve, raw, hi, lo, [Sem(sem(f"s_w{i}")) for i in range(RR)], plan)
        c.banks = Pool([ctx.enter_context(nc.psum_tensor(f"bank{i}", [128, 512], F32))[:, :] for i in range(8)])
        X = sb("X", [128, 8, S])
        Hh = c.at("Hh", [128, 8, S], 0, F32R)
        Hl = c.at("Hl", [128, 8, S], 16384, F32R)
        c.hhi = lambda k: Hh[:, k, :]
        c.hlo = lambda k: Hl[:, k, :]
        c.nacc = sb("nacc", [128, S])
        c.rs = sb("rs", [128, S])
        c.nfree = None
        c.sq = Pool([sb(f"sq{i}", [128, S])[:, :] for i in range(2)])
        c.ones = sb("ones", [128, 128])
        c.ident = sb("ident", [128, 128])
        c.epst = sb("epst", [128, 2])
        vecs = sb("vecs", [128, 16, 8])
        c.g_l0, c.g_l1, c.g_fin, c.g_pre, c.g_post, c.g_fpre, c.g_fpost, c.g_retw, c.g_retb, c.g_gla, c.g_d = [
            vecs[:, i, :] for i in range(11)]
        c.galpha = vecs[:, 11, 0:4]
        c.mag8 = sb("mag8", [128, 32])
        c.sq2 = Pool([sb(f"sqb{i}", [128, S])[:, :] for i in range(2)])
        c.ss = Squares(c)
        c.s5t = {}
        c.side = None

        def tick(n=1):
            for _ in range(n):
                if c.side is not None:
                    next(c.side, None)
        c.tick = tick

        def drain():
            for _ in c.side:
                pass
            c.side = None
        c.drain = drain
        c.dCA, c.dW, c.dR = [nc.dram_tensor("scratch_" + n, [4, 128, w], F32, kind="Internal").ap()
                             for n, w in (("CA", 2304), ("W", 2048), ("R", 1024))]
        c.dK = nc.dram_tensor("scratch_K", [4, 16, 16, 256], F32, kind="Internal").ap()
        xt = []
        for k in range(8):
            xt.append(load(c, X[:, k, :], ins["xT"][k]))
            c.ss.add(X[:, k, :], xt[-1])
        dv = load(c, vecs[:, 0:12, :], ins["vecs"])
        di = load(c, c.ident[:, :], ins["c_ident"])
        m1 = c.dve.do(lambda e, c=c: e.memset(c.ones[:, :], 1.0))
        m2 = c.dve.do(lambda e, c=c: e.memset(c.epst[:, 0:1], 1e-6))
        m3 = c.dve.do(lambda e, c=c: e.memset(c.epst[:, 1:2], 1e-5))
        c.gtok = dv
        for q in (c.pe, c.act, c.dve):
            q.wait(dv, di, m3)
        r = nsa(c, X, xt)
        taps = {}
        if tap is None or tap not in ("proj", "nsa"):
            H = norm(c, X, r, c.g_l1, c.hhi, c.hlo, c.hfree, perm=True)
            r = s5(c, X, r, H)
            if tap != "s5":
                r = second(c, X, r)
        if tap:
            if isinstance(r, dict):
                taps = {n: t for n, t in r.items()}
            else:
                taps = {"X": X}
        if taps:
            end = [q.now() for q in c.queues]
            fs = Sem(sem("s_fin"))
            for n, t in taps.items():
                o = nc.dram_tensor("tap_" + n, list(t.shape), F32, kind="ExternalOutput").ap()
                c.sp.dma(lambda e, o=o, t=t: e.dma_start(o, t[tuple(slice(None) for _ in t.shape)]), fs, end)
            c.sp.wait((fs, fs.n))
        if plan is None:
            return c.w.asked
        block = ctx.enter_context(nc.Block())
        block.tensor(lambda e, c=c: c.pe.play(e))
        block.scalar(lambda e, c=c: c.act.play(e))
        block.vector(lambda e, c=c: c.dve.play(e))
        block.gpsimd(lambda e, c=c: c.gp.play(e))
        block.sync(lambda e, c=c: c.sp.play(e))


SHAPES = {}


def build(nc, arrays, tap=None):
    def declare(n):
        return {k: n.dram_tensor("in_" + k, list(a.shape), F32, kind="ExternalInput").ap() for k, a in arrays.items()}

    def result(n):
        return n.dram_tensor("out_0", [8, 128, S], F32, kind="ExternalOutput").ap()
    scratch = bass.Bass(dynamic_dma_scratch_size=RING)
    plan = program(scratch, declare(scratch), result(scratch), None, tap)
    program(nc, declare(nc), result(nc), plan, tap)


def layout(x):
    f = lambda a: np.ascontiguousarray(a, dtype=np.float32)

    def tiles(w, M=128):
        K, C = w.shape
        return f(w.reshape(K // 128, 128, C // M, M).transpose(2, 1, 0, 3).reshape(C // M, 128, K // 128 * M))

    def rows(w, n, kper):
        K, C = w.shape
        return f(w.reshape(K // 128 // kper, kper, 128, C // n, n).transpose(3, 0, 2, 1, 4).reshape(
            C // n, K // 128 // kper, 128, kper * n))

    def vec(v):
        return f(v.reshape(-1, 128).T)

    A = {}
    A["xT"] = f(x["x"][0].T.reshape(8, 128, S))
    w = x["l0_w_in"]
    hd = np.arange(64)
    order = np.concatenate([((2 * (t // 4) + a) * 4 + t % 4) * 64 + hd for t in range(8) for a in range(2)])
    A["w_kvc"] = tiles(w[:, 1024:1536])
    A["w_gate"] = tiles(w[:, 2560:2608], 48)
    A["w_q"] = tiles(w[:, order])
    A["w_ksw"] = tiles(np.concatenate([w[:, 1536:1792], w[:, 2048:2304]], 1))
    A["w_vsw"] = rows(np.concatenate([w[:, 1792:2048], w[:, 2304:2560]], 1), 512, 2)
    A["w_z0"] = tiles(w[:, 2608 + order])
    A["w_o0"] = tiles(x["l0_w_out"][order])
    p = [x["l0_cmp_k_pe"].T, x["l0_cmp_v_pe"].T]
    A["cmp_pe"] = f(np.stack([np.concatenate([q, q]) for q in p], 1))
    A["cmp_w1"] = f(np.stack([x[n].reshape(2, 8, 128, 2, 128).transpose(3, 0, 2, 1, 4).reshape(2, 2, 128, 1024)
                              for n in ("l0_cmp_k_w1", "l0_cmp_v_w1")]))
    A["cmp_w2"] = f(np.stack([x[n].reshape(2, 128, 64).transpose(1, 0, 2)
                              for n in ("l0_cmp_k_w2", "l0_cmp_v_w2")], 1))
    t = np.arange(512).reshape(4, 128).T
    n = np.arange(32)
    slopes = np.exp2(-8.0 * np.arange(1, 17, dtype=np.float32) / np.float32(16)).astype(np.float32).reshape(4, 4)
    seen = (16 * n + 31)[None, None, :] <= t[:, :, None]
    seen &= n < 31
    gap = (t[:, :, None] - (16 * n + 15.5)).astype(np.float32)
    b = -slopes.T[None, None, :, :, None] * gap[:, :, None, None, :]
    b = np.where(seen[:, :, None, None, :], b, np.float32(NEG))
    A["c_biasc"] = f(b.reshape(128, 4, 512))
    A["c_maskc"] = f(seen)
    d = 384 + np.arange(128)[:, None] - np.arange(512)[None, :]
    A["c_dist"] = f(np.where(d >= 0, d, np.float32(MASKED)))
    A["c_ident"] = f(np.eye(128))
    V = [vec(x[k]) for k in ("l0_norm", "l1_norm", "final_norm", "norm_mix_pre_2", "norm_mix_post_2",
                             "norm_ffn_pre_2", "norm_ffn_post_2", "ret_norm_w_2", "ret_norm_b_2", "gla_norm_w_2")]
    V.append(vec(x["l1_d"]))
    V.append(np.concatenate([vec(x["gla_b_alpha_2"]), np.zeros((128, 4), np.float32)], 1))
    A["vecs"] = f(np.stack(V, 1))
    more(x, A, f, tiles, rows)
    return A


def kernel(**inputs):
    import concourse.bacc as bacc
    from concourse.bass_utils import run_bass_kernel_spmd as run

    x = {k: np.asarray(v) for k, v in inputs.items()}
    A = layout(x)
    nc = bacc.Bacc("TRN2", target_bir_lowering=False, num_devices=1, dynamic_dma_scratch_size=RING)
    build(nc, A)
    r = run(nc, [{"in_" + k: a for k, a in A.items()}], core_ids=[0])
    return r.results[0]["out_0"].reshape(1024, S).T.reshape(1, S, 1024)
```

```python
from contextlib import ExitStack

import numpy as np

import concourse.bass as bass
from concourse import mybir

F32 = mybir.dt.float32
F32R = mybir.dt.float32r
U32 = mybir.dt.uint32
ALU = mybir.AluOpType
ACT = mybir.ActivationFunctionType
AX = mybir.AxisListType.X

S = 512
D = 1024
KT = 8
NEG = -1.0e30
MASKED = 3.0e33
RR = 3
RH = 3
LOOK = 2
RING = 1024


class Sem:

    def __init__(self, handle):
        self.handle = handle
        self.n = 0


class Queue:

    def __init__(self, sem):
        self.sem = Sem(sem)
        self.items = []
        self.seen = {}

    def wait(self, *toks):
        for t in toks:
            if t is None:
                continue
            if isinstance(t, list):
                self.wait(*t)
                continue
            s, n = t
            if self.seen.get(s, 0) < n:
                self.seen[s] = n
                self.items.append((0, s.handle, n))

    def do(self, fn, *toks):
        self.wait(*toks)
        self.sem.n += 1
        self.items.append((1, fn, self.sem.handle, 1))
        return (self.sem, self.sem.n)

    def quiet(self, fn, *toks):
        self.wait(*toks)
        self.items.append((2, fn))

    def dma(self, fn, sem, *toks):
        self.wait(*toks)
        sem.n += 16
        self.items.append((1, fn, sem.handle, 16))
        return (sem, sem.n)

    def now(self):
        return (self.sem, self.sem.n) if self.sem.n else None

    def play(self, eng):
        for it in self.items:
            if it[0] == 0:
                eng.wait_ge(it[1], it[2])
            elif it[0] == 1:
                it[1](eng).then_inc(it[2], it[3])
            else:
                it[1](eng)


class Slot:
    def __init__(self, ap):
        self.ap = ap
        self.free = None


class Pool:

    def __init__(self, aps):
        self.slots = [Slot(a) for a in aps]
        self.idle = list(self.slots)

    def take(self):
        return self.idle.pop(0)

    def give(self, slot, *toks):
        slot.free = list(toks)
        self.idle.append(slot)


class Weights:

    def __init__(self, ins, sp, act, dve, raw, hi, lo, sems, plan):
        self.ins = ins
        self.sp, self.act, self.dve = sp, act, dve
        self.raw, self.hi, self.lo = raw, hi, lo
        self.sems = sems
        self.plan = plan
        self.limit = next(i for i, p in enumerate(plan) if p[0][0] == "w_o0") if plan else 0
        self.asked = []
        self.rawfree = [None] * RR
        self.rawuser = [-1] * RR
        self.ringfree = [None] * RH
        self.ringuser = [-1] * RH
        self.loaded = {}
        self.ready = {}
        self.done = set()
        self.nsplit = 0
        self.splits = 0

    def pump(self, upto):
        if self.plan is None:
            return
        while True:
            moved = False
            i = len(self.loaded)
            if i < self.limit and i <= upto + RR:
                r = i % RR
                u = self.rawuser[r]
                if u < 0 or u in self.done:
                    _, (name, at, lo), n, _ = self.plan[i]
                    dst = self.raw[r][:, 0:n]
                    src = self.ins[name][at][:, lo:lo + n]
                    self.loaded[i] = self.sp.dma(
                        lambda e, dst=dst, src=src: e.dma_start(dst, src), self.sems[r], self.rawfree[r])
                    self.rawuser[r] = i
                    moved = True
            j = self.nsplit
            if j < self.limit and j <= upto and j in self.loaded:
                _, _, n, split = self.plan[j]
                if not split:
                    self.ready[j] = (self.raw[j % RR], None, [self.loaded[j]], None)
                    self.nsplit += 1
                    moved = True
                else:
                    q = self.splits % RH
                    u = self.ringuser[q]
                    if u < 0 or u in self.done:
                        raw = self.raw[j % RR][:, 0:n]
                        hi = self.hi[q][:, 0:n]
                        lo = self.lo[q][:, 0:n]
                        a = self.act.do(lambda e, o=hi, i_=raw: e.activation(o, i_, ACT.Copy),
                                        self.loaded[j], self.ringfree[q])
                        v = self.dve.do(lambda e, o=lo, i_=raw, h=hi: e.tensor_tensor(
                            o, i_, h.bitcast(F32), ALU.subtract), a, self.ringfree[q])
                        self.rawfree[j % RR] = [a, v]
                        self.done.add(("raw", j))
                        self.rawuser[j % RR] = -1
                        self.ringuser[q] = j
                        self.ready[j] = (self.hi[q], self.lo[q], [a, v], q)
                        self.splits += 1
                        self.nsplit += 1
                        moved = True
            if not moved:
                return

    def resume(self, *toks):
        if self.plan is None:
            return
        self.limit = len(self.plan)
        self.rawfree = [list(toks)] * RR
        self.ringfree = [list(toks)] * RH
        self.pump(len(self.loaded) + LOOK - 1)

    def get(self, key, src, n, split=True):
        i = len(self.asked)
        self.asked.append((key, src, n, split))
        if self.plan is None:
            return i, self.hi[0] if split else self.raw[0], self.lo[0], []
        assert self.plan[i][0] == key
        self.pump(i + LOOK)
        hi, lo, toks, _ = self.ready[i]
        return i, hi, lo, toks

    def release(self, i, tok):
        if self.plan is None:
            return
        if self.asked[i][3]:
            q = self.ready[i][3]
            self.ringfree[q] = tok
            self.ringuser[q] = -1
        else:
            self.rawfree[i % RR] = tok
            self.rawuser[i % RR] = -1


class Core:
    pass


def twin(c, ctx, name, shape):
    off = (c.nc.sbuf_base + 31) // 32 * 32
    t = ctx.enter_context(c.nc.sbuf_tensor(name, shape, F32))
    return t, c.nc.alloc_sbuf_tensor_at(name + "r", shape, F32R, offset=off)


def gemm_steps(c, w, col, K, hi, lo, toks, M=128):
    bank = c.banks.take()
    k0 = 0
    while k0 < K:
        nk = min(8, K - k0)
        i, wh, wl, wt = c.w.get((w, col, k0), (w, (col,), k0 * M), nk * M)
        for k in range(k0, k0 + nk):
            for p, (a, b) in enumerate(((wh, hi), (wh, lo), (wl, hi))):
                st = k == 0 and p == 0
                sp = k == K - 1 and p == 2
                lhs = a[:, (k - k0) * M:(k - k0 + 1) * M]
                fn = lambda e, o=bank.ap[0:M, :], l=lhs, r=b(k), st=st, sp=sp: e.matmul(o, l, r, start=st, stop=sp)
                if k == k0 + nk - 1 and p == 2:
                    tok = c.pe.do(fn, wt, toks[k], bank.free)
                else:
                    c.pe.quiet(fn, wt, toks[k], bank.free)
            if k % 4 == 3 and k < K - 1:
                yield None
        c.w.release(i, tok)
        k0 += nk
    yield bank, tok


def gemm(c, *args, **kw):
    for r in gemm_steps(c, *args, **kw):
        pass
    return r


def gemm_pair(c, cols, hi, lo, toks):
    banks = [c.banks.take() for _ in cols]
    ws = [c.w.get((w, col, 0), (w, (col,), 0), 1024) for w, col in cols]
    out = []
    for k in range(KT):
        for bank, (i, wh, wl, wt) in zip(banks, ws):
            for p, (a, b) in enumerate(((wh, hi), (wh, lo), (wl, hi))):
                st = k == 0 and p == 0
                sp = k == KT - 1 and p == 2
                fn = lambda e, o=bank.ap, l=a[:, k * 128:(k + 1) * 128], r=b(k), st=st, sp=sp: e.matmul(
                    o, l, r, start=st, stop=sp)
                if sp:
                    tok = c.pe.do(fn, wt, toks[k], bank.free)
                    c.w.release(i, tok)
                    out.append((bank, tok))
                else:
                    c.pe.quiet(fn, wt, toks[k], bank.free)
    return out


def pair_or_two(c, pair, a, b, toks):
    if pair:
        return gemm_pair(c, [a, b], c.hhi, c.hlo, toks)
    return [gemm(c, w, col, KT, c.hhi, c.hlo, toks) for w, col in (a, b)]


def gemm_tok(c, w, m, n, kper, hi, lo, toks):
    banks = [c.banks.take() for _ in range(4)]
    for j in range(KT // kper):
        i, wh, wl, wt = c.w.get((w, m, j), (w, (m, j), 0), kper * n)
        for t in range(4):
            for kk in range(kper):
                k = j * kper + kk
                for p, (a, b) in enumerate(((hi, wh), (lo, wh), (hi, wl))):
                    st = k == 0 and p == 0
                    sp = k == KT - 1 and p == 2
                    fn = lambda e, o=banks[t].ap[:, 0:n], l=a(k)[:, t * 128:(t + 1) * 128], \
                        r=b[:, kk * n:(kk + 1) * n], st=st, sp=sp: e.matmul(o, l, r, start=st, stop=sp)
                    if kk == kper - 1 and p == 2:
                        tok = c.pe.do(fn, wt, toks[k], banks[t].free)
                    else:
                        c.pe.quiet(fn, wt, toks[k], banks[t].free)
            if j == KT // kper - 1:
                banks[t].tok = tok
        c.w.release(i, tok)
    return banks


def split(c, src, hi, lo, *toks):
    a = c.act.do(lambda e, hi=hi, src=src: e.activation(hi, src, ACT.Copy), *toks)
    v = c.dve.do(lambda e, lo=lo, src=src, hi=hi: e.tensor_tensor(lo, src, hi.bitcast(F32), ALU.subtract), a, *toks)
    return [a, v]


class Squares:

    def __init__(self, c, acc):
        self.c = c
        self.acc = acc
        self.last = None
        self.free = None

    def start(self):
        self.last = None

    def add(self, t, *toks, g=1.0, eng=None):
        c = self.c
        acc = self.acc
        if self.last is None:
            self.last = c.act.do(lambda e, t=t, acc=acc, g=g: e.activation(acc[:, :], t, ACT.Square, scale=g), *toks, self.free)
        else:
            s = c.sq2.take()
            a = c.act.do(lambda e, t=t, s=s, g=g: e.activation(s.ap, t, ACT.Square, scale=g), *toks, s.free)
            eng = eng or c.dve
            self.last = eng.do(lambda e, acc=acc, s=s: e.tensor_tensor(acc[:, :], acc[:, :], s.ap, ALU.add), a, self.last)
            c.sq2.give(s, self.last)

    def total(self):
        c = self.c
        acc = self.acc
        b = c.banks.take()
        self.free = c.pe.do(lambda e, b=b, acc=acc, c=c: e.matmul(b.ap, c.ones[:, :], acc[:, :], start=True, stop=True),
                            self.last, b.free)
        return b, self.free

    def inv(self, eps, scale):
        c = self.c
        b, p = self.total()
        return rsqrt(c, c.rs[:, :], b, scale, eps, p, c.rsfree)


def split_scaled(c, x, g, hi, lo, *toks):
    a = c.act.do(lambda e, hi=hi, x=x, g=g: e.activation(hi, x, ACT.Copy, scale=g), *toks)
    v = c.dve.do(lambda e, lo=lo, x=x, g=g, hi=hi: e.scalar_tensor_tensor(lo, x, g, hi.bitcast(F32), ALU.mult, ALU.subtract), a, *toks)
    return [a, v]


def rsqrt(c, dst, b, scale, eps, *toks):
    a = c.act.do(lambda e, dst=dst, b=b, scale=scale, c=c, eps=eps: e.activation(dst, b.ap, ACT.Ln, bias=c.epst[:, eps:eps + 1], scale=scale), *toks)
    c.banks.give(b, a)
    return c.act.do(lambda e, dst=dst: e.activation(dst, dst, ACT.Exp, scale=-0.5), a)


def norm(c, X, xtoks, g, hi, lo, hfree, perm=False):
    r = c.ss.inv(0, 1.0 / D)
    out = []
    for k in range(KT):
        s = c.sq.take()
        x = X[:, k, :]
        rs = c.rs[:, :]
        o = s.ap
        if perm:
            x = x.rearrange("p (n s) -> p s n", s=8)
            rs = rs.rearrange("p (n s) -> p s n", s=8)
            o = o.rearrange("p (s n) -> p s n", s=8)
        v = c.dve.do(lambda e, x=x, o=o, k=k, rs=rs, g=g: e.scalar_tensor_tensor(
            o, x, g[:, k:k + 1], rs, ALU.mult, ALU.mult), r, s.free, c.gtok)
        a = c.act.do(lambda e, s=s, k=k, hi=hi: e.activation(hi(k), s.ap, ACT.Copy), v, hfree)
        v2 = c.dve.do(lambda e, s=s, k=k, lo=lo, hi=hi: e.tensor_tensor(lo(k), s.ap, hi(k).bitcast(F32), ALU.subtract), a, hfree)
        c.sq.give(s, v2)
        out.append([a, v2])
    c.rsfree = v2
    return out


def barrier(c):
    toks = [q.now() for q in c.queues] + c.dma_toks
    for q in (c.act, c.dve, c.gp, c.sp):
        q.wait(*toks)
    c.dma_toks = []


def load(c, dst, src, *toks):
    t = c.sp.dma(lambda e, dst=dst, src=src: e.dma_start(dst, src), c.dsem(), *toks)
    return t


def nsa(c, X, xtoks):
    pe, act, dve, gp, banks = c.pe, c.act, c.dve, c.gp, c.banks
    I = c.ins
    with ExitStack() as ctx:
        def sb(name, shape, dt=F32):
            return ctx.enter_context(c.nc.sbuf_tensor(name, shape, dt))

        qs = sb("qs", [128, 8, 2, S], F32R)
        kh = sb("kh", [128, 2, 2, 2, S], F32R)
        kl = sb("kl", [128, 2, 2, S], F32R)
        kch = sb("kch", [128, 2, 2, 32], F32R)
        kcl = sb("kcl", [128, 2, 32], F32R)
        vbase = (c.nc.sbuf_base + 31) // 32 * 32
        vsw = sb("vsw", [128, 4, 512])
        zbase = (c.nc.sbuf_base + 31) // 32 * 32
        zs, zsr = twin(c, ctx, "zs", [128, 8, S])
        gT = sb("gT", [48, S])
        gate = sb("gate", [128, 4, 48])
        vc = sb("vc", [128, 64])
        pcT = sb("pcT", [128, 4, S])
        dist = sb("dist", [128, S])
        st = sb("st", [128, 64])

        d_dist = load(c, dist[:, :], I["c_dist"])
        c.w.pump(LOOK)
        H = norm(c, X, xtoks, c.g_l0, c.hhi, c.hlo, None)
        proj = lambda w, col, **kw: gemm(c, w, col, KT, c.hhi, c.hlo, H, **kw)

        with ExitStack() as cx:
            def sc(name, shape, dt=F32):
                return cx.enter_context(c.nc.sbuf_tensor(name, shape, dt))
            lent = lambda name, shape, at: c.nc.alloc_sbuf_tensor_at(name, shape, F32, offset=at)
            blk = [lent(f"blk{i}", [128, 16, 128], zbase + 8192 * i) for i in range(2)]
            pe2 = lent("pe2", [128, 2, 32], vbase)
            w2 = lent("w2", [128, 2, 2, 64], vbase + 256)
            hid = lent("hid", [128, 2, 2, 128], vbase + 1280)
            biasc = sc("biasc", [128, 4, 512])
            maskc = sc("maskc", [128, 4, 32])
            sC = sc("sC", [128, 512])
            cs = sc("cs", [128, 3, 16])
            d_pe = load(c, pe2[:, :, :], I["cmp_pe"])
            d_w2 = load(c, w2[:, :, :, :], I["cmp_w2"])
            d_bc = load(c, biasc[:, :, :], I["c_biasc"])
            d_mc = load(c, maskc[:, :, :], I["c_maskc"])
            zt = [gp.do(lambda e, i=i, blk=blk: e.memset(blk[i][:, :, :], 0.0)) for i in range(2)]
            btoks = []
            for i in range(2):
                bt = []
                pair = gemm_pair(c, [("w_kvc", 2 * i), ("w_kvc", 2 * i + 1)], c.hhi, c.hlo, H)
                for gpair in range(2):
                    b, tok = pair[gpair]
                    src = b.ap.rearrange("p (n q two) -> p two q n", q=8, two=2)
                    for a in range(2):
                        for par in range(2):
                            for hf in range(2):
                                o = blk[i][par * 64:par * 64 + 64, hf * 8:hf * 8 + 8, :].rearrange(
                                    "p q (g n) -> p q g n", g=4)[:, :, 2 * gpair + a, 0:31]
                                i0 = src[a * 64:a * 64 + 64, par, :, hf:hf + 31]
                                i1 = pe2[a * 64:a * 64 + 64, i, :].rearrange("p (q two) -> p two q", two=2)[
                                    :, par, hf * 8:hf * 8 + 8].unsqueeze(2).broadcast_to([64, 8, 31])
                                v = dve.do(lambda e, o=o, i0=i0, i1=i1: e.tensor_tensor(o, i0, i1, ALU.add),
                                           tok, d_pe, zt[i])
                    banks.give(b, v)
                    bt.append(v)
                btoks.append(bt)
            b, tok = proj("w_gate", 0, M=48)
            tg = act.do(lambda e, b=b, gT=gT: e.activation(gT[:, :], b.ap[0:48, :], ACT.Sigmoid), tok)
            banks.give(b, tg)
            b = banks.take()
            for t in range(4):
                tok = pe.do(lambda e, t=t, b=b, gT=gT, c=c: e.transpose(b.ap[:, t * 48:t * 48 + 48], gT[:, t * 128:t * 128 + 128],
                                                            c.ident[0:48, 0:48]), tg, b.free)
            tgate = dve.do(lambda e, b=b, gate=gate: e.tensor_copy(gate[:, :, :].rearrange("p a b -> p (a b)"), b.ap[:, 0:192]), tok)
            banks.give(b, tgate)
            for i in range(2):
                b = banks.take()
                for m in range(2):
                    for hf in range(2):
                        j, w1, _, wt = c.w.get(("cmp_w1", i, m, hf), ("cmp_w1", (i, m, hf), 0), 1024, split=False)
                        for q in range(8):
                            fn = lambda e, b=b, m=m, q=q, hf=hf, i=i, w1=w1, blk=blk: e.matmul(
                                b.ap[:, m * 128:m * 128 + 128], w1[:, q * 128:q * 128 + 128],
                                blk[i][:, hf * 8 + q, :], start=(hf == 0 and q == 0), stop=(hf == 1 and q == 7))
                            tok = pe.do(fn, wt, btoks[i], b.free)
                        c.w.release(j, tok)
                th = act.do(lambda e, b=b, i=i, hid=hid: e.activation(hid[:, i, :, :].rearrange("p a b -> p (a b)"),
                                                             b.ap[:, 0:256], ACT.Silu), tok)
                banks.give(b, th)
                b = banks.take()
                if i == 0:
                    for g in range(4):
                        for m in range(2):
                            fn = lambda e, g=g, m=m, b=b, w2=w2, hid=hid: e.matmul(
                                b.ap[(g % 2) * 64:(g % 2) * 64 + 64, (g // 2) * 32:(g // 2) * 32 + 32],
                                w2[:, 0, m, :], hid[:, 0, m, g * 32:g * 32 + 32], start=(m == 0), stop=(m == 1))
                            tok = pe.do(fn, th, d_w2, b.free)
                    kc = b.ap[:, 0:64].rearrange("p (g n) -> p g n", g=2)
                    for a in range(2):
                        for o in (a, 1 - a):
                            tkc = act.do(lambda e, kch=kch, kc=kc, a=a, o=o: e.activation(kch[o * 64:o * 64 + 64, :, a, :],
                                                                kc[a * 64:a * 64 + 64, :, :], ACT.Copy), tok)
                    for a in range(2):
                        R_ = slice(a * 64, a * 64 + 64)
                        vkc = dve.do(lambda e, kcl=kcl, kc=kc, R_=R_, kch=kch, a=a: e.tensor_tensor(kcl[R_, :, :], kc[R_, :, :],
                                                               kch[R_, :, a, :].bitcast(F32), ALU.subtract), tkc)
                    banks.give(b, vkc)
                    tkc = [tkc, vkc]
                else:
                    for m in range(2):
                        fn = lambda e, m=m, b=b, hid=hid, w2=w2: e.matmul(b.ap[:, 0:64], hid[:, 1, m, :], w2[:, 1, m, :],
                                                          start=(m == 0), stop=(m == 1))
                        tok = pe.do(fn, th, d_w2, b.free)
                    tvc = act.do(lambda e, b=b, vc=vc: e.activation(vc[:, :], b.ap[:, 0:64], ACT.Copy), tok)
                    banks.give(b, tvc)
            tq = []
            for t in range(8):
                b, tok = proj("w_q", t)
                halves = [(a, slice(a * 64, a * 64 + 64), slice(64 - a * 64, 128 - a * 64)) for a in range(2)]
                for a, R_, Q_ in halves:
                    x = act.do(lambda e, qs=qs, R_=R_, t=t, a=a, b=b: e.activation(qs[R_, t, a, :], b.ap[R_, :], ACT.Copy, scale=0.125), tok)
                for a, R_, Q_ in halves:
                    v = dve.do(lambda e, qs=qs, Q_=Q_, t=t, a=a, b=b, R_=R_: e.scalar_tensor_tensor(qs[Q_, t, a, :], b.ap[R_, :], 0.125,
                                                                qs[R_, t, a, :].bitcast(F32), ALU.mult,
                                                                ALU.subtract), x)
                banks.give(b, v)
                tq.append([x, v])
            tk = []
            for i in range(2):
                for g2 in range(2):
                    b, tok = proj("w_ksw", 2 * i + g2)
                    for a, R_, Q_ in halves:
                        for o in (R_, Q_):
                            x = act.do(lambda e, kh=kh, o=o, i=i, g2=g2, a=a, b=b, R_=R_: e.activation(kh[o, i, g2, a, :], b.ap[R_, :], ACT.Copy), tok)
                    for a, R_, Q_ in halves:
                        v = dve.do(lambda e, kl=kl, R_=R_, i=i, g2=g2, b=b, kh=kh, a=a: e.tensor_tensor(kl[R_, i, g2, :], b.ap[R_, :],
                                                             kh[R_, i, g2, a, :].bitcast(F32), ALU.subtract), x)
                    banks.give(b, v)
                    tk.append([x, v])
            tv = []
            for t, b in enumerate(gemm_tok(c, "w_vsw", 0, 512, 2, c.hhi, c.hlo, H)):
                a = act.do(lambda e, b=b, t=t, vsw=vsw: e.activation(vsw[:, t, :], b.ap, ACT.Copy), b.tok, tvc)
                banks.give(b, a)
                tv.append(a)

            tz = []

            def z_tiles():
                for t in range(8):
                    for r in gemm_steps(c, "w_z0", t, KT, c.hhi, c.hlo, H):
                        yield
                    b, tok = r
                    a = act.do(lambda e, zs=zs, b=b, t=t: e.activation(zs[:, t, :], b.ap, ACT.Silu), tok, tvc)
                    banks.give(b, a)
                    tz.append(a)
                    yield
            c.side = z_tiles()
            tpc = []
            prev = None
            for j in range(4):
                for a in range(2):
                    b = banks.take()
                    for t in range(8):
                        r, g2 = t % 4, t // 4
                        col = (r * 2 + g2) * 32
                        R_ = slice(a * 64, a * 64 + 64)
                        pe.quiet(lambda e, qs=qs, kch=kch, b=b, t=t, a=a, g2=g2, col=col, j=j: e.matmul(b.ap[:, col:col + 32], qs[:, t, a, j * 128:j * 128 + 128],
                                                    kch[:, g2, a, :], start=True, stop=False), tq[t], tkc, b.free)
                        tok = pe.do(lambda e, qs=qs, kcl=kcl, b=b, R_=R_, t=t, a=a, g2=g2, col=col, j=j: e.matmul(b.ap[:, col:col + 32], qs[R_, t, a, j * 128:j * 128 + 128],
                                                       kcl[R_, g2, :], start=False, stop=True))
                    view = lambda ap, a=a: ap.rearrange("p (h a n) -> p h a n", a=2, n=32)[:, :, a, :]
                    v = dve.do(lambda e, b=b, j=j, view=view, sC=sC, biasc=biasc: e.tensor_tensor(
                        view(sC[:, :]), b.ap[:, 0:256].rearrange("p (h n) -> p h n", n=32), view(biasc[:, j, :]),
                        ALU.add), tok, d_bc, prev)
                    banks.give(b, v)
                c.tick(2)
                s3 = sC[:, :].rearrange("p (h n) -> p h n", n=32)
                bc = lambda ap: ap.unsqueeze(2).broadcast_to([128, 16, 32])
                v = dve.do(lambda e, s3=s3, cs=cs: e.tensor_reduce(cs[:, 0, :], s3, axis=AX, op=ALU.max), v)
                v = dve.do(lambda e, s3=s3, bc=bc, cs=cs: e.tensor_tensor(s3, s3, bc(cs[:, 0, :]), ALU.subtract), v)
                a = act.do(lambda e, sC=sC: e.activation(sC[:, :], sC[:, :], ACT.Exp), v)
                v = dve.do(lambda e, j=j, s3=s3, maskc=maskc: e.tensor_tensor(s3, s3, maskc[:, j, :].unsqueeze(1).broadcast_to(
                    [128, 16, 32]), ALU.mult), a, d_mc)
                v = dve.do(lambda e, s3=s3, cs=cs: e.tensor_reduce(cs[:, 1, :], s3, axis=AX, op=ALU.add), v)
                v = dve.do(lambda e, cs=cs: e.tensor_scalar(cs[:, 1, :], cs[:, 1, :], 1e-30, None, ALU.max), v)
                v = dve.do(lambda e, cs=cs: e.reciprocal(cs[:, 2, :], cs[:, 1, :]), v)
                v = dve.do(lambda e, j=j, cs=cs, gate=gate: e.tensor_tensor(
                    cs[:, 0, :].rearrange("p (r g) -> p r g", g=4), cs[:, 2, :].rearrange("p (r g) -> p r g", g=4),
                    gate[:, j, 0:16].rearrange("p (g r) -> p r g", g=4), ALU.mult), v, tgate)
                v = dve.do(lambda e, s3=s3, bc=bc, cs=cs: e.tensor_tensor(s3, s3, bc(cs[:, 0, :]), ALU.mult), v)
                c.tick(4)
                b = banks.take()
                for r in range(4):
                    tok = pe.do(lambda e, b=b, r=r, sC=sC, c=c: e.transpose(b.ap[:, r * 128:r * 128 + 128],
                                                                sC[:, r * 128:r * 128 + 128], c.ident[:, :]), v, b.free)
                prev = tok
                a = act.do(lambda e, b=b, j=j, pcT=pcT: e.activation(pcT[:, :, j * 128:j * 128 + 128],
                                                            b.ap.rearrange("p (r q) -> p r q", r=4), ACT.Copy), tok)
                banks.give(b, a)
                tpc.append(a)
            c.drain()
            cmpdone = [pe.now(), act.now(), dve.now(), gp.now()]
        if c.tap == "proj":
            return dict(vsw=vsw, gate=gate, vc=vc, pcT=pcT, zs=zs)

        with ExitStack() as cx:
            def sc(name, shape, dt=F32):
                return cx.enter_context(c.nc.sbuf_tensor(name, shape, dt))
            for q in (act, dve, gp):
                q.wait(cmpdone)
            c.sp.wait(cmpdone)
            c.side = s5_prep(c, cx)
            ring = lambda name, shape, off: c.nc.alloc_sbuf_tensor_at(name, shape, F32, offset=c.wbase + off)
            Pb = Pool([ring(f"Pb{i}", [128, 2, 512], 4096 * i)[:, :, :] for i in range(4)])
            pT = Pool([ring(f"pT{i}", [128, 4, 128], 16384 + 2048 * i)[:, :, :] for i in range(8)])
            bias = Pool([ring(f"bias{i}", [128, 512], 32768 + 2048 * i)[:, :] for i in range(2)])
            stp = Pool([sc(f"stp{i}", [128, 8])[:, :] for i in range(4)])
            units = [(t, a, j) for t in range(8) for a in range(2) for j in range(4)]
            live = {}
            ob = {}
            otok = []
            htoks = []

            def head_bias(t, a):
                h = (2 * (t // 4) + a) * 4 + t % 4
                bs = bias.take()
                slope = -float(np.exp2(np.float32(-8.0 * (h + 1) / 16)))
                bt = gp.do(lambda e, slope=slope, bs=bs, dist=dist: e.tensor_scalar(bs.ap, dist[:, :], slope, 1.0, ALU.mult, ALU.mult),
                           d_dist, bs.free)
                live["bias", t, a] = (bs, bt)

            head_bias(0, 0)

            def stage_a(u):
                t, a, j = units[u]
                g2, r = t // 4, t % 4
                h = (2 * g2 + a) * 4 + r
                W = 128 * (j + 1)
                bs, bt = live["bias", t, a]
                if j == 1 and u + 3 < len(units):
                    head_bias(*units[u + 3][0:2])
                P = Pb.take()
                s = stp.take()
                vs_ = []
                R_ = slice(a * 64, a * 64 + 64)
                for br in range(2):
                    b = banks.take()
                    pe.quiet(lambda e, qs=qs, kh=kh, b=b, t=t, a=a, br=br, g2=g2, W=W, j=j: e.matmul(b.ap[:, 0:W], qs[:, t, a, j * 128:j * 128 + 128],
                                                kh[:, br, g2, a, 0:W], start=True, stop=False),
                             tq[t], tk[2 * br + g2], b.free)
                    tok = pe.do(lambda e, qs=qs, kl=kl, b=b, R_=R_, t=t, a=a, br=br, g2=g2, W=W, j=j: e.matmul(b.ap[:, 0:W], qs[R_, t, a, j * 128:j * 128 + 128],
                                                   kl[R_, br, g2, 0:W], start=False, stop=True))
                    v = dve.do(lambda e, b=b, br=br, P=P, bs=bs, s=s, W=W: e.tensor_tensor_reduce(
                        out=P.ap[:, br, 0:W], in0=b.ap[:, 0:W], in1=bs.ap[:, 512 - W:512], scale=1.0, scalar=-3.0e38,
                        op0=ALU.add, op1=ALU.max, accum_out=s.ap[:, br:br + 1]), tok, bt, P.free, s.free)
                    banks.give(b, v)
                if j == 3:
                    bias.give(bs, v)
                v = dve.do(lambda e, s=s: e.tensor_scalar(s.ap[:, 2:4], s.ap[:, 0:2], -1.0, None, ALU.mult), v)
                for br in range(2):
                    x = act.do(lambda e, br=br, P=P, W=W, s=s: e.activation(P.ap[:, br, 0:W], P.ap[:, br, 0:W], ACT.Exp,
                                                            bias=s.ap[:, 2 + br:3 + br],
                                                            accum_out=s.ap[:, 4 + br:5 + br]), v)
                live[u] = (P, s, x)

            def stage_b(u):
                t, a, j = units[u]
                g2, r = t // 4, t % 4
                h = (2 * g2 + a) * 4 + r
                W = 128 * (j + 1)
                P, s, x = live[u]
                v = dve.do(lambda e, s=s: e.reciprocal(s.ap[:, 6:8], s.ap[:, 4:6]), x)
                gv = gate[:, j, 16 + h:48:16]
                v = dve.do(lambda e, gv=gv, s=s: e.tensor_tensor(s.ap[:, 6:8], s.ap[:, 6:8], gv, ALU.mult), v, tgate)
                g_ = [gp.do(lambda e, P=P, s=s, W=W: e.tensor_scalar(
                    P.ap[:, 0, 0:W], P.ap[:, 0, 0:W], s.ap[:, 6:7], 1.0, ALU.mult, ALU.mult), v, x)]
                g_.append(act.do(lambda e, P=P, W=W, s=s: e.activation(P.ap[:, 1, 0:W], P.ap[:, 1, 0:W], ACT.Copy,
                                                        scale=s.ap[:, 7:8]), v, x))
                stp.give(s, *g_)
                live[u] = (P, g_)

            def stage_c(u):
                t, a, j = units[u]
                g2, r = t // 4, t % 4
                g = 2 * g2 + a
                P, g_ = live[u]
                if (t, a, j) == (t, 0, 0):
                    ob[t] = banks.take()
                blocks = [(br, k) for br in range(2) for k in range(j + 1)]
                hold = {}
                for i in range(0, len(blocks), 4 if j < 2 else j + 1):
                    part = blocks[i:i + (4 if j < 2 else j + 1)]
                    b = banks.take()
                    for m, (br, k) in enumerate(part):
                        tok = pe.do(lambda e, b=b, br=br, k=k, P=P, c=c, m=m: e.transpose(
                            b.ap[:, m * 128:m * 128 + 128], P.ap[:, br, k * 128:k * 128 + 128], c.ident[:, :]),
                            g_[br], b.free)
                    p = pT.take()
                    n = len(part) * 128
                    dst = p.ap.rearrange("p k q -> p (k q)")[:, 0:n]
                    if i or (j < 2 and u % 2):
                        x = act.do(lambda e, b=b, dst=dst, n=n: e.activation(dst, b.ap[:, 0:n], ACT.Copy), tok, p.free)
                    else:
                        x = dve.do(lambda e, b=b, dst=dst, n=n: e.tensor_copy(dst, b.ap[:, 0:n]), tok, p.free)
                    banks.give(b, x)
                    for m, q in enumerate(part):
                        hold[q] = (p, m, x, m == len(part) - 1)
                Pb.give(P, tok)
                live[u] = hold

            def stage_d(u):
                t, a, j = units[u]
                g2, r = t // 4, t % 4
                g = 2 * g2 + a
                hold = live[u]
                o = ob[t]
                oap = o.ap[a * 64:a * 64 + 64, j * 128:j * 128 + 128]
                pe.do(lambda e, oap=oap, vc=vc, pcT=pcT, r=r, g=g, j=j: e.matmul(oap, vc[32 * g:32 * g + 31, :], pcT[32 * g:32 * g + 31, r, j * 128:j * 128 + 128],
                                         start=True, stop=False, skip_group_check=True), tvc, tpc[j], o.free)
                for (br, k), (p, m, x, last) in hold.items():
                    tok = pe.do(lambda e, oap=oap, vsw=vsw, k=k, p=p, m=m, br=br, j=j, g=g: e.matmul(
                        oap, vsw[:, k, br * 256 + g * 64:br * 256 + g * 64 + 64], p.ap[:, m, :], start=False,
                        stop=(br == 1 and k == j), skip_group_check=True), x, tv)
                    if last:
                        pT.give(p, tok)
                if (a, j) == (1, 3):
                    v = dve.do(lambda e, zs=zs, o=o, t=t: e.tensor_tensor(zs[:, t, :], zs[:, t, :], o.ap, ALU.mult), tok, tz[t])
                    banks.give(o, v)
                    htoks.append(v)

            n = len(units)
            for i in range(n + 5):
                if i < n:
                    stage_a(i)
                c.tick()
                if 1 <= i <= n:
                    stage_b(i - 1)
                c.tick()
                if 3 <= i <= n + 2:
                    stage_c(i - 3)
                if i >= 5:
                    stage_d(i - 5)
                c.tick()
            c.drain()
            free = [list(c.s5t.values()), pe.now(), gp.now(), act.now()]
            free[0] = [x for y in free[0] for x in (y if isinstance(y, list) else [y])]
            c.w.resume(pe.now(), act.now(), dve.now(), gp.now())
            ghi = lambda t: qs[:, t, 0, :]
            glo = lambda t: zsr[:, t, :]
            htoks = [split(c, zs[:, t, :], ghi(t), glo(t), htoks[t], free) for t in range(8)]
            out, H = [], []
            c.ss.start()
            pair = gemm_pair(c, [("w_o0", 0), ("w_o0", 1)], ghi, glo, htoks)
            for t in range(8):
                b, tok = pair[t] if t < 2 else gemm(c, "w_o0", t, KT, ghi, glo, htoks)
                x = X[:, t, :]
                v = dve.do(lambda e, x=x, b=b: e.tensor_tensor(x, x, b.ap, ALU.add), tok, xtoks[t])
                banks.give(b, v)
                out.append(v)
                H.append(split_scaled(c, x.rearrange("p (n s) -> p s n", s=8), c.g_l1[:, t:t + 1],
                                      c.hhi(t).rearrange("p (s n) -> p s n", s=8),
                                      c.hlo(t).rearrange("p (s n) -> p s n", s=8), v, free))
                c.ss.add(x, v)
    barrier(c)
    return out, H


HOLD = 7


def s5_prep(c, ctx):
    pe, act, dve, gp, banks = c.pe, c.act, c.dve, c.gp, c.banks
    I = c.ins
    M, A_, S_ = ALU.mult, ALU.add, ALU.subtract

    def sb(name, shape, dt=F32):
        return ctx.enter_context(c.nc.sbuf_tensor(name, shape, dt))

    par = sb("par", [128, 3, 32])
    sm = sb("sm", [128, 19, 32])
    pw = sb("pw", [128, 2, 9, 32])
    pr = sb("pr", [128, 2, 8, 32])
    e8 = sb("e8", [128, 2, 32])
    Bq = c.at("Bq", [128, 2, 8, 16], 30208)
    Cq = c.at("Cq", [128, 2, 8, 16], 31232)
    Bb = sb("Bb", [128, 2, 8, 16])
    Bd = sb("Bd", [128, 2, 8, 32])
    CA = c.at("CA", [128, 2, 8, 9, 16], 0)
    WT = c.at("WT", [128, 8, 8, 16], 9216)
    Ws = sb("Ws", [128, 4, 128])
    Kp = c.at("Kp", [64, 4, 16, 16], 13312)
    Rt = c.at("Rt", [128, 2, 8, 64], 17408)
    tA = c.at("tA", [128, 8, 144], 21504)
    tG = c.at("tG", [128, 8, 128], 26112)
    dp = load(c, par[:, :, :], I["s5_par"])

    def V(fn, *t):
        return dve.do(fn, *t, dve.now())

    def tt(o, a, b, op, *t):
        return V(lambda e, o=o, a=a, b=b, op=op: e.tensor_tensor(o, a, b, op), *t)

    def ts(o, a, s1, op, s2=None, op2=None, *t):
        if op2 is None:
            return V(lambda e, o=o, a=a, s1=s1, op=op: e.tensor_scalar(o, a, s1, None, op), *t)
        return V(lambda e, o=o, a=a, s1=s1, s2=s2, op=op, op2=op2: e.tensor_scalar(o, a, s1, s2, op, op2), *t)

    def cmul(ore, oim, xr, xi, yr, yi, t1, t2, *t):
        tt(t1, xr, yr, M, *t)
        tt(t2, xi, yi, M, *t)
        tt(ore, t1, t2, S_)
        tt(t1, xr, yi, M)
        tt(t2, xi, yr, M)
        return tt(oim, t1, t2, A_)

    s = lambda i: sm[:, i, :]
    lre, lim, ldt = par[:, 0, :], par[:, 1, :], par[:, 2, :]
    a = act.do(lambda e, ldt=ldt, s=s: e.activation(s(0), ldt, ACT.Exp), dp)
    ts(s(1), lre, -1e-4, ALU.min, None, None, dp, a)
    tt(s(2), s(1), s(0), M)
    v = tt(s(3), lim, s(0), M)
    a = act.do(lambda e, s=s: e.activation(s(4), s(2), ACT.Exp), v)
    c.mag8_tok = act.do(lambda e, s=s, c=c: e.activation(c.mag8[:, :], s(2), ACT.Exp, scale=8.0), v)
    yield
    big = float(np.float32(1.5 * 2 ** 23))
    ts(s(5), s(3), float(np.float32(1 / (2 * np.pi))), M, big, A_)
    ts(s(5), s(5), big, S_)
    c1 = 6.28125
    c2 = float(np.float32(np.round((2 * np.pi - c1) * 2 ** 20) / 2 ** 20))
    c3 = float(np.float32(2 * np.pi - c1 - c2))
    cur = s(3)
    for cc in (c1, c2, c3):
        ts(s(6), s(5), cc, M)
        tt(s(7), cur, s(6), S_)
        cur = s(7)
    lim_ = 3.1415925
    ts(s(7), s(7), lim_, ALU.min, -lim_, ALU.max)
    ts(s(8), s(7), -1.0, M)
    tt(s(8), s(7), s(8), ALU.max)
    v = ts(s(8), s(8), -1.0, M, float(np.float32(np.pi / 2)), A_)
    a1 = act.do(lambda e, s=s: e.activation(s(9), s(8), ACT.Sin), v)
    a2 = act.do(lambda e, s=s: e.activation(s(10), s(7), ACT.Sin), v)
    yield
    cos, sin = s(9), s(10)
    P = lambda i, k: pw[:, i, k, :]
    V(lambda e, P=P: e.memset(P(0, 0), 1.0))
    V(lambda e, P=P: e.memset(P(1, 0), 0.0))
    tt(P(0, 1), s(4), cos, M, a, a1)
    tt(P(1, 1), s(4), sin, M, a2)
    t1, t2 = s(11), s(12)
    cmul(P(0, 2), P(1, 2), P(0, 1), P(1, 1), P(0, 1), P(1, 1), t1, t2)
    yield
    for k in (3, 4):
        cmul(P(0, k), P(1, k), P(0, k - 2), P(1, k - 2), P(0, 2), P(1, 2), t1, t2)
    yield
    for k in (5, 6, 7, 8):
        cmul(P(0, k), P(1, k), P(0, k - 4), P(1, k - 4), P(0, 4), P(1, 4), t1, t2)
        yield
    for k in range(8):
        vpr = V(lambda e, pr=pr, pw=pw, k=k: e.tensor_copy(pr[:, :, k, :], pw[:, :, 7 - k, :]))
    yield
    E = (s(13), s(14))
    cmul(E[0], E[1], cos, sin, cos, sin, t1, t2)
    cmul(s(15), s(16), E[0], E[1], E[0], E[1], t1, t2)
    cmul(e8[:, 0, :], e8[:, 1, :], s(15), s(16), s(15), s(16), t1, t2)
    yield
    tt(s(11), s(1), s(1), M)
    tt(s(12), lim, lim, M)
    tt(s(11), s(11), s(12), A_)
    V(lambda e, s=s: e.reciprocal(s(11), s(11)))
    ts(s(12), P(0, 1), -1.0, A_)
    tt(s(13), s(12), s(1), M)
    tt(s(14), P(1, 1), lim, M)
    tt(s(13), s(13), s(14), A_)
    tt(s(17), s(13), s(11), M)
    tt(s(13), P(1, 1), s(1), M)
    tt(s(14), s(12), lim, M)
    tt(s(13), s(13), s(14), S_)
    tt(s(18), s(13), s(11), M)
    V(lambda e, Bd=Bd: e.memset(Bd[:, :, :, :], 0.0))
    zero = V(lambda e, Kp=Kp: e.memset(Kp[:, :, 0:8, :], 0.0))
    yield
    cafree = wsfree = kfree = rfree = bfree = None
    dB = load(c, Bq[:, :, :, :], I["s5_B"][0])
    dC = load(c, Cq[:, :, :, :], I["s5_C"][0])
    for b4 in range(4):
        p8 = slice(8 * b4, 8 * b4 + 8)
        bc = lambda ap, n: ap.unsqueeze(2).broadcast_to([128, 8, n])
        vbb = cmul(Bb[:, 0, :, :], Bb[:, 1, :, :], Bq[:, 0, :, :], Bq[:, 1, :, :], bc(sm[:, 17, p8], 16),
                   bc(sm[:, 18, p8], 16), tA[:, :, 0:16], tA[:, :, 16:32], dB, bfree)
        for i in range(2):
            for h in range(2):
                vb = V(lambda e, Bd=Bd, Bb=Bb, i=i, h=h: e.tensor_copy(Bd[h * 64:h * 64 + 64, i, :, h * 16:h * 16 + 16],
                                               Bb[h * 64:h * 64 + 64, i, :, :]))
        yield
        x3 = tA[:, :, :].rearrange("p q (k n) -> p q k n", k=9)
        g3 = tG[:, :, :].rearrange("p q (k n) -> p q k n", k=8)

        def cplx(eng, x, w, n, y, i, o, *t):
            wk = lambda i: w[:, i, 0:n, p8].rearrange("p k q -> p q k").unsqueeze(3).broadcast_to([128, 8, n, 16])
            yk = lambda i: y[:, i, :, :].unsqueeze(2).broadcast_to([128, 8, n, 16])
            op = A_ if i else S_
            for hf in (slice(0, 4), slice(4, 8)):
                y0, y1, w0, w1, oo = [ap[:, hf] for ap in (yk(0), yk(1), wk(i), wk(1 - i), o)]
                xx = x[:, 0:4]
                eng.do(lambda e, oo=oo, y0=y0, w0=w0, M=M: e.tensor_tensor(oo, y0, w0, M), *t, eng.now())
                yield
                eng.do(lambda e, xx=xx, y1=y1, w1=w1, M=M: e.tensor_tensor(xx, y1, w1, M), eng.now())
                yield
                eng.do(lambda e, oo=oo, xx=xx, op=op: e.tensor_tensor(oo, oo, xx, op), eng.now())
                yield
        h3 = tG[:, :, :].rearrange("p q n -> p (q n)")[:, 0:576].rearrange("p (q k n) -> p q k n", q=4, k=9)
        for _ in zip(cplx(dve, x3, pw, 9, Cq, 0, CA[:, 0, :, :, :], cafree, dC),
                     cplx(gp, h3, pw, 9, Cq, 1, CA[:, 1, :, :, :], cafree, dC, vbb)):
            yield
        vc_ = [dve.now(), gp.now()]
        if b4 < 3:
            dB = load(c, Bq[:, :, :, :], I["s5_B"][b4 + 1], vbb)
            dC = load(c, Cq[:, :, :, :], I["s5_C"][b4 + 1], vc_)
        yield
        vca = [vc_, gp.do(lambda e, M=M, CA=CA: e.tensor_scalar(CA[:, 1, :, :, :], CA[:, 1, :, :, :], -1.0, 1.0, M, M),
                          gp.now())]
        d = c.sp.dma(lambda e, b4=b4, c=c, CA=CA: e.dma_start(c.dCA[b4], CA[:, :, :, :, :].rearrange("p i q k n -> p (i q k n)")),
                     c.dsem(), vca)
        c.s5t["CA", b4] = d
        for _ in range(HOLD):
            yield
        ak = []
        for hf in range(2):
            bk = banks.take()
            for q in range(4):
                p = 4 * hf + q
                for i in range(2):
                    tok = pe.do(lambda e, Bd=Bd, bk=bk, i=i, p=p, CA=CA, hf=hf, q=q: e.matmul(
                        bk.ap[hf * 32:hf * 32 + 32, q * 128:q * 128 + 128], Bd[:, i, p, :],
                        CA[:, i, p, 0:8, :].rearrange("p k n -> p (k n)"), start=(i == 0), stop=(i == 1)),
                        vca, vb, bk.free)
            a = act.do(lambda e, Kp=Kp, bk=bk, hf=hf: e.activation(
                Kp[hf * 32:hf * 32 + 32, :, 8:16, :].rearrange("p q k n -> p q (k n)"),
                bk.ap[hf * 32:hf * 32 + 32, :].rearrange("p (q n) -> p q n", q=4), ACT.Copy), tok, zero, kfree)
            banks.give(bk, a)
            yield
        cafree = [d, tok]
        bfree = tok
        ks = Sem(c.tsems[b4])
        for hf in range(2):
            for h in range(2):
                dst = c.dK[b4][:, 8 * hf:8 * hf + 8, :].rearrange("c (q h) n -> c q h n", h=2)[:, :, h, :]
                src = Kp[hf * 32 + h * 16:hf * 32 + h * 16 + 16, :, :, :].rearrange("p q k n -> p q (k n)")
                kfree = c.sp.dma(lambda e, dst=dst, src=src: e.dma_start(dst, src), ks, a)
        c.s5t["K", b4] = kfree
        yield
        for i in range(2):
            yield from cplx(gp, g3, pr, 8, Bb, i, WT[:, :, :, :], pe.now(), vbb, vpr)
            vwt = gp.now()
            for _ in range(HOLD):
                yield
            for hf in range(2):
                bk = banks.take()
                for q in range(4):
                    p = 4 * hf + q
                    tok = pe.do(lambda e, bk=bk, c=c, WT=WT, q=q, p=p: e.transpose(
                        bk.ap[:, q * 128:q * 128 + 128], WT[:, p, :, :].rearrange("p k n -> p (k n)"),
                        c.ident[:, :]), vwt, bk.free)
                aw = act.do(lambda e, bk=bk, Ws=Ws: e.activation(Ws[:, :, :].rearrange("p q n -> p (q n)"), bk.ap, ACT.Copy),
                            tok, wsfree)
                banks.give(bk, aw)
                o = 1024 * i + 512 * hf
                wsfree = c.sp.dma(lambda e, b4=b4, c=c, o=o, Ws=Ws: e.dma_start(c.dW[b4][:, o:o + 512],
                                                        Ws[:, :, :].rearrange("p q n -> p (q n)")), c.dsem(), aw)
                c.s5t["W", b4] = c.s5t.get(("W", b4), []) + [wsfree]
                yield
        bfree = [bfree, vwt]
        R = lambda i, n0, n1: Rt[:, i, :, n0:n1]
        V(lambda e, Rt=Rt, e8=e8, p8=p8: e.tensor_copy(Rt[:, :, :, 0], e8[:, :, p8]), rfree)
        n = 1
        while n < 64:
            bl = lambda i: Rt[:, i, :, n - 1:n].broadcast_to([128, 8, n])
            vr = cmul(R(0, n, 2 * n), R(1, n, 2 * n), R(0, 0, n), R(1, 0, n), bl(0), bl(1),
                      tA[:, :, 0:n], tA[:, :, 64:64 + n])
            n *= 2
            yield
        rfree = c.sp.dma(lambda e, b4=b4, c=c, Rt=Rt: e.dma_start(c.dR[b4], Rt[:, :, :, :].rearrange("p i q n -> p (i q n)")),
                         c.dsem(), vr)
        c.s5t["R", b4] = rfree
        yield


def s5(c, X, xtoks, H):
    pe, act, dve, gp, banks = c.pe, c.act, c.dve, c.gp, c.banks
    M, A_, S_ = ALU.mult, ALU.add, ALU.subtract
    with ExitStack() as ctx:
        def sb(name, shape, dt=F32):
            return ctx.enter_context(c.nc.sbuf_tensor(name, shape, dt))

        mats = Pool([(sb(f"mCA{i}", [128, 2, 8, 9, 16]), sb(f"mT{i}", [128, 16, 128])) for i in range(2)])
        turns = Pool([(sb("mW", [128, 2, 8, 128]), sb("mR", [128, 2, 8, 64]))])
        D0 = sb("D0", [128, 8, 64])
        wre = sb("wre", [128, 8, 64])
        wim = sb("wim", [128, 8, 64])
        xt = sb("xt", [128, 8, 64])
        Xs = Pool([sb(f"Xs{i}", [128, 2, 8, 64]) for i in range(2)])
        Us = Pool([sb(f"U{i}", [128, 16, 64]) for i in range(2)])
        Yt = sb("Yt", [128, 16, 64])
        zy, zyr = twin(c, ctx, "zy", [128, 8, S])
        yt = c.sq
        Y, Yr = twin(c, ctx, "Y5", [128, 8, S])
        gg = c.gg
        gt = dve.do(lambda e, gg=gg, c=c: e.tensor_tensor(gg, c.g_fin, c.g_pre, ALU.mult), c.gtok)
        z0 = dve.do(lambda e, D0=D0: e.memset(D0[:, :, 0:1], 0.0))
        for x in Xs.slots:
            z1 = dve.do(lambda e, x=x: e.memset(x.ap[:, :, :, 0:1], 0.0))

        def V(fn, *t):
            return dve.do(fn, *t, dve.now())

        def tt(o, a, b, op, *t):
            return V(lambda e, o=o, a=a, b=b, op=op: e.tensor_tensor(o, a, b, op), *t)

        fl = lambda t, n: t[tuple(slice(None) for _ in t.shape)].rearrange(n)

        def fetch_turn(b4):
            m = turns.take()
            W, R = m.ap
            sm = Sem(c.tsems[4 + b4])
            c.sp.dma(lambda e, fl=fl, W=W, b4=b4, c=c: e.dma_start(fl(W, "p i q n -> p (i q n)"), c.dW[b4]), sm, c.s5t["W", b4], m.free)
            d = c.sp.dma(lambda e, fl=fl, R=R, b4=b4, c=c: e.dma_start(fl(R, "p i q n -> p (i q n)"), c.dR[b4]), sm, c.s5t["R", b4])
            return m, d

        def fetch(b4):
            m = mats.take()
            CA, T = m.ap
            sm = Sem(c.tsems[16 + b4])
            c.sp.dma(lambda e, fl=fl, CA=CA, b4=b4, c=c: e.dma_start(fl(CA, "p i q k n -> p (i q k n)"), c.dCA[b4]), sm, c.s5t["CA", b4], m.free)
            for st in range(8):
                dst = T[st * 16:st * 16 + 16, :, :]
                src = c.dK[b4][:, :, (8 - st) * 16:(16 - st) * 16]
                d = c.sp.dma(lambda e, dst=dst, src=src: e.dma_start(dst, src), sm, c.s5t["K", b4])
            return m, d

        uts = {}

        def u_tile(k):
            b, tok = first[k] if k < 2 else gemm(c, "w_s5", k, KT, c.hhi, c.hlo, H)
            a_ = normed(Y[:, k, :], b, tok)
            uts[k] = (Y[:, k, :], a_)

        def z_tile(k):
            b, tok = gemm(c, "w_s5", 8 + k, KT, c.hhi, c.hlo, H)
            v = normed(zy[:, k, :], b, tok)
            a_ = act.do(lambda e, zy=zy, k=k: e.activation(zy[:, k, :], zy[:, k, :], ACT.Silu), v)
            tz.append(a_)

        tz, ytoks = [], []
        mfetch, live = {}, {}
        mturn = {0: fetch_turn(0)}
        mfetch[0] = fetch(0)
        mfetch[1] = fetch(1)
        first = gemm_pair(c, [("w_s5", 0), ("w_s5", 1)], c.hhi, c.hlo, H)
        rt = c.ss.inv(0, 1.0 / D)
        rsp = c.rs[:, :].rearrange("p (n s) -> p s n", s=8)

        def normed(dst, b, tok):
            v = dve.do(lambda e, rsp=rsp, M=M, dst=dst, b=b: e.tensor_tensor(dst.rearrange("p (s n) -> p s n", s=8),
                                                 b.ap.rearrange("p (s n) -> p s n", s=8), rsp, M), tok, rt)
            banks.give(b, v)
            c.rsfree = v
            return v

        def rows(b4):
            uds = Sem(c.tsems[8 + b4])
            for kk in range(2):
                u, ut = uts[2 * b4 + kk]
                dw = c.sp.dma(lambda e, u=u, c=c, b4=b4, kk=kk: e.dma_start(c.du[b4, kk], u), uds, ut)
            U = Us.take()
            for st in range(8):
                dst = U.ap[st * 16:st * 16 + 16, :, :]
                src = c.du[b4].rearrange("k (g c) (s n) -> s c (k g) n", c=16, s=8)[st]
                du = c.sp.dma(lambda e, dst=dst, src=src: e.dma_start(dst, src), uds, dw, U.free)
            live[b4] = (U, du)

        def states(b4):
            U, du = live[b4]
            m, dm = mturn[b4]
            W, R = m.ap
            vb_ = [banks.take(), banks.take()]
            for i in range(2):
                for g in range(16):
                    p, h = g // 2, g % 2
                    tok = pe.do(lambda e, W=W, i=i, p=p, U=U, g=g, vb_=vb_, h=h: e.matmul(
                        vb_[i].ap[h * 64:h * 64 + 64, p * 64:p * 64 + 64], W[:, i, p, h * 64:h * 64 + 64],
                        U.ap[:, g, :], start=True, stop=True), dm, du, vb_[i].free)
            p8 = slice(8 * b4, 8 * b4 + 8)
            X_ = Xs.take()
            V(lambda e, D0=D0, c=c, p8=p8: e.tensor_copy(D0[:, :, 1:64], c.mag8[:, p8].unsqueeze(2).broadcast_to([128, 8, 63])),
              c.mag8_tok, z0)
            vr = vb_[0].ap.rearrange("p (q n) -> p q n", q=8)
            vi = vb_[1].ap.rearrange("p (q n) -> p q n", q=8)
            tt(wre[:, :, :], vr, R[:, 0, :, :], M, tok, dm)
            tt(xt[:, :, :], vi, R[:, 1, :, :], M)
            tt(wre[:, :, :], wre[:, :, :], xt[:, :, :], A_)
            tt(wim[:, :, :], vi, R[:, 0, :, :], M)
            v = tt(xt[:, :, :], vr, R[:, 1, :, :], M)
            banks.give(vb_[0], v)
            banks.give(vb_[1], v)
            tt(wim[:, :, :], wim[:, :, :], xt[:, :, :], S_)
            for w_ in (wre, wim):
                fl = w_[:, :, :].rearrange("p q n -> p (q n)")
                V(lambda e, fl=fl, M=M, A_=A_, D0=D0: e.tensor_tensor_scan(fl, D0[:, :, :].rearrange("p q n -> p (q n)"), fl, 0.0, M, A_))
            lo_ = lambda ap: ap[:, :, 0:63]
            x63 = xt[:, :, 0:63]
            xs = X_.ap
            tt(xs[:, 0, :, 1:64], lo_(wre), lo_(R[:, 0, :, :]), M, X_.free, z1)
            tt(x63, lo_(wim), lo_(R[:, 1, :, :]), M)
            tt(xs[:, 0, :, 1:64], xs[:, 0, :, 1:64], x63, S_)
            tt(xs[:, 1, :, 1:64], lo_(wre), lo_(R[:, 1, :, :]), M)
            tt(x63, lo_(wim), lo_(R[:, 0, :, :]), M)
            vx = tt(xs[:, 1, :, 1:64], xs[:, 1, :, 1:64], x63, A_)
            turns.give(m, tok, vx)
            if b4 < 3:
                mturn[b4 + 1] = fetch_turn(b4 + 1)
            live[b4] = (U, du, X_, vx)

        yfree = [None]

        def outputs(b4):
            U, du, X_, vx = live[b4]
            m, dm = mfetch[b4]
            CA, T = m.ap
            for h in range(2):
                yb = banks.take()
                for q in range(8):
                    g = 2 * q + h
                    o = yb.ap[:, q * 64:q * 64 + 64]
                    pe.do(lambda e, o=o, T=T, g=g, U=U: e.matmul(o, T[:, g, :], U.ap[:, g, :], start=True, stop=False), dm, du, yb.free)
                    for i in range(2):
                        tok = pe.do(lambda e, o=o, X_=X_, i=i, q=q, CA=CA, h=h: e.matmul(
                            o, CA[h * 64:h * 64 + 64, i, q, 1:9, :].rearrange("p k n -> p (k n)"),
                            X_.ap[h * 64:h * 64 + 64, i, q, :], start=False, stop=(i == 1)), vx)
                ay = act.do(lambda e, h=h, yb=yb, Yt=Yt: e.activation(
                    Yt[:, :, :].rearrange("p (q h) n -> p q h n", h=2)[:, :, h, :],
                    yb.ap.rearrange("p (q n) -> p q n", q=8), ACT.Copy), tok, yfree[0])
                banks.give(yb, ay)
            mats.give(m, tok, vx)
            Us.give(U, tok)
            Xs.give(X_, tok)
            if b4 + 2 < 4:
                mfetch[b4 + 2] = fetch(b4 + 2)
            yds = Sem(c.tsems[12 + b4])
            for st in range(8):
                dst = c.dy[b4].rearrange("k (g c) (s n) -> s c (k g) n", c=16, s=8)[st]
                src = Yt[st * 16:st * 16 + 16, :, :]
                dyw = c.sp.dma(lambda e, dst=dst, src=src: e.dma_start(dst, src), yds, ay)
            ys = [yt.take(), yt.take()]
            for kk in range(2):
                y = ys[kk]
                dy = c.sp.dma(lambda e, y=y, c=c, b4=b4, kk=kk: e.dma_start(y.ap, c.dy[b4, kk]), yds, dyw, y.free)
            yfree[0] = dyw
            live[b4] = (ys, dy)

        def finish(b4):
            ys, dy = live[b4]
            for kk in range(2):
                k = 2 * b4 + kk
                y = ys[kk]
                u, ut = uts[k]
                v = dve.do(lambda e, u=u, M=M, A_=A_, y=y, c=c, k=k: e.scalar_tensor_tensor(u, u, c.g_d[:, k:k + 1], y.ap, M, A_), dy, ut)
                yt.give(y, v)
                ytoks.append(act.do(lambda e, u=u: e.activation(u, u, ACT.Gelu_apprx_tanh), v))

        order = "u0 u1 r0 u2 u3 r1 s0 u4 u5 o0 r2 s1 u6 f0 u7 o1 r3 s2 z0 f1 z1 z2 o2 s3 z3 f2 z4 z5 o3 z6 z7 f3"
        fns = dict(u=u_tile, r=rows, s=states, o=outputs, z=z_tile, f=finish)
        Us.slots[0].free = Us.slots[1].free = None
        for step in order.split():
            fns[step[0]](int(step[1]))
        hd = pe.now()
        ytoks = [split(c, Y[:, k, :], c.hhi(k), c.hlo(k), ytoks[k], hd) for k in range(8)]
        gv = []
        for k in range(8):
            (ba, ta), (bb, tb) = pair_or_two(c, k == 0, ("w_glu", k), ("w_glu", 8 + k), ytoks)
            y = yt.take()
            a = act.do(lambda e, y=y, bb=bb: e.activation(y.ap, bb.ap, ACT.Sigmoid), tb, y.free)
            banks.give(bb, a)
            v = dve.do(lambda e, M=M, zy=zy, y=y, k=k: e.tensor_tensor(zy[:, k, :], zy[:, k, :], y.ap, M), a, tz[k])
            yt.give(y, v)
            v = dve.do(lambda e, M=M, zy=zy, ba=ba, k=k: e.tensor_tensor(zy[:, k, :], zy[:, k, :], ba.ap, M), ta, v)
            banks.give(ba, v)
            gv.append(v)
        hd = pe.now()
        ghi = lambda k: Yr[:, k, :]
        glo = lambda k: zyr[:, k, :]
        g2 = [split(c, zy[:, k, :], ghi(k), glo(k), gv[k], ytoks) for k in range(8)]
        out, H = [], []
        c.ss.start()
        c.sf.start()
        pair = gemm_pair(c, [("w_o1", 0), ("w_o1", 1)], ghi, glo, g2)
        for k in range(8):
            b, tok = pair[k] if k < 2 else gemm(c, "w_o1", k, KT, ghi, glo, g2)
            x = X[:, k, :].rearrange("p (n s) -> p s n", s=8)
            v = dve.do(lambda e, x=x, A_=A_, b=b: e.tensor_tensor(x, x, b.ap.rearrange("p (s n) -> p s n", s=8), A_),
                       tok, xtoks[k])
            banks.give(b, v)
            out.append(v)
            H.append(split_scaled(c, X[:, k, :], gg[:, k:k + 1], c.hhi(k), c.hlo(k), v, hd, gt))
            c.ss.add(X[:, k, :], v)
            c.sf.add(X[:, k, :], v, g=c.g_fin[:, k:k + 1])
    barrier(c)
    return out, H


def add_normed(c, X, xtoks, Y, ytoks, g, after):
    r = c.ss.inv(0, 1.0 / D)
    c.ss.start()
    out = []
    for k in range(KT + 1):
        if k < KT:
            v = c.dve.do(lambda e, Y=Y, g=g, k=k, c=c: e.scalar_tensor_tensor(
                Y[:, k, :], Y[:, k, :], g[:, k:k + 1], c.rs[:, :], ALU.mult, ALU.mult), r, ytoks[k])
            out.append(v)
        if k:
            j = k - 1
            out[j] = c.dve.do(lambda e, X=X, Y=Y, j=j: e.tensor_tensor(X[:, j, :], X[:, j, :], Y[:, j, :], ALU.add), out[j], xtoks[j])
            after(j, out[j])
    c.rsfree = out[-1]
    return out


def branch(c, n, bhi, blo, btoks, H, mg, mtoks, out):
    for k in range(8):
        for r in gemm_steps(c, "w_bgate", 8 * n + k, KT, c.hhi, c.hlo, H):
            if r is None:
                yield
        bg, tg = r
        s = c.sq.take()
        v = c.dve.do(lambda e, s=s, bg=bg, c=c: e.tensor_tensor(s.ap, bg.ap, c.rst[:, :], ALU.mult), tg, s.free)
        c.banks.give(bg, v)
        a = c.act.do(lambda e, s=s: e.activation(s.ap, s.ap, ACT.Sigmoid), v)
        yield
        for r in gemm_steps(c, "w_branch", 8 * n + k, KT, bhi, blo, btoks):
            if r is None:
                yield
        bp, tp = r
        if n == 0:
            v = c.dve.do(lambda e, mg=mg, s=s, bp=bp, k=k: e.tensor_tensor(mg[:, k, :], s.ap, bp.ap, ALU.mult), a, tp)
        else:
            v = c.dve.do(lambda e, s=s, bp=bp: e.tensor_tensor(s.ap, s.ap, bp.ap, ALU.mult), a, tp)
        c.banks.give(bp, v)
        if n:
            v = c.dve.do(lambda e, mg=mg, s=s, k=k: e.tensor_tensor(mg[:, k, :], mg[:, k, :], s.ap, ALU.add), v, mtoks[k])
        c.sq.give(s, v)
        out.append(v)
        yield
    c.bfree = c.pe.now()


def gate_tiles(c, name, dst, toks, free, H):
    for k in range(8):
        for r in gemm_steps(c, name, k, KT, c.hhi, c.hlo, H):
            if r is None:
                yield
        b, tok = r
        v = c.dve.do(lambda e, dst=dst, b=b, k=k, c=c: e.tensor_tensor(dst[:, k, :], b.ap, c.rst[:, :], ALU.mult), tok, free)
        c.banks.give(b, v)
        toks[k] = c.act.do(lambda e, dst=dst, k=k: e.activation(dst[:, k, :], dst[:, k, :], ACT.Silu), v)
        yield


def both(*steps):
    for s in steps:
        yield from s


def second(c, X, xtoks, H):
    pe, act, dve, gp, banks = c.pe, c.act, c.dve, c.gp, c.banks
    I = c.ins
    pair = gemm_pair(c, [("w_r", 0), ("w_r", 1)], c.hhi, c.hlo, H)
    r1 = c.ss.inv(0, 1.0 / D)
    rst, rs = c.rst[:, :], c.rs[:, :]
    b, p = c.sf.total()
    v = dve.do(lambda e, rst=rst, rs=rs: e.tensor_tensor(rst, rs, rs, ALU.mult), r1)
    s = c.sq.take()
    v = dve.do(lambda e, rst=rst, s=s, b=b: e.tensor_tensor(s.ap, rst, b.ap, ALU.mult), v, p, s.free)
    banks.give(b, v)
    a = act.do(lambda e, s=s, c=c: e.activation(s.ap, s.ap, ACT.Ln, bias=c.epst[:, 0:1], scale=1.0 / D), v)
    a = act.do(lambda e, s=s: e.activation(s.ap, s.ap, ACT.Exp, scale=-0.5), a)
    rtok = dve.do(lambda e, rst=rst, rs=rs, s=s: e.tensor_tensor(rst, s.ap, rs, ALU.mult), a)
    c.sq.give(s, rtok)
    b = banks.take()
    for t in range(4):
        p = pe.do(lambda e, b=b, c=c, t=t: e.matmul(b.ap[:, t:t + 1], c.rst[:, t * 128:t * 128 + 128], c.ident[:, 0:1], start=True,
                                     stop=True), rtok, b.free)
    rT = dve.do(lambda e, c=c, b=b: e.tensor_copy(c.rsT, b.ap[:, 0:4]), p)
    banks.give(b, rT)
    xt = [dve.do(lambda e, rs=rs, X=X, k=k, c=c: e.scalar_tensor_tensor(X[:, k, :], X[:, k, :], c.g_fin[:, k:k + 1], rs, ALU.mult,
                                                  ALU.mult), r1, H[k], c.ss.last, c.sf.last) for k in range(KT)]
    c.rsfree = xt[-1]

    def ev(name, col, dst, scale=1.0, M=128, free=None, made=None):
        b, tok = made or gemm(c, name, col, KT, c.hhi, c.hlo, H, M=M)
        v = dve.do(lambda e, dst=dst, scale=scale, b=b, c=c, M=M: e.scalar_tensor_tensor(dst, b.ap[0:M, :], scale, c.rst[0:M, :], ALU.mult, ALU.mult),
                   tok, free, rtok)
        banks.give(b, v)
        return v

    QS = float(128 ** -0.5)

    with ExitStack() as ctx:
        def sb(name, shape, dt=F32):
            return ctx.enter_context(c.nc.sbuf_tensor(name, shape, dt))
        Bh = sb("Bh", [128, 8, S], F32R)
        Bl = sb("Bl", [128, 8, S], F32R)
        bhi = lambda k: Bh[:, k, :]
        blo = lambda k: Bl[:, k, :]
        mg = sb("mg", [128, 8, S])
        of = sb("of", [128, 8, S])

        def rows_v(name, dst):
            toks = []
            for m in range(2):
                for t, b in enumerate(gemm_tok(c, name, m, 512, 2, c.hhi, c.hlo, H)):
                    a = act.do(lambda e, dst=dst, b=b, t=t, c=c, m=m: e.activation(dst[:, t, m * 512:m * 512 + 512], b.ap, ACT.Copy,
                                                      scale=c.rsT[:, t:t + 1]), b.tok, rT)
                    banks.give(b, a)
                    toks.append(a)
            return toks

        def square_pair(tiles, tok):
            s0, s1 = c.sq2.take(), c.sq2.take()
            a0 = act.do(lambda e, s0=s0, tiles=tiles: e.activation(s0.ap, tiles[0], ACT.Square), tok, s0.free)
            a1 = act.do(lambda e, s1=s1, tiles=tiles: e.activation(s1.ap, tiles[1], ACT.Square), tok, s1.free)
            v = dve.do(lambda e, s0=s0, s1=s1: e.tensor_tensor(s0.ap, s0.ap, s1.ap, ALU.add), a0, a1)
            c.sq2.give(s1, v)
            return s0, v

        def head_inv(s0, v, rs, eps):
            b = banks.take()
            p = pe.do(lambda e, b=b, s0=s0, c=c: e.matmul(b.ap, c.ones[:, :], s0.ap, start=True, stop=True), v, b.free)
            c.sq2.give(s0, p)
            return rsqrt(c, rs, b, 1.0 / 256, eps, p)

        with ExitStack() as cx:
            def sc(name, shape, dt=F32):
                return cx.enter_context(c.nc.sbuf_tensor(name, shape, dt))
            q = sc("rq", [128, 4, S])
            kk = sc("rk", [128, 4, S])
            v_ = sc("rv", [128, 4, 1024])
            dec = sc("dec", [128, 4, S])
            sT = Pool([sc(f"sT{i}", [128, S])[:, :] for i in range(3)])
            ot = Pool([sc(f"ro{i}", [128, 2, S])[:, :, :] for i in range(2)])
            hr = sc("hr", [128, S])
            dd = load(c, dec[:, :, :], I["c_decay"])
            tq = [ev("w_r", h, q[:, h, :], scale=QS, made=pair[h] if h < 2 else None) for h in range(4)]
            tk = [ev("w_r", 4 + h, kk[:, h, :]) for h in range(4)]
            tv = rows_v("w_rv", v_)
            btoks = []
            gt = {}
            c.side = gate_tiles(c, "w_rg", of, gt, None, H)
            units = [(h, kt) for h in range(4) for kt in range(4)]
            live, ob = {}, {}

            def scores(u):
                h, kt = units[u]
                W = S - 128 * kt
                b = banks.take()
                tok = pe.do(lambda e, kk=kk, q=q, b=b, h=h, W=W, kt=kt: e.matmul(b.ap[:, 0:W], kk[:, h, kt * 128:kt * 128 + 128],
                                               q[:, h, kt * 128:S], start=True, stop=True), tq[h], tk[h], b.free)
                s = sT.take()
                v = dve.do(lambda e, dec=dec, s=s, b=b, h=h, W=W: e.tensor_tensor(s.ap[:, 0:W], b.ap[:, 0:W], dec[:, h, 0:W], ALU.mult),
                           tok, dd, s.free)
                banks.give(b, v)
                live[u] = (s, v)

            def products(u):
                h, kt = units[u]
                W = S - 128 * kt
                s, v = live[u]
                if kt == 0:
                    ob[h] = [banks.take(), banks.take()]
                for e2 in range(2):
                    col = h * 256 + e2 * 128
                    o_ = ob[h][e2]
                    tok = pe.do(lambda e, v_=v_, o_=o_, kt=kt, s=s, col=col, W=W: e.matmul(o_.ap[:, kt * 128:S], v_[:, kt, col:col + 128],
                                                   s.ap[:, 0:W], start=(kt == 0), stop=(kt == 3)),
                                v, tv, o_.free)
                sT.give(s, tok)
                return tok

            hrs = [None]

            def ending(h, tok):
                o = ot.take()
                for e2 in range(2):
                    a = act.do(lambda e, o=o, e2=e2, ob=ob, h=h: e.activation(o.ap[:, e2, :], ob[h][e2].ap, ACT.Copy), tok, o.free)
                    banks.give(ob[h][e2], a)
                yield
                b = banks.take()
                for e2 in range(2):
                    tok = pe.do(lambda e, b=b, c=c, o=o, e2=e2: e.matmul(b.ap, c.ones[:, :], o.ap[:, e2, :], start=(e2 == 0),
                                                   stop=(e2 == 1)), a, b.free)
                for e2 in range(2):
                    v = dve.do(lambda e, b=b, o=o, e2=e2: e.scalar_tensor_tensor(o.ap[:, e2, :], b.ap, -1.0 / 256, o.ap[:, e2, :],
                                                                ALU.mult, ALU.add), tok)
                banks.give(b, v)
                s0, s1 = square_pair([o.ap[:, 0, :], o.ap[:, 1, :]], [v, hrs[0]])
                yield
                r = head_inv(s0, s1, hr[:, :], 1)
                for e2 in range(2):
                    k = 2 * h + e2
                    while k not in gt:
                        c.tick()
                    x = o.ap[:, e2, :]
                    v = dve.do(lambda e, x=x, hr=hr, c=c, k=k: e.scalar_tensor_tensor(x, x, c.g_retw[:, k:k + 1], hr[:, :],
                                                                ALU.mult, ALU.mult), r)
                    hrs[0] = v
                    v = dve.do(lambda e, x=x, of=of, c=c, k=k: e.scalar_tensor_tensor(x, x, c.g_retb[:, k:k + 1], of[:, k, :],
                                                                ALU.add, ALU.mult), v, gt[k])
                    btoks.append(split(c, x, bhi(k), blo(k), v))
                ot.give(o, *btoks[-1])

            post = iter(())
            for i in range(18):
                if i < 16:
                    scores(i)
                c.tick()
                next(post, None)
                if i >= 2:
                    tok = products(i - 2)
                    if units[i - 2][1] == 3:
                        post = ending(units[i - 2][0], tok)
                        next(post)
            c.tick()
            next(post)
            c.tick()
            next(post, None)
            c.drain()
            done = [x.now() for x in (pe, act, dve, gp)]
        mt = []
        gt = {}
        c.side = both(gate_tiles(c, "w_gg", of, gt, done, H), branch(c, 0, bhi, blo, btoks, H, mg, None, mt))

        with ExitStack() as cx:
            def sc(name, shape, dt=F32):
                return cx.enter_context(c.nc.sbuf_tensor(name, shape, dt))
            for x in (act, dve, gp):
                x.wait(done)
            qs = Pool([sc(f"gq{i}", [128, S])[:, :] for i in range(2)])
            ks = Pool([sc(f"gk{i}", [128, S])[:, :] for i in range(2)])
            v_ = sc("gv", [128, 4, 1024])
            ga = sc("ga", [16, S])
            al = sc("al", [16, 512])
            kd = sc("kd", [128, 4, 128])
            St = sc("St", [128, 7, 256])
            At = sc("At", [128, 4, 64])
            mk = sc("mk", [128, 4, 64])
            rm = sc("rm", [128, S])
            ta, tb, tc = [sc(f"gt{i}", [128, S]) for i in range(3)]
            cd = sc("cd", [128, 8])
            o = sc("go", [128, 2, S])
            hr = sc("ghr", [128, S])
            tga = ev("w_ga", 0, ga[:, :], M=16)
            def heads(h):
                q, k = qs.take(), ks.take()
                a = ev("w_g", h, q.ap, scale=QS, free=q.free)
                b = ev("w_g", 4 + h, k.ap, free=k.free)
                return q, a, k, b
            nxt = heads(0)
            d1 = load(c, al[:, :], I["alpha2"], done)
            d2 = load(c, mk[:, :, :], I["c_tri"], done)
            d3 = load(c, rm[:, :], I["c_reset"], done)
            tv = rows_v("w_gv", v_)
            z = dve.do(lambda e, At=At: e.memset(At[:, :, :], 0.0))
            btoks = []
            pfree = gfree = None
            for h in range(4):
                qslot, tq, kslot, tk = nxt
                q, kk = qslot.ap, kslot.ap
                b = banks.take()
                tok = pe.do(lambda e, b=b, al=al, ga=ga, h=h: e.matmul(b.ap, al[:, h * 128:h * 128 + 128], ga[:, :], start=True, stop=True),
                            d1, tga, b.free)
                v = dve.do(lambda e, ta=ta, b=b, c=c, h=h: e.tensor_scalar(ta[:, :], b.ap, c.galpha[:, h:h + 1], None, ALU.add), tok, gfree)
                banks.give(b, v)
                a = act.do(lambda e, tb=tb, ta=ta: e.activation(tb[:, :], ta[:, :], ACT.Abs), v, gfree)
                a = act.do(lambda e, tb=tb: e.activation(tb[:, :], tb[:, :], ACT.Exp, scale=-1.0), a)
                a = act.do(lambda e, tb=tb, c=c: e.activation(tb[:, :], tb[:, :], ACT.Ln, bias=c.ones[:, 0:1]), a)
                v = dve.do(lambda e, ta=ta, tb=tb: e.scalar_tensor_tensor(ta[:, :], ta[:, :], 0.0, tb[:, :], ALU.min,
                                                            ALU.subtract), a, v)
                v = dve.do(lambda e, ta=ta: e.tensor_scalar(ta[:, :], ta[:, :], 1.0 / 16, -1.0, ALU.mult, ALU.max), v)
                c.tick(2)
                v = dve.do(lambda e, tb=tb, rm=rm, ta=ta: e.tensor_tensor_scan(tb[:, :], rm[:, :], ta[:, :], 0.0, ALU.mult, ALU.add),
                           v, d3)
                a1 = act.do(lambda e, ta=ta, tb=tb: e.activation(ta[:, :], tb[:, :], ACT.Exp), v)
                a2 = act.do(lambda e, tc=tc, tb=tb: e.activation(tc[:, :], tb[:, :], ACT.Exp, scale=-1.0), v, gfree)
                t3 = tb[:, :].rearrange("p (n s) -> p n s", s=64)
                a3 = act.do(lambda e, cd=cd, t3=t3: e.activation(cd[:, :], t3[:, :, 63], ACT.Exp), v, gfree)
                vq = dve.do(lambda e, q=q, ta=ta: e.tensor_tensor(q, q, ta[:, :], ALU.mult), a1, tq)
                v = dve.do(lambda e, t3=t3, ta=ta: e.tensor_tensor(
                    ta[:, :].rearrange("p (n s) -> p n s", s=64), t3[:, :, 63:64].broadcast_to([128, 8, 64]), t3,
                    ALU.subtract), vq, a2, a3)
                a = act.do(lambda e, ta=ta: e.activation(ta[:, :], ta[:, :], ACT.Exp), v)
                v = dve.do(lambda e, kk=kk, ta=ta: e.tensor_tensor(ta[:, :], ta[:, :], kk, ALU.mult), a, tk)
                vk = dve.do(lambda e, kk=kk, tc=tc: e.tensor_tensor(kk, kk, tc[:, :], ALU.mult), v)
                c.tick(3)
                b = banks.take()
                for t in range(4):
                    tok = pe.do(lambda e, ta=ta, b=b, c=c, t=t: e.transpose(b.ap[:, t * 128:t * 128 + 128], ta[:, t * 128:t * 128 + 128],
                                                      c.ident[:, :]), v, b.free)
                gfree = tok
                akd = act.do(lambda e, b=b, kd=kd: e.activation(kd[:, :, :].rearrange("p t d -> p (t d)"), b.ap, ACT.Copy),
                             tok, pfree)
                banks.give(b, akd)
                b = banks.take()
                for n in range(8):
                    p, t = 64 * (n % 2), n // 2
                    tok = pe.do(lambda e, kk=kk, q=q, b=b, p=p, t=t, n=n: e.matmul(b.ap[p:p + 64, t * 64:t * 64 + 64], kk[:, n * 64:n * 64 + 64],
                                                   q[:, n * 64:n * 64 + 64], start=True, stop=True), vk, b.free)
                va = dve.do(lambda e, At=At, mk=mk, b=b: e.copy_predicated(At[:, :, :], mk[:, :, :].bitcast(U32),
                                                        b.ap[:, 0:256].rearrange("p (t i) -> p t i", t=4)),
                            tok, d2, z, pfree)
                banks.give(b, va)
                c.tick()
                last = None
                for n in range(7):
                    p, t = 64 * (n % 2), n // 2
                    b = banks.take()
                    tok = pe.do(lambda e, kd=kd, v_=v_, b=b, t=t, p=p, h=h: e.matmul(b.ap[:, 0:256], kd[p:p + 64, t, :],
                                                   v_[p:p + 64, t, h * 256:h * 256 + 256], start=True, stop=True),
                                akd, tv, b.free)
                    if n == 0:
                        last = dve.do(lambda e, St=St, b=b: e.tensor_copy(St[:, 0, :], b.ap[:, 0:256]), tok, pfree)
                    else:
                        last = dve.do(lambda e, St=St, cd=cd, n=n, b=b: e.scalar_tensor_tensor(
                            St[:, n, :], St[:, n - 1, :], cd[:, n:n + 1], b.ap[:, 0:256], ALU.mult, ALU.add),
                            tok, last, a3)
                    banks.give(b, last)
                if h < 3:
                    nxt = heads(h + 1)
                c.tick(3)
                ao = None
                for e2 in range(2):
                    col = h * 256 + e2 * 128
                    bb = [banks.take(), banks.take()]
                    for n in range(8):
                        p, t = 64 * (n % 2), n // 2
                        o_ = bb[n % 2].ap[:, t * 64:t * 64 + 64]
                        tok = pe.do(lambda e, o_=o_, v_=v_, At=At, t=t, n=n, p=p, col=col: e.matmul(o_, v_[p:p + 64, t, col:col + 128], At[p:p + 64, t, :],
                                                       start=True, stop=(n == 0)), va, bb[n % 2].free)
                        if n:
                            tok = pe.do(lambda e, o_=o_, St=St, q=q, n=n, e2=e2: e.matmul(o_, St[:, n - 1, e2 * 128:e2 * 128 + 128],
                                                           q[:, n * 64:n * 64 + 64], start=False, stop=True), last)
                    for i in range(2):
                        ao = act.do(lambda e, i=i, o=o, e2=e2, bb=bb: e.activation(
                            o[:, e2, :].rearrange("p (t i s) -> p t i s", i=2, s=64)[:, :, i, :],
                            bb[i].ap[:, 0:256].rearrange("p (t s) -> p t s", t=4), ACT.Copy), tok, pfree)
                        banks.give(bb[i], ao)
                qs.give(qslot, tok, vk)
                ks.give(kslot, tok, vk)
                c.tick(2)
                s0, v = square_pair([o[:, 0, :], o[:, 1, :]], [ao, pfree])
                c.tick()
                r = head_inv(s0, v, hr[:, :], 0)
                for e2 in range(2):
                    k = 2 * h + e2
                    while k not in gt:
                        c.tick()
                    x = o[:, e2, :]
                    v = dve.do(lambda e, x=x, hr=hr, c=c, k=k: e.scalar_tensor_tensor(x, x, c.g_gla[:, k:k + 1], hr[:, :],
                                                                ALU.mult, ALU.mult), r)
                    btoks.append(dve.do(lambda e, x=x, of=of, k=k: e.tensor_tensor(of[:, k, :], of[:, k, :], x, ALU.mult), v, gt[k]))
                pfree = [tok, gfree, btoks[-1]]
                gfree = [gfree, last, vk]
            c.drain()
            done = [x.now() for x in (pe, act, dve, gp)]
        btoks = [split(c, of[:, k, :], bhi(k), blo(k), btoks[k], c.bfree) for k in range(8)]
        done = done + btoks
        m2 = []
        c.side = branch(c, 1, bhi, blo, btoks, H, mg, mt, m2)

        with ExitStack() as cx:
            def sc(name, shape, dt=F32):
                return cx.enter_context(c.nc.sbuf_tensor(name, shape, dt))
            for x in (act, dve, gp):
                x.wait(done)
            q = sc("sq_", [128, 8, S])
            kk = sc("sk_", [128, 2, S])
            v_ = sc("sv_", [128, 4, 256])
            dist = sc("dist2", [128, 256])
            sink = sc("sink", [128, 16])
            Pb = Pool([sc(f"Ps{i}", [128, 4, 256])[:, :, :] for i in range(3)])
            pT = Pool([sc(f"pTs{i}", [128, 8, 128])[:, :, :] for i in range(2)])
            bias = Pool([sc(f"bs{i}", [128, 256])[:, :] for i in range(3)])
            stp = Pool([sc(f"ss{i}", [128, 5, 4])[:, :, :] for i in range(4)])
            tq = [ev("w_sq", t, q[:, t, :], scale=0.125) for t in range(8)]
            dd = load(c, dist[:, :], I["c_dist2"], done)
            ds = load(c, sink[:, :], I["sinks"], done)
            tk = [ev("w_sk", t, kk[:, t, :]) for t in range(2)]
            tv = []
            for t, b in enumerate(gemm_tok(c, "w_sv", 0, 256, 4, c.hhi, c.hlo, H)):
                a = act.do(lambda e, v_=v_, t=t, b=b, c=c: e.activation(v_[:, t, :], b.ap[:, 0:256], ACT.Copy, scale=c.rsT[:, t:t + 1]),
                           b.tok, rT)
                banks.give(b, a)
                tv.append(a)
            live, ob, btoks = {}, {}, []
            units = [(t, a) for t in range(8) for a in range(2)]
            span = [(0, 128)] + [(128 * (j - 1), 256) for j in (1, 2, 3)]

            def stage_a(u):
                t, a = units[u]
                g2, r = t // 4, t % 4
                h = (2 * g2 + a) * 4 + r
                bs = bias.take()
                slope = -float(np.exp2(np.float32(-8.0 * (h + 1) / 16)))
                bt = gp.do(lambda e, slope=slope, bs=bs, dist=dist: e.tensor_scalar(bs.ap, dist[:, :], slope, 1.0, ALU.mult, ALU.mult), dd, bs.free)
                P = Pb.take()
                s = stp.take()
                for jj in range(2):
                    b = banks.take()
                    for j in (2 * jj, 2 * jj + 1):
                        k0, W = span[j]
                        col = (j % 2) * 256
                        tok = pe.do(lambda e, q=q, kk=kk, b=b, t=t, g2=g2, col=col, k0=k0, W=W, a=a, j=j: e.matmul(
                            b.ap[:, col:col + W], q[a * 64:a * 64 + 64, t, j * 128:j * 128 + 128],
                            kk[a * 64:a * 64 + 64, g2, k0:k0 + W], start=True, stop=True), tq[t], tk[g2], b.free)
                    for j in (2 * jj, 2 * jj + 1):
                        k0, W = span[j]
                        col = (j % 2) * 256
                        v = dve.do(lambda e, P=P, j=j, b=b, bs=bs, s=s, W=W, col=col: e.tensor_tensor_reduce(
                            out=P.ap[:, j, 0:W], in0=b.ap[:, col:col + W], in1=bs.ap[:, 256 - W:256], scale=1.0,
                            scalar=-3.0e38, op0=ALU.add, op1=ALU.max, accum_out=s.ap[:, 0, j:j + 1]),
                            tok, bt, P.free, s.free)
                    banks.give(b, v)
                bias.give(bs, v)
                hs = sink[:, h:h + 1]
                v = dve.do(lambda e, hs=hs, s=s: e.tensor_scalar(s.ap[:, 1, :], s.ap[:, 0, :], hs, -1.0, ALU.max, ALU.mult), v, ds)
                for j in range(4):
                    k0, W = span[j]
                    x = act.do(lambda e, P=P, j=j, W=W, s=s: e.activation(P.ap[:, j, 0:W], P.ap[:, j, 0:W], ACT.Exp,
                                                      bias=s.ap[:, 1, j:j + 1], accum_out=s.ap[:, 2, j:j + 1]), v)
                x = act.do(lambda e, hs=hs, s=s: e.activation(s.ap[:, 3, :], s.ap[:, 1, :], ACT.Exp, bias=hs), v)
                live[u] = (P, s, x)

            def stage_b(u):
                P, s, x = live[u]
                v = dve.do(lambda e, s=s: e.tensor_tensor(s.ap[:, 2, :], s.ap[:, 2, :], s.ap[:, 3, :], ALU.add), x)
                v = dve.do(lambda e, s=s: e.reciprocal(s.ap[:, 4, :], s.ap[:, 2, :]), v)
                for j in range(4):
                    W = span[j][1]
                    g_ = gp.do(lambda e, P=P, j=j, s=s, W=W: e.tensor_scalar(P.ap[:, j, 0:W], P.ap[:, j, 0:W], s.ap[:, 4, j:j + 1], 1.0,
                                                         ALU.mult, ALU.mult), v, x)
                stp.give(s, g_)
                live[u] = (P, g_)

            def stage_c(u):
                t, a = units[u]
                g = 2 * (t // 4) + a
                P, g_ = live[u]
                if a == 0:
                    ob[t] = banks.take()
                p = pT.take()
                blocks = [(j, k) for j in range(4) for k in range(span[j][1] // 128)]
                x = None
                for i in range(2):
                    b = banks.take()
                    part = blocks[4 * i:4 * i + 4]
                    for n, (j, k) in enumerate(part):
                        tok = pe.do(lambda e, b=b, P=P, j=j, c=c, n=n, k=k: e.transpose(b.ap[:, n * 128:n * 128 + 128],
                                                          P.ap[:, j, k * 128:k * 128 + 128], c.ident[:, :]), g_, b.free)
                    w = len(part) * 128
                    dst = p.ap.rearrange("p k q -> p (k q)")[:, i * 512:i * 512 + w]
                    if i:
                        y = act.do(lambda e, dst=dst, b=b, w=w: e.activation(dst, b.ap[:, 0:w], ACT.Copy), tok, p.free)
                    else:
                        y = dve.do(lambda e, dst=dst, b=b, w=w: e.tensor_copy(dst, b.ap[:, 0:w]), tok, p.free)
                    banks.give(b, y)
                    x = [x, y]
                Pb.give(P, tok)
                live[u] = (p, x, blocks)

            def stage_d(u):
                t, a = units[u]
                g = 2 * (t // 4) + a
                p, x, blocks = live[u]
                o = ob[t]
                for n, (j, k) in enumerate(blocks):
                    nb = span[j][1] // 128
                    kt = span[j][0] // 128 + k
                    tok = pe.do(lambda e, v_=v_, o=o, kt=kt, p=p, n=n, k=k, nb=nb, a=a, j=j, g=g: e.matmul(
                        o.ap[a * 64:a * 64 + 64, j * 128:j * 128 + 128], v_[:, kt, g * 64:g * 64 + 64], p.ap[:, n, :],
                        start=(k == 0), stop=(k == nb - 1), skip_group_check=True), x, tv, o.free)
                pT.give(p, tok)
                if a == 1:
                    y = act.do(lambda e, of=of, o=o, t=t: e.activation(of[:, t, :], o.ap, ACT.Copy), tok, done)
                    banks.give(o, y)
                    btoks.append(y)

            n = len(units)
            for i in range(n + 3):
                if i < n:
                    stage_a(i)
                c.tick()
                if 1 <= i <= n:
                    stage_b(i - 1)
                if i >= 3:
                    stage_d(i - 3)
                if 2 <= i <= n + 1:
                    stage_c(i - 2)
                c.tick()
        c.drain()
        btoks = [split(c, of[:, k, :], bhi(k), blo(k), btoks[k], c.bfree) for k in range(8)]
        mt = []
        c.side = branch(c, 2, bhi, blo, btoks, H, mg, m2, mt)
        c.drain()
        mt = [split(c, mg[:, k, :], bhi(k), blo(k), mt[k], c.bfree) for k in range(8)]
        yt = []
        c.ss.start()
        for k in range(8):
            b, tok = gemm(c, "w_o2", k, KT, bhi, blo, mt)
            a = act.do(lambda e, mg=mg, b=b, k=k: e.activation(mg[:, k, :], b.ap, ACT.Copy), tok, mt)
            banks.give(b, a)
            yt.append(a)
            c.ss.add(mg[:, k, :], a)
        hd = pe.now()
        H = []

        def after(k, tok):
            H.append(split_scaled(c, X[:, k, :], c.g_fpre[:, k:k + 1], c.hhi(k), c.hlo(k), tok, hd))
            c.ss.add(X[:, k, :], tok, eng=gp)
        xt = add_normed(c, X, xt, mg, yt, c.g_post, after)
        done = [x.now() for x in (pe, act, dve, gp)]
    with ExitStack() as ctx:
        def sb(name, shape, dt=F32):
            return ctx.enter_context(c.nc.sbuf_tensor(name, shape, dt))
        for x in (act, dve, gp):
            x.wait(done)
        Fh = sb("Fh", [128, 22, S], F32R)
        Fl = sb("Fl", [128, 22, S], F32R)
        y = sb("fy", [128, 8, S])
        ft = Pool([sb(f"ft{i}", [128, S])[:, :] for i in range(3)])
        ftoks = []
        rt = None
        for k in range(22):
            (bg, tg), (bu, tu) = pair_or_two(c, k == 0, ("w_fg", k), ("w_fu", k), H)
            if k == 0:
                rt = c.ss.inv(0, 1.0 / D)
            s = ft.take()
            v = dve.do(lambda e, s=s, bg=bg, c=c: e.tensor_tensor(s.ap, bg.ap, c.rs[:, :], ALU.mult), tg, s.free, rt)
            banks.give(bg, v)
            a = act.do(lambda e, s=s: e.activation(s.ap, s.ap, ACT.Silu), v)
            v = dve.do(lambda e, s=s, bu=bu: e.tensor_tensor(s.ap, s.ap, bu.ap, ALU.mult), a, tu)
            banks.give(bu, v)
            v = gp.do(lambda e, s=s, c=c: e.tensor_tensor(s.ap, s.ap, c.rs[:, :], ALU.mult), v)
            h2 = split(c, s.ap, Fh[:, k, :], Fl[:, k, :], v)
            ft.give(s, *h2)
            ftoks.append(h2)
        c.rsfree = v
        yt = []
        c.ss.start()
        for k in range(8):
            b, tok = gemm(c, "w_fd", k, 22, lambda i: Fh[:, i, :], lambda i: Fl[:, i, :], ftoks)
            a = act.do(lambda e, y=y, b=b, k=k: e.activation(y[:, k, :], b.ap, ACT.Copy), tok)
            banks.give(b, a)
            yt.append(a)
            c.ss.add(y[:, k, :], a)
        so = Sem(c.osem)
        sent = []

        def send(k, tok):
            sent.append(c.sp.dma(lambda e, k=k, X=X, c=c: e.dma_start(c.out[k], X[:, k, :]), so, tok))
        xt = add_normed(c, X, xt, y, yt, c.g_fpost, send)
        t = sent[-1]
        c.sp.wait(t)
    return xt


def more(x, A, f, tiles, rows):
    A["w_s5"] = tiles(x["l1_w_in"])
    A["w_glu"] = tiles(x["l1_w_glu"])
    A["w_o1"] = tiles(x["l1_w_out"])
    pair = lambda v: v.reshape(32, 2, 64, *v.shape[2:]).transpose(1, 2, 0, *range(3, v.ndim + 1)).reshape(
        128, 32, *v.shape[2:])
    dt = np.broadcast_to(x["l1_log_dt"][:, None], (64, 64))
    A["s5_par"] = f(np.stack([pair(x["l1_lambda_re"]), pair(x["l1_lambda_im"]), pair(dt)], 1))
    cut = lambda r, i: f(np.stack([r, i], 1).reshape(128, 2, 4, 8, 16).transpose(2, 0, 1, 3, 4))
    A["s5_B"] = cut(pair(x["l1_b_re"]), pair(x["l1_b_im"]))
    A["s5_C"] = cut(pair(x["l1_c_re"].transpose(0, 2, 1)), pair(x["l1_c_im"].transpose(0, 2, 1)))
    w = x["w_in_2"][0]
    at = np.concatenate([[0], np.cumsum([512, 512, 1024, 1024, 512, 512, 1024, 1024, 16, 1024, 256, 256, 3072])])
    s = lambda i, j=None: w[:, at[i]:at[(j or i) + 1]]
    hd = np.arange(64)
    order = np.concatenate([((2 * (t // 4) + a) * 4 + t % 4) * 64 + hd for t in range(8) for a in range(2)])
    A["w_r"] = tiles(s(0, 1))
    A["w_rv"] = rows(s(2), 512, 2)
    A["w_rg"] = tiles(s(3))
    A["w_g"] = tiles(s(4, 5))
    A["w_gv"] = rows(s(6), 512, 2)
    A["w_gg"] = tiles(s(7))
    A["w_ga"] = tiles(s(8), 16)
    A["w_sq"] = tiles(s(9)[:, order])
    A["w_sk"] = tiles(s(10))
    A["w_sv"] = rows(s(11), 256, 4)
    A["w_bgate"] = tiles(s(12))
    wb = x["w_branch_2"][0]
    A["w_branch"] = tiles(np.concatenate([wb[0], wb[1], wb[2][order]], 1))
    A["w_o2"] = tiles(x["w_out_2"][0])
    A["w_fg"] = tiles(x["ffn_w_gate_2"][0])
    A["w_fu"] = tiles(x["ffn_w_up_2"][0])
    A["w_fd"] = tiles(x["ffn_w_down_2"][0])
    A["alpha2"] = f(x["gla_w_alpha2_2"][0])
    A["sinks"] = f(np.broadcast_to(x["attn_sinks_2"], (128, 16)))
    p, m = np.arange(128)[:, None], np.arange(512)[None, :]
    lg = np.log1p(-np.exp2(-5.0 - np.arange(4)))
    rel = (m - p)[:, None, :]
    A["c_decay"] = f(np.where(rel >= 0, np.exp(np.maximum(rel, 0) * lg[None, :, None]), 0.0))
    j, i = np.arange(128)[:, None] % 64, np.arange(64)[None, :]
    A["c_tri"] = f(np.broadcast_to((j <= i)[:, None, :], (128, 4, 64)))
    A["c_reset"] = f(np.broadcast_to(np.arange(512) % 64 != 0, (128, 512)))
    d = 128 + p - np.arange(256)[None, :]
    A["c_dist2"] = f(np.where((d >= 0) & (d < 128), d, np.float32(MASKED)))


def program(nc, ins, out, plan, tap=None):
    c = Core()
    c.nc, c.ins, c.out, c.tap = nc, ins, out, tap
    with ExitStack() as ctx:
        def sb(name, shape, dt=F32):
            return ctx.enter_context(nc.sbuf_tensor(name, shape, dt))

        def sem(name):
            return ctx.enter_context(nc.semaphore(name))

        c.pe, c.act, c.dve, c.gp, c.sp = [Queue(sem(n)) for n in ("s_pe", "s_act", "s_dve", "s_gp", "s_sp")]
        c.queues = [c.pe, c.act, c.dve, c.gp, c.sp]
        c.sems = [Sem(sem(f"s_d{i}")) for i in range(64)]
        c.tsems = [sem(f"s_t{i}") for i in range(20)]
        c.osem = sem("s_out")
        c.sem_at = 0
        c.dma_toks = []

        def dsem():
            s = c.sems[c.sem_at]
            c.sem_at += 1
            return s
        c.dsem = dsem
        c.du = nc.dram_tensor("scratch_u", [4, 2, 128, S], F32, kind="Internal").ap()
        c.dy = nc.dram_tensor("scratch_y", [4, 2, 128, S], F32, kind="Internal").ap()
        base = (nc.sbuf_base + 31) // 32 * 32
        sb("hspan", [128, 8192])
        c.at = lambda name, shape, off, dt=F32: nc.alloc_sbuf_tensor_at(name, shape, dt, offset=base + off)
        c.wbase = (nc.sbuf_base + 31) // 32 * 32
        raw = [sb(f"wraw{i}", [128, 1024]) for i in range(RR)]
        hi = [sb(f"whi{i}", [128, 1024], F32R) for i in range(RH)]
        lo = [sb(f"wlo{i}", [128, 1024], F32R) for i in range(RH)]
        c.w = Weights(ins, c.sp, c.act, c.dve, raw, hi, lo, [Sem(sem(f"s_w{i}")) for i in range(RR)], plan)
        c.banks = Pool([ctx.enter_context(nc.psum_tensor(f"bank{i}", [128, 512], F32))[:, :] for i in range(8)])
        X = sb("X", [128, 8, S])
        Hh = c.at("Hh", [128, 8, S], 0, F32R)
        Hl = c.at("Hl", [128, 8, S], 16384, F32R)
        c.hhi = lambda k: Hh[:, k, :]
        c.hlo = lambda k: Hl[:, k, :]
        c.rs = sb("rs", [128, S])
        c.rsfree = None
        c.sq = Pool([sb(f"sq{i}", [128, S])[:, :] for i in range(2)])
        c.ones = sb("ones", [128, 128])
        c.ident = sb("ident", [128, 128])
        c.epst = sb("epst", [128, 2])
        vecs = sb("vecs", [128, 16, 8])
        c.g_l0, c.g_l1, c.g_fin, c.g_pre, c.g_post, c.g_fpre, c.g_fpost, c.g_retw, c.g_retb, c.g_gla, c.g_d = [
            vecs[:, i, :] for i in range(11)]
        c.galpha = vecs[:, 11, 0:4]
        c.mag8 = sb("mag8", [128, 32])
        c.sq2 = Pool([sb(f"sqb{i}", [128, S])[:, :] for i in range(2)])
        c.ss = Squares(c, sb("nacc", [128, S]))
        c.sf = Squares(c, sb("nacc2", [128, S]))
        c.rst = sb("rst", [128, S])
        c.gg = vecs[:, 12, :]
        c.rsT = vecs[:, 13, 0:4]
        c.s5t = {}
        c.side = None

        def tick(n=1):
            for _ in range(n):
                if c.side is not None:
                    next(c.side, None)
        c.tick = tick

        def drain():
            for _ in c.side:
                pass
            c.side = None
        c.drain = drain
        c.dCA, c.dW, c.dR = [nc.dram_tensor("scratch_" + n, [4, 128, w], F32, kind="Internal").ap()
                             for n, w in (("CA", 2304), ("W", 2048), ("R", 1024))]
        c.dK = nc.dram_tensor("scratch_K", [4, 16, 16, 256], F32, kind="Internal").ap()
        xt = []
        for k in range(8):
            xt.append(load(c, X[:, k, :], ins["xT"][k]))
            c.ss.add(X[:, k, :], xt[-1])
        dv = load(c, vecs[:, 0:12, :], ins["vecs"])
        di = load(c, c.ident[:, :], ins["c_ident"])
        m1 = c.dve.do(lambda e, c=c: e.memset(c.ones[:, :], 1.0))
        m2 = c.dve.do(lambda e, c=c: e.memset(c.epst[:, 0:1], 1e-6))
        m3 = c.dve.do(lambda e, c=c: e.memset(c.epst[:, 1:2], 1e-5))
        c.gtok = dv
        for q in (c.pe, c.act, c.dve):
            q.wait(dv, di, m3)
        r = nsa(c, X, xt)
        taps = {}
        if tap is None or tap not in ("proj", "nsa"):
            r, H = s5(c, X, r[0], r[1])
            if tap != "s5":
                r = second(c, X, r, H)
        if tap:
            if isinstance(r, dict):
                taps = {n: t for n, t in r.items()}
            else:
                taps = {"X": X}
        if taps:
            end = [q.now() for q in c.queues]
            fs = Sem(sem("s_fin"))
            for n, t in taps.items():
                o = nc.dram_tensor("tap_" + n, list(t.shape), F32, kind="ExternalOutput").ap()
                c.sp.dma(lambda e, o=o, t=t: e.dma_start(o, t[tuple(slice(None) for _ in t.shape)]), fs, end)
            c.sp.wait((fs, fs.n))
        if plan is None:
            return c.w.asked
        block = ctx.enter_context(nc.Block())
        block.tensor(lambda e, c=c: c.pe.play(e))
        block.scalar(lambda e, c=c: c.act.play(e))
        block.vector(lambda e, c=c: c.dve.play(e))
        block.gpsimd(lambda e, c=c: c.gp.play(e))
        block.sync(lambda e, c=c: c.sp.play(e))


SHAPES = {}


def build(nc, arrays, tap=None):
    def declare(n):
        return {k: n.dram_tensor("in_" + k, list(a.shape), F32, kind="ExternalInput").ap() for k, a in arrays.items()}

    def result(n):
        return n.dram_tensor("out_0", [8, 128, S], F32, kind="ExternalOutput").ap()
    scratch = bass.Bass(dynamic_dma_scratch_size=RING)
    plan = program(scratch, declare(scratch), result(scratch), None, tap)
    program(nc, declare(nc), result(nc), plan, tap)


def layout(x):
    f = lambda a: np.ascontiguousarray(a, dtype=np.float32)

    def tiles(w, M=128):
        K, C = w.shape
        return f(w.reshape(K // 128, 128, C // M, M).transpose(2, 1, 0, 3).reshape(C // M, 128, K // 128 * M))

    def rows(w, n, kper):
        K, C = w.shape
        return f(w.reshape(K // 128 // kper, kper, 128, C // n, n).transpose(3, 0, 2, 1, 4).reshape(
            C // n, K // 128 // kper, 128, kper * n))

    def vec(v):
        return f(v.reshape(-1, 128).T)

    A = {}
    A["xT"] = f(x["x"][0].T.reshape(8, 128, S))
    w = x["l0_w_in"]
    hd = np.arange(64)
    order = np.concatenate([((2 * (t // 4) + a) * 4 + t % 4) * 64 + hd for t in range(8) for a in range(2)])
    A["w_kvc"] = tiles(w[:, 1024:1536])
    A["w_gate"] = tiles(w[:, 2560:2608], 48)
    A["w_q"] = tiles(w[:, order])
    A["w_ksw"] = tiles(np.concatenate([w[:, 1536:1792], w[:, 2048:2304]], 1))
    A["w_vsw"] = rows(np.concatenate([w[:, 1792:2048], w[:, 2304:2560]], 1), 512, 2)
    A["w_z0"] = tiles(w[:, 2608 + order])
    A["w_o0"] = tiles(x["l0_w_out"][order])
    p = [x["l0_cmp_k_pe"].T, x["l0_cmp_v_pe"].T]
    A["cmp_pe"] = f(np.stack([np.concatenate([q, q]) for q in p], 1))
    A["cmp_w1"] = f(np.stack([x[n].reshape(2, 8, 128, 2, 128).transpose(3, 0, 2, 1, 4).reshape(2, 2, 128, 1024)
                              for n in ("l0_cmp_k_w1", "l0_cmp_v_w1")]))
    A["cmp_w2"] = f(np.stack([x[n].reshape(2, 128, 64).transpose(1, 0, 2)
                              for n in ("l0_cmp_k_w2", "l0_cmp_v_w2")], 1))
    t = np.arange(512).reshape(4, 128).T
    n = np.arange(32)
    slopes = np.exp2(-8.0 * np.arange(1, 17, dtype=np.float32) / np.float32(16)).astype(np.float32).reshape(4, 4)
    seen = (16 * n + 31)[None, None, :] <= t[:, :, None]
    seen &= n < 31
    gap = (t[:, :, None] - (16 * n + 15.5)).astype(np.float32)
    b = -slopes.T[None, None, :, :, None] * gap[:, :, None, None, :]
    b = np.where(seen[:, :, None, None, :], b, np.float32(NEG))
    A["c_biasc"] = f(b.reshape(128, 4, 512))
    A["c_maskc"] = f(seen)
    d = 384 + np.arange(128)[:, None] - np.arange(512)[None, :]
    A["c_dist"] = f(np.where(d >= 0, d, np.float32(MASKED)))
    A["c_ident"] = f(np.eye(128))
    V = [vec(x[k]) for k in ("l0_norm", "l1_norm", "final_norm", "norm_mix_pre_2", "norm_mix_post_2",
                             "norm_ffn_pre_2", "norm_ffn_post_2", "ret_norm_w_2", "ret_norm_b_2", "gla_norm_w_2")]
    V.append(vec(x["l1_d"]))
    V.append(np.concatenate([vec(x["gla_b_alpha_2"]), np.zeros((128, 4), np.float32)], 1))
    A["vecs"] = f(np.stack(V, 1))
    more(x, A, f, tiles, rows)
    return A


def kernel(**inputs):
    import concourse.bacc as bacc
    from concourse.bass_utils import run_bass_kernel_spmd as run

    x = {k: np.asarray(v) for k, v in inputs.items()}
    A = layout(x)
    nc = bacc.Bacc("TRN2", target_bir_lowering=False, num_devices=1, dynamic_dma_scratch_size=RING)
    build(nc, A)
    r = run(nc, [{"in_" + k: a for k, a in A.items()}], core_ids=[0])
    return r.results[0]["out_0"].reshape(1024, S).T.reshape(1, S, 1024)
```
